# Optimizing a Trainium2 kernel written in Bass

```python
import jax
import jax.numpy as jnp
from jax import lax
import numpy as np

D_MODEL = 1024
BATCH = 1
SEQ = 1024
DEPTH = 1

CHUNK = 64
EPS = 1e-6
D_MIX = D_MODEL

LRU_W = D_MIX // 4
LRU_BLOCKS = 4
LRU_BLK = LRU_W // LRU_BLOCKS
CONV_W = 4
LRU_C = 8.0

GLA_HEADS = 4
GLA_DV = (D_MIX // 4) // GLA_HEADS
GLA_DK = GLA_DV // 2
GLA_RANK = 16
GLA_TAU = 16.0

SWA_W = D_MIX - LRU_W - GLA_HEADS * GLA_DV
HEAD_DIM = 64
SWA_HEADS = SWA_W // HEAD_DIM
SWA_KV_HEADS = 2
SWA_GROUP = SWA_HEADS // SWA_KV_HEADS
WINDOW = 128
WINDOW_CHUNKS = WINDOW // CHUNK
ROPE_THETA = 10000.0

N_GROUPS = 4
EXPERTS_PER_GROUP = 8
N_EXPERTS = N_GROUPS * EXPERTS_PER_GROUP
TOP_K = 2
EXPERT_FF = D_MODEL // 2
MOE_BLOCK = 128

IN_SIZES = (LRU_W, LRU_W,
            GLA_HEADS * GLA_DK, GLA_HEADS * GLA_DK, GLA_HEADS * GLA_DV, GLA_HEADS * GLA_DV, GLA_RANK,
            SWA_W, SWA_KV_HEADS * HEAD_DIM, SWA_KV_HEADS * HEAD_DIM)
D_IN = sum(IN_SIZES)

kernel_name = "hymba_style_lru_gla_swa_hiermoe"

def _split_points(sizes):
    pts, acc = [], 0
    for s in sizes[:-1]:
        acc += s
        pts.append(acc)
    return pts

def _rmsnorm(x, g):
    xf = x.astype(jnp.float32)
    y = xf * lax.rsqrt(jnp.mean(xf * xf, axis=-1, keepdims=True) + EPS)
    return (y * g.astype(jnp.float32)).astype(x.dtype)

def _rope_tables(positions):
    inv_freq = 1.0 / (ROPE_THETA ** (jnp.arange(0, HEAD_DIM, 2, dtype=jnp.float32) / HEAD_DIM))
    ang = positions.astype(jnp.float32)[..., None] * inv_freq
    return jnp.cos(ang)[:, :, None, :], jnp.sin(ang)[:, :, None, :]

def _apply_rope(t, cos, sin):
    tf = t.astype(jnp.float32)
    t1, t2 = tf[..., :HEAD_DIM // 2], tf[..., HEAD_DIM // 2:]
    return jnp.concatenate([t1 * cos - t2 * sin, t2 * cos + t1 * sin], axis=-1).astype(t.dtype)

def _lru_combine(c1, c2):
    a1, b1 = c1
    a2, b2 = c2
    return a1 * a2, a2 * b1 + b2

def _rglru_group(u, gate, conv_w, conv_b, wr, br, wi, bi, lam, out_g):
    bsz, seq, _ = u.shape
    up = jnp.pad(u, ((0, 0), (CONV_W - 1, 0), (0, 0)))
    uc = conv_b
    for tap in range(CONV_W):
        uc = uc + up[:, tap:tap + seq] * conv_w[tap]
    ub = uc.reshape(bsz, seq, LRU_BLOCKS, LRU_BLK)
    r = jax.nn.sigmoid(jnp.einsum('bsni,nij->bsnj', ub, wr).reshape(bsz, seq, LRU_W) + br)
    i = jax.nn.sigmoid(jnp.einsum('bsni,nij->bsnj', ub, wi).reshape(bsz, seq, LRU_W) + bi)
    log_a = -LRU_C * r.astype(jnp.float32) * jax.nn.softplus(-lam.astype(jnp.float32))
    a = jnp.exp(log_a)
    xin = jnp.sqrt(-jnp.expm1(2.0 * log_a)) * (i * uc).astype(jnp.float32)
    _, h = lax.associative_scan(_lru_combine, (a, xin), axis=1)
    y = h * jax.nn.gelu(gate.astype(jnp.float32))
    return _rmsnorm(y, out_g).astype(u.dtype)

def _to_chunks(t):
    bsz, seq = t.shape[:2]
    return jnp.moveaxis(t.reshape(bsz, seq // CHUNK, CHUNK, *t.shape[2:]), 1, 0)

def _gla_group(q, k, v, g, a_lr, wa2, ba, norm_g):
    bsz, seq, _ = q.shape
    f32 = jnp.float32
    q = q.reshape(bsz, seq, GLA_HEADS, GLA_DK).astype(f32) * (GLA_DK ** -0.5)
    k = k.reshape(bsz, seq, GLA_HEADS, GLA_DK).astype(f32)
    v = v.reshape(bsz, seq, GLA_HEADS, GLA_DV).astype(f32)
    log_alpha = (jax.nn.log_sigmoid((a_lr @ wa2 + ba).astype(f32)) / GLA_TAU).reshape(
        bsz, seq, GLA_HEADS, GLA_DK)
    causal = jnp.tril(jnp.ones((CHUNK, CHUNK), dtype=bool))[None, :, :, None, None]

    def chunk_step(state, inp):
        qc, kc, vc, lc = inp
        b = jnp.cumsum(lc, axis=1)
        b_last = b[:, -1]
        o_inter = jnp.einsum('bihd,bhdv->bihv', qc * jnp.exp(b), state)
        decay = jnp.exp(jnp.where(causal, b[:, :, None] - b[:, None, :], -jnp.inf))
        att = jnp.einsum('bihd,bjhd,bijhd->bhij', qc, kc, decay)
        o_intra = jnp.einsum('bhij,bjhv->bihv', att, vc)
        state = jnp.exp(b_last)[..., None] * state + jnp.einsum(
            'bjhd,bjhv->bhdv', kc * jnp.exp(b_last[:, None] - b), vc)
        return state, o_inter + o_intra

    state0 = jnp.zeros((bsz, GLA_HEADS, GLA_DK, GLA_DV), f32)
    _, o = lax.scan(chunk_step, state0,
                    (_to_chunks(q), _to_chunks(k), _to_chunks(v), _to_chunks(log_alpha)))
    o = jnp.moveaxis(o, 0, 1).reshape(bsz, seq, GLA_HEADS, GLA_DV)
    o = _rmsnorm(o, norm_g).reshape(bsz, seq, GLA_HEADS * GLA_DV)
    return (o * jax.nn.silu(g.astype(f32))).astype(g.dtype)

def _shift_chunks(t, off):
    if off == 0:
        return t
    pad = [(0, 0)] * t.ndim
    pad[1] = (off, 0)
    return jnp.pad(t, pad)[:, :t.shape[1]]

def _swa_group(q, k, v, cos, sin, q_g, k_g, sinks, out_g):
    bsz, seq, _ = q.shape
    n = seq // CHUNK
    q = _apply_rope(_rmsnorm(q.reshape(bsz, seq, SWA_HEADS, HEAD_DIM), q_g), cos, sin)
    k = _apply_rope(_rmsnorm(k.reshape(bsz, seq, SWA_KV_HEADS, HEAD_DIM), k_g), cos, sin)
    v = v.reshape(bsz, seq, SWA_KV_HEADS, HEAD_DIM)
    qc = q.reshape(bsz, n, CHUNK, SWA_KV_HEADS, SWA_GROUP, HEAD_DIM)
    kc = k.reshape(bsz, n, CHUNK, SWA_KV_HEADS, HEAD_DIM)
    vc = v.reshape(bsz, n, CHUNK, SWA_KV_HEADS, HEAD_DIM)
    offs = list(range(WINDOW_CHUNKS - 1, -1, -1))
    kb = jnp.concatenate([_shift_chunks(kc, o) for o in offs], axis=2)
    vb = jnp.concatenate([_shift_chunks(vc, o) for o in offs], axis=2)
    chunk_idx = jnp.arange(n)[:, None]
    valid = jnp.concatenate([jnp.broadcast_to(chunk_idx >= o, (n, CHUNK)) for o in offs], axis=1)
    s = jnp.einsum('bnqhgd,bnjhd->bnhgqj', qc, kb).astype(jnp.float32) * (HEAD_DIM ** -0.5)
    s = jnp.where(valid[None, :, None, None, None, :], s, -jnp.inf)
    sink = sinks.astype(jnp.float32).reshape(1, 1, SWA_KV_HEADS, SWA_GROUP, 1, 1)
    m = jnp.maximum(jnp.max(s, axis=-1, keepdims=True), sink)
    p = jnp.exp(s - m)
    probs = p / (jnp.sum(p, axis=-1, keepdims=True) + jnp.exp(sink - m))
    o = jnp.einsum('bnhgqj,bnjhd->bnqhgd', probs.astype(vb.dtype), vb).reshape(bsz, seq, SWA_W)
    return _rmsnorm(o, out_g)

def _hier_moe(h, wg, bg, we, be, w_gate, w_up, w_down):
    bsz, seq, dm = h.shape
    t = bsz * seq
    n_assign = t * TOP_K
    xt = h.reshape(t, dm)
    pg = jax.nn.softmax((xt @ wg + bg).astype(jnp.float32), axis=-1)
    gw, gi = lax.top_k(pg, 1)
    le = (xt @ we + be).astype(jnp.float32).reshape(t, N_GROUPS, EXPERTS_PER_GROUP)
    le = jnp.take_along_axis(le, gi[:, :, None], axis=1)[:, 0]
    ew, ei = lax.top_k(jax.nn.softmax(le, axis=-1), TOP_K)
    ew = ew / jnp.sum(ew, axis=-1, keepdims=True)
    eid = (gi * EXPERTS_PER_GROUP + ei).reshape(-1)
    cw = (gw * ew).reshape(-1)
    tok = jnp.repeat(jnp.arange(t, dtype=jnp.int32), TOP_K)
    order = jnp.argsort(eid)
    e_s, tok_s, cw_s = eid[order], tok[order], cw[order]
    counts = jnp.bincount(eid, length=N_EXPERTS)
    padded = (counts + MOE_BLOCK - 1) // MOE_BLOCK * MOE_BLOCK
    pad_end = jnp.cumsum(padded)
    pad_start = pad_end - padded
    cnt_start = jnp.cumsum(counts) - counts
    dest = pad_start[e_s] + jnp.arange(n_assign) - cnt_start[e_s]
    n_blk = -(-n_assign // MOE_BLOCK) + N_EXPERTS
    rows = n_blk * MOE_BLOCK
    buf = jnp.zeros((rows, dm), xt.dtype).at[dest].set(xt[tok_s])
    blk_e = jnp.minimum(jnp.searchsorted(pad_end, jnp.arange(n_blk) * MOE_BLOCK, side='right'),
                        N_EXPERTS - 1)

    def expert_block(args):
        xb, e = args
        hb = jax.nn.silu(xb @ w_gate[e]) * (xb @ w_up[e])
        return hb @ w_down[e]

    out = lax.map(expert_block, (buf.reshape(n_blk, MOE_BLOCK, dm), blk_e)).reshape(rows, dm)
    y = jax.ops.segment_sum(out[dest] * cw_s[:, None].astype(out.dtype), tok_s, num_segments=t)
    return y.reshape(bsz, seq, dm)

def setup_inputs(seed: int = 0) -> dict:
    key = jax.random.key(seed)
    ks = jax.random.split(key, 32)
    f32 = jnp.float32

    def nrm(k, shape, scale):
        return jax.random.normal(k, shape, f32) * scale

    def gain(k, shape):
        return 1.0 + 0.02 * jax.random.normal(k, shape, f32)

    x = jax.random.normal(ks[0], (BATCH, SEQ, D_MODEL), f32)
    offset = jax.random.randint(ks[1], (BATCH, 1), 0, 4096, dtype=jnp.int32)
    positions = offset + jnp.arange(SEQ, dtype=jnp.int32)[None, :]
    a8 = jax.random.uniform(ks[2], (DEPTH, LRU_W), f32, minval=0.9, maxval=0.999)
    s = a8 ** (1.0 / LRU_C)
    lru_lambda = jnp.log(s) - jnp.log1p(-s)
    return {
        "x": x,
        "positions": positions,
        "norm1_g": gain(ks[3], (DEPTH, D_MODEL)),
        "w_in": nrm(ks[4], (DEPTH, D_MODEL, D_IN), D_MODEL ** -0.5),
        "lru_conv_w": nrm(ks[5], (DEPTH, CONV_W, LRU_W), CONV_W ** -0.5),
        "lru_conv_b": nrm(ks[6], (DEPTH, LRU_W), 0.02),
        "lru_wr": nrm(ks[7], (DEPTH, LRU_BLOCKS, LRU_BLK, LRU_BLK), LRU_BLK ** -0.5),
        "lru_br": nrm(ks[8], (DEPTH, LRU_W), 0.02),
        "lru_wi": nrm(ks[9], (DEPTH, LRU_BLOCKS, LRU_BLK, LRU_BLK), LRU_BLK ** -0.5),
        "lru_bi": nrm(ks[10], (DEPTH, LRU_W), 0.02),
        "lru_lambda": lru_lambda,
        "lru_out_g": gain(ks[11], (DEPTH, LRU_W)),
        "gla_wa2": nrm(ks[12], (DEPTH, GLA_RANK, GLA_HEADS * GLA_DK), GLA_RANK ** -0.5),
        "gla_ba": nrm(ks[13], (DEPTH, GLA_HEADS * GLA_DK), 0.02),
        "gla_norm_g": gain(ks[14], (DEPTH, GLA_DV)),
        "swa_q_norm_g": gain(ks[15], (DEPTH, HEAD_DIM)),
        "swa_k_norm_g": gain(ks[16], (DEPTH, HEAD_DIM)),
        "swa_sinks": nrm(ks[17], (DEPTH, SWA_HEADS), 0.5),
        "swa_out_g": gain(ks[18], (DEPTH, SWA_W)),
        "w_out": nrm(ks[19], (DEPTH, D_MIX, D_MODEL), D_MIX ** -0.5),
        "norm2_g": gain(ks[20], (DEPTH, D_MODEL)),
        "moe_wg": nrm(ks[21], (DEPTH, D_MODEL, N_GROUPS), D_MODEL ** -0.5),
        "moe_bg": nrm(ks[22], (DEPTH, N_GROUPS), 0.01),
        "moe_we": nrm(ks[23], (DEPTH, D_MODEL, N_EXPERTS), D_MODEL ** -0.5),
        "moe_be": nrm(ks[24], (DEPTH, N_EXPERTS), 0.01),
        "moe_w_gate": nrm(ks[25], (DEPTH, N_EXPERTS, D_MODEL, EXPERT_FF), D_MODEL ** -0.5),
        "moe_w_up": nrm(ks[26], (DEPTH, N_EXPERTS, D_MODEL, EXPERT_FF), D_MODEL ** -0.5),
        "moe_w_down": nrm(ks[27], (DEPTH, N_EXPERTS, EXPERT_FF, D_MODEL), EXPERT_FF ** -0.5),
    }

def reference(x, positions, norm1_g, w_in, lru_conv_w, lru_conv_b, lru_wr, lru_br, lru_wi, lru_bi,
              lru_lambda, lru_out_g, gla_wa2, gla_ba, gla_norm_g, swa_q_norm_g, swa_k_norm_g,
              swa_sinks, swa_out_g, w_out, norm2_g, moe_wg, moe_bg, moe_we, moe_be,
              moe_w_gate, moe_w_up, moe_w_down):
    cos, sin = _rope_tables(positions)
    splits = _split_points(IN_SIZES)
    for l in range(DEPTH):
        h = _rmsnorm(x, norm1_g[l])
        z = h @ w_in[l]
        a_x, a_g, b_q, b_k, b_v, b_g, b_a, c_q, c_k, c_v = jnp.split(z, splits, axis=-1)
        y_a = _rglru_group(a_x, a_g, lru_conv_w[l], lru_conv_b[l], lru_wr[l], lru_br[l],
                           lru_wi[l], lru_bi[l], lru_lambda[l], lru_out_g[l])
        y_b = _gla_group(b_q, b_k, b_v, b_g, b_a, gla_wa2[l], gla_ba[l], gla_norm_g[l])
        y_c = _swa_group(c_q, c_k, c_v, cos, sin, swa_q_norm_g[l], swa_k_norm_g[l],
                         swa_sinks[l], swa_out_g[l])
        x = x + jnp.concatenate([y_a, y_b, y_c], axis=-1) @ w_out[l]
        x = x + _hier_moe(_rmsnorm(x, norm2_g[l]), moe_wg[l], moe_bg[l], moe_we[l], moe_be[l],
                          moe_w_gate[l], moe_w_up[l], moe_w_down[l])
    return x


_drawn_inputs = setup_inputs


def setup_inputs(seed=0):
    import zlib

    import numpy as np

    out = dict(_drawn_inputs(seed))
    spreads = {}
    factors = {'lru_br': 8.0,
     'lru_bi': 6.737,
     'lru_out_g': 15.582,
     'gla_ba': 5.748,
     'gla_norm_g': 24.681,
     'swa_q_norm_g': 3.315,
     'swa_sinks': 29.559,
     'swa_out_g': 11.062,
     'moe_bg': 18.954,
     'moe_be': 21.499,
     'norm2_g': 5.361}
    for name, (base, spread) in spreads.items():
        noise = np.random.default_rng([zlib.crc32(name.encode()), seed]).standard_normal(out[name].shape)
        drawn = base * np.exp(spread * noise) if base else spread * noise
        out[name] = jnp.asarray(drawn.astype(out[name].dtype))
    for name, factor in factors.items():
        out[name] = (out[name] * factor).astype(out[name].dtype)
    return out
```

```python
from contextlib import ExitStack

import numpy as np

import concourse.bass as bass
from concourse import mybir

ALU = mybir.AluOpType
ACT = mybir.ActivationFunctionType
AX = mybir.AxisListType.X
F32 = mybir.dt.float32
BF16 = mybir.dt.bfloat16
I32 = mybir.dt.int32

P = 128
T = 1024
D = 1024
NT = T // P
KD = D // P
BANK = 512
CHUNK = 64
NCH = T // CHUNK
EPS = 1e-6

LRU_W = 256
LRU_BLK = 64
CONV_W = 4
GLA_H, GLA_DK, GLA_DV, GLA_R = 4, 32, 64, 16
SWA_H, SWA_KV, HD = 8, 2, 64
SWA_W = SWA_H * HD
HALF = HD // 2

C_A = 0
C_BQ = 2 * LRU_W
C_BV = C_BQ + 2 * GLA_H * GLA_DK
C_BA = C_BV + 2 * GLA_H * GLA_DV
C_CQ = C_BA + GLA_R
C_CK = C_CQ + SWA_W
C_CV = C_CK + SWA_KV * HD
QK = SWA_W + SWA_KV * HD
NQK = QK // HD
AV = GLA_R + SWA_KV * HD

NG, EPG, NE, TOPK = 4, 8, 32, 2
FF = 512
KF = FF // P
NR = NG + NE
NOVF = (T * TOPK - 1) // (P + 1)
NBLK = NE + NOVF
BIG = 1.0e30
GLA_CLAMP = 43.0
GLA_TAU = 16.0

TWO_PI = 2.0 * np.pi
PI_A = 6.28125
PI_B = float(np.float32(np.round((TWO_PI - PI_A) * 2.0**21) / 2.0**21))
PI_C = float(TWO_PI - PI_A - PI_B)
ROUND = 12582912.0
PI_SAFE = 3.1415925


def build(nc, a, out):
    with ExitStack() as ctx:
        def sb(name, shape, dt=F32):
            return ctx.enter_context(nc.sbuf_tensor(name, shape, dt))

        def sem(name):
            return ctx.enter_context(nc.semaphore(name))

        x_d = a["x"][0]
        w_in = a["w_in"][0]
        w_out = a["w_out"][0]
        w_gate = a["moe_w_gate"][0]
        w_up = a["moe_w_up"][0]
        w_down = a["moe_w_down"][0]
        out_d = out[0]
        xn_d = nc.dram_tensor("xn_scratch", [T, D], F32)[:, :]
        slot_d = nc.dram_tensor("slot_table", [P * NBLK, 1], I32)
        y_d = nc.dram_tensor("expert_rows", [NBLK * P, D], F32)[:, :]

        ring = sb("ring", [P, 5, KD * BANK])
        hT = sb("hT", [P, KD, T])
        zA = sb("zA", [P, 4, T])
        zG = sb("zG", [P, 2, T])
        late = sb("late", [P, 9216])
        zAV = sb("zAV", [P, NT, AV])
        uc = sb("uc", [P, 2, T])
        kT = sb("kT", [P, T])
        wa_sb = sb("wa_sb", [P, KD, GLA_R])
        ident = sb("ident", [P, P])
        ones = sb("ones", [P, P])
        cmask = sb("cmask", [P, P])
        ltri = sb("ltri", [P, P], BF16)
        onesb = sb("onesb", [P, P], BF16)
        hm = sb("hm", [P, GLA_H])
        wrbd = sb("wrbd", [P, 2, P])
        wibd = sb("wibd", [P, 2, P])
        wa2 = sb("wa2", [GLA_R, P])
        rw = sb("rw", [P, KD, NR])
        rb = sb("rb", [P, NR])
        qg = sb("qg", [P, HD])
        kg = sb("kg", [P, HD])
        g1 = sb("g1", [P, KD])
        g2 = sb("g2", [P, KD])
        cw = sb("cw", [P, CONV_W, 2])
        cb = sb("cb", [P, 2])
        br = sb("br", [P, 2])
        bi = sb("bi", [P, 2])
        lam = sb("lam", [P, 2])
        lrug = sb("lrug", [P, 2])
        ba = sb("ba", [P, 1])
        glag = sb("glag", [P, 1])
        swag = sb("swag", [P, 4])
        sinks = sb("sinks", [P, 4])
        posi = sb("posi", [P, NT], I32)
        sp = sb("sp", [P, 8, 2])
        cos = sb("cos", [P, NT, HALF])
        sin = sb("sin", [P, NT, HALF])
        eps = sb("eps", [P, 1])
        half_neg = sb("half_neg", [P, NQK])
        ss = sb("ss", [P, NT])
        rs = sb("rs", [P, NT])
        dec = sb("dec", [P, NCH])
        kdt = sb("kdt", [P, 2, P])
        vE = sb("vE", [P, 2, P])
        qst = sb("qst", [P, 2, NQK])
        sst = sb("sst", [P, 6, 8])
        gst = sb("gst", [P, 2, GLA_H])
        ra = sb("ra", [P, NT])
        rc = sb("rc", [P, NT])
        desc_i = sb("desc_i", [P, NE], I32)
        desc = sb("desc", [P, NE])
        jrow = sb("jrow", [P, NOVF])
        addr_i = sb("addr_i", [P, TOPK, NT], I32)
        orow_i = sb("orow_i", [P, TOPK, NT], I32)
        wts = sb("wts", [P, TOPK, NT])
        obuf = sb("obuf", [P, 2, 256])
        idx = sb("idx", [P, NBLK], I32)
        idxc = sb("idxc", [P, 2, 1], I32)
        tokid = sb("tokid", [P, NT], I32)
        ctrl = sb("ctrl", [P, 16], I32)

        xs = late[:, 0:NT * D].rearrange("p (t d) -> p t d", t=NT)
        x2 = xs
        zVG = late[:, 0:NT * 512].rearrange("p (t c) -> p t c", t=NT)
        zQ = late[:, NT * 512:NT * 512 + NT * QK].rearrange("p (t c) -> p t c", t=NT)
        ri = late[:, 0:4 * T].rearrange("p (n t) -> p n t", n=4)
        GB = ring[:, 2, :].rearrange("p (n t) -> p n t", n=4)
        wA = ring[:, 0, :].rearrange("p (k n) -> p k n", k=KD)
        wQK = ring[:, 1, 0:KD * 256].rearrange("p (k n) -> p k n", k=KD)
        wKV = ring[:, 1, KD * 256:KD * 512].rearrange("p (k n) -> p k n", k=KD)
        wQ = ring[:, 3, :].rearrange("p (k n) -> p k n", k=KD)
        wVG = ring[:, 4, :].rearrange("p (k n) -> p k n", k=KD)
        wO = [ring[:, n, :].rearrange("p (k n) -> p k n", k=KD) for n in range(2)]
        Pb = zA[:, 0, :].rearrange("p (n k) -> p n k", n=8)
        ysq = zA[:, 1, 0:512].rearrange("p (n k) -> p n k", n=4)
        vkm = zA[:, 1, 512:768]
        PT = uc[:, 0, :].rearrange("p (n k) -> p n k", n=8)
        qT = uc[:, 1, :].rearrange("p (b c n q) -> p b c n q", b=2, c=2, n=4)
        qx = zG[:, 0, 0:512].rearrange("p (h t) -> p h t", h=GLA_H)
        attT = zG[:, 0, 512:1024].rearrange("p (h t) -> p h t", h=GLA_H)
        St = zG[:, 1, :].rearrange("p (n v) -> p n v", n=4)
        sqs = sb("sqs", [P, QK])
        rt = sqs[:, :].rearrange("p (n h d) -> p n h d", n=2, d=HALF)

        xn = [zG[:, b, :] for b in range(2)]
        h2T = [zA[:, b, :].rearrange("p (k t) -> p k t", k=KD) for b in range(2)]
        route = kT
        slots = [ring[:, 3, :], ring[:, 4, :], ring[:, 2, :],
                 hT[:, 0:4, :].rearrange("p k t -> p (k t)"), ring[:, 0, :], ring[:, 1, :]]
        xg = [hT[:, 4 + b, :] for b in range(2)]
        xT = [hT[:, 6 + b, :].rearrange("p (k t) -> p k t", k=KD) for b in range(2)]
        yo = [zA[:, b, :] for b in range(2)]
        sg = zA[:, 2, 0:FF]
        hb = zA[:, 2, FF:2 * FF]
        hbT = zA[:, 3, 0:FF].rearrange("p (k t) -> p k t", k=KF)
        back = [ring[:, n // 4, (n % 4) * D:(n % 4 + 1) * D] for n in range(16)]

        bank = [ctx.enter_context(nc.psum_tensor(f"bank{i}", [P, BANK], F32)) for i in range(8)]

        x_in = [sem(f"x_in{t}") for t in range(NT)]
        c_in = sem("c_in")
        c_late = sem("c_late")
        w_in_full = [sem(f"w_in_full{n}") for n in range(6)]
        w_out_full = [sem(f"w_out_full{n}") for n in range(2)]
        const_ready = sem("const_ready")
        wbd_zero = sem("wbd_zero")
        x_ss = sem("x_ss")
        x_rs = sem("x_rs")
        x_scaled = sem("x_scaled")
        xT_ps = sem("xT_ps")
        hT_ready = sem("hT_ready")
        proj_ps = sem("proj_ps")
        proj_out = sem("proj_out")
        dv = sem("dv")
        av = sem("av")
        pv_ = sem("pool_chain")
        conv_done = sem("conv_done")
        lru_ps = sem("lru_ps")
        lru_sig = sem("lru_sig")
        lru_iu = sem("lru_iu")
        lru_tanh = sem("lru_tanh")
        lru_m2 = sem("lru_m2")
        lru_sqrt = sem("lru_sqrt")
        lru_gelu = sem("lru_gelu")
        lru_y = sem("lru_y")
        lru_ysq = sem("lru_ysq")
        lru_sum = sem("lru_sum")
        lru_rs = sem("lru_rs")
        lru_done = sem("lru_done")
        lam_e = sem("lam_e")
        lam_in = sem("lam_in")
        c8_ready = sem("c8_ready")
        rope_arg = sem("rope_arg")
        rope_ready = sem("rope_ready")
        aT_ps = sem("aT_ps")
        aT_out = sem("aT_out")
        alpha_ps = sem("alpha_ps")
        gla_na = sem("gla_na")
        gla_ln = sem("gla_ln")
        gla_b = sem("gla_b")
        gla_exp = sem("gla_exp")
        gla_prep = sem("gla_prep")
        qk_sq = sem("qk_sq")
        qk_ss = sem("qk_ss")
        qk_rs = sem("qk_rs")
        qk_scaled = sem("qk_scaled")
        qk_gained = sem("qk_gained")
        qk_ready = sem("qk_ready")
        t1_ps = sem("t1_ps")
        t1_out = sem("t1_out")
        s_ps = sem("s_ps")
        s_negm = sem("s_negm")
        p_exp = sem("p_exp")
        p_ready = sem("p_ready")
        pt_ps = sem("pt_ps")
        pt_out = sem("pt_out")
        vE_ready = sem("vE_ready")
        pv_ps = sem("pv_ps")
        yc_sq = sem("yc_sq")
        yc_raw = sem("yc_raw")
        ysum_ps = sem("ysum_ps")
        ysum_out = sem("ysum_out")
        yc_rs = sem("yc_rs")
        qx_ready = sem("qx_ready")
        att_ps = sem("att_ps")
        att_out = sem("att_out")
        kv_ps = sem("kv_ps")
        st_ready = sem("st_ready")
        o_ps = sem("o_ps")
        o_sq = sem("o_sq")
        o_ss = sem("o_ss")
        o_rs = sem("o_rs")
        o_tanh = sem("o_tanh")
        o_ready = sem("o_ready")
        yb_ps = sem("yb_ps")
        yb_ready = sem("yb_ready")
        wo_ps = sem("wo_ps")
        x2_ready = sem("x2_ready")
        x2_ss = sem("x2_ss")
        x2_rs = sem("x2_rs")
        xn_ready = sem("xn_ready")
        xn_stored = [sem(f"xn_stored{b}") for b in range(2)]
        xn_ps = sem("xn_ps")
        h2T_ready = sem("h2T_ready")
        lg_ps = sem("lg_ps")
        lg_out = sem("lg_out")
        rt_arg = sem("rt_arg")
        rt_exp = sem("rt_exp")
        hot_ready = sem("hot_ready")
        rank_ps = sem("rank_ps")
        addr_ready = sem("addr_ready")
        ctrl_ready = sem("ctrl_ready")
        slot_zero = sem("slot_zero")
        slot_put = sem("slot_put")
        slot_back = sem("slot_back")
        fill_stored = sem("fill_stored")
        e_w = [sem(f"e_w{m}") for m in range(6)]
        e_x = [sem(f"e_x{b}") for b in range(2)]
        y_stored = [sem(f"y_stored{b}") for b in range(2)]
        (e_xps, e_col, e_xT, e_gate, e_up, e_sg, e_hb, e_hps, e_hT, e_down, e_ya, e_yb,
         turn, o_w, o_x, o_xps, o_xT, o_gu, o_sg, o_hb, o_hps, o_hT, o_down, o_y, o_stored, out_ready,
         out_stored) = (sem(n) for n in (
             "e_xps", "e_col", "e_xT", "e_gate", "e_up", "e_sg", "e_hb", "e_hps", "e_hT", "e_down", "e_ya", "e_yb",
             "turn", "o_w", "o_x", "o_xps", "o_xT", "o_gu", "o_sg", "o_hb", "o_hps", "o_hT", "o_down", "o_y", "o_stored",
             "out_ready", "out_stored"))
        back_in = [sem(f"back_in{t}") for t in range(NT)]

        block = ctx.enter_context(nc.Block())

        C_LATE = 16 * 24
        PROJ_A, PROJ_G, PROJ_KV, PROJ_Q, PROJ_VG = 0, 8, 12, 20, 28

        def rows(w, c0, n):
            return w[:, c0:c0 + n].rearrange("(k p) n -> p k n", p=P)

        def bc(ap, shape):
            return ap.to_broadcast(shape)

        @block.sync
        def _(sp_):
            for t in range(NT):
                sp_.dma_start(xs[:, t, :], x_d[t * P:(t + 1) * P, :]).then_inc(x_in[t], 16)
                if t == 3:
                    sp_.dma_start(wA, rows(w_in, C_A, 512)).then_inc(w_in_full[0], 16)
            sp_.dma_start(wQK, rows(w_in, C_BQ, 256)).then_inc(w_in_full[1], 16)
            sp_.dma_start(wKV, rows(w_in, C_CK, 256)).then_inc(w_in_full[2], 16)
            sp_.dma_start(wa_sb[:, :, :], rows(w_in, C_BA, GLA_R)).then_inc(w_in_full[3], 16)
            sp_.dma_start(wQ, rows(w_in, C_CQ, 512)).then_inc(w_in_full[4], 16)
            sp_.dma_start(wVG, rows(w_in, C_BV, 512)).then_inc(w_in_full[5], 16)
            sp_.wait_ge(w_in_full[0], 16)
            fills = range(0, NOVF, 4)
            for j in fills:
                m = min(4, NOVF - j)
                sp_.dma_start(y_d[(NE + j) * P:(NE + j + m) * P, :].rearrange("(b p) d -> p b d", p=P),
                              ring[:, 0, 0:m * D].rearrange("p (b d) -> p b d", b=m)).then_inc(fill_stored, 16)
            sp_.wait_ge(fill_stored, 16 * len(fills))
            sp_.wait_ge(proj_ps, PROJ_G)
            sp_.dma_start(wO[0], rows(w_out, 0, 512)).then_inc(w_out_full[0], 16)
            sp_.wait_ge(proj_ps, PROJ_Q)
            sp_.dma_start(wO[1], rows(w_out, 512, 512)).then_inc(w_out_full[1], 16)

            def expert_unit(m, e, s_):
                w = (w_gate, w_up, w_down)[m % 3]
                src = w[e] if isinstance(e, int) else w[bass.ds(e, 1)].rearrange("o r c -> (o r) c")
                k = KF if m % 3 == 2 else KD
                sp_.dma_start(slots[m].rearrange("p (k n) -> p k n", k=k),
                              src.rearrange("(k p) n -> p k n", p=P)).then_inc(s_, 16)

            sp_.wait_ge(proj_ps, PROJ_VG)
            expert_unit(0, 0, e_w[0])
            sp_.wait_ge(yb_ps, NT)
            sp_.wait_ge(qk_ready, NT)
            sp_.wait_ge(t1_ps, NT)
            sp_.wait_ge(yc_sq, NT)
            for t in range(NT):
                sp_.dma_start(x2[:, t, :], x_d[t * P:(t + 1) * P, :]).then_inc(x_in[t], 16)
            for m in (1, 2):
                expert_unit(m, 0, e_w[m])
            for t in range(NT):
                sp_.wait_ge(xn_ready, t + 1)
                sp_.dma_start(xn_d[t * P:(t + 1) * P, :], xn[t % 2]).then_inc(xn_stored[t % 2], 16)
            sp_.wait_ge(wo_ps, 2 * NT)
            for m in (3, 4, 5):
                expert_unit(m, 1, e_w[m])
            with sp_.Fori(0, NE // 2 - 1) as i:
                for m in range(6):
                    e = 2 * i + m // 3
                    if m % 3 == 2:
                        sp_.wait_ge(e_down, 2 * e + 2)
                    else:
                        sp_.wait_ge(e_up if m % 3 else e_gate, e + 1)
                    expert_unit(m, 2 * i + (2 + m // 3), e_w[m])
            sp_.wait_ge(e_down, 2 * NE)
            sp_.wait_ge(ctrl_ready, 1)
            n_ovf = sp_.value_load(ctrl[0:1, 0:1], min_val=0, max_val=NOVF)
            with sp_.Fori(0, NOVF) as j:
                with sp_.If(j < n_ovf):
                    e = sp_.value_load(ctrl[0:1, bass.ds(j + 1, 1)], min_val=0, max_val=NE - 1)
                    for m in range(3):
                        expert_unit(m, e, o_w)
                    sp_.wait_ge(o_down, j + 1)
                    sp_.sem_inc(turn, 1)
                sp_.nop()
            for t in range(NT):
                sp_.wait_ge(out_ready, t + 1)
                sp_.dma_start(out_d[t * P:(t + 1) * P, :], x2[:, t, :]).then_inc(out_stored, 16)
            sp_.wait_ge(out_stored, 16 * NT)

        @block.gpsimd
        def _(pool):
            n = [0]

            def link(ins):
                n[0] += 1
                ins.then_inc(pv_, 1)
                pool.wait_ge(pv_, n[0])

            link(nc.gpsimd.memset(ident[:], 0.0))
            link(nc.gpsimd.affine_select(out=ident[:], in_=ident[:], compare_op=ALU.not_equal, fill=1.0, base=0,
                                         pattern=[[-1, P]], channel_multiplier=1))
            link(nc.gpsimd.memset(half_neg[:], -0.5))
            link(nc.gpsimd.memset(eps[:], EPS))
            nc.gpsimd.memset(ones[:], 1.0).then_inc(const_ready, 1)
            pool.wait_ge(const_ready, 1)
            link(nc.gpsimd.memset(wrbd[:], 0.0))
            nc.gpsimd.memset(wibd[:], 0.0).then_inc(wbd_zero, 1)
            pool.wait_ge(wbd_zero, 1)
            link(nc.gpsimd.memset(onesb[:], 1.0))
            link(nc.gpsimd.memset(cmask[:], 1.0))
            link(nc.gpsimd.affine_select(out=cmask[:], in_=cmask[:], compare_op=ALU.is_ge, fill=0.0, base=0,
                                         pattern=[[1, P]], channel_multiplier=-1))
            link(nc.gpsimd.memset(cmask[0:CHUNK, CHUNK:P], 0.0))
            link(nc.gpsimd.memset(ltri[:], 1.0))
            link(nc.gpsimd.affine_select(out=ltri[:], in_=ltri[:], compare_op=ALU.is_ge, fill=0.0, base=-1,
                                         pattern=[[1, P]], channel_multiplier=-1))
            link(nc.gpsimd.memset(hm[:], 0.0))
            for h in range(GLA_H):
                link(nc.gpsimd.memset(hm[32 * h:32 * h + 32, h:h + 1], 1.0))
            link(nc.gpsimd.iota(tokid[:], [[P, NT]], base=0, channel_multiplier=1))
            link(nc.gpsimd.iota(desc_i[:], [[-1, NE]], base=NE, channel_multiplier=0))
            link(nc.gpsimd.memset(idx[:], 0))
            nc.gpsimd.memset(vE[CHUNK:P, 0, :], 0.0).then_inc(const_ready, 1)
            pool.wait_ge(const_ready, 2)

            def rstd_x(t):
                pool.wait_ge(x_ss, t + 1)
                link(nc.gpsimd.tensor_scalar(rs[:, t:t + 1], ss[:, t:t + 1], 1.0 / D, EPS, ALU.mult, ALU.add))
                nc.gpsimd.tensor_tensor(rs[:, t:t + 1], rs[:, t:t + 1], half_neg[:, 0:1], ALU.pow).then_inc(x_rs, 1)

            for t in range(NT):
                rstd_x(t)
            pool.dma_start(slot_d[:, :].rearrange("(p b) o -> p (b o)", p=P), idx[:, :]).then_inc(slot_zero, 16)

            def qk_norm(t):
                pool.wait_ge(qk_ss, t + 1)
                link(nc.gpsimd.tensor_scalar(qst[:, 1, :], qst[:, 0, :], 1.0 / HD, EPS, ALU.mult, ALU.add))
                nc.gpsimd.tensor_tensor(qst[:, 1, :], qst[:, 1, :], half_neg[:, 0:NQK], ALU.pow).then_inc(qk_rs, 1)
                pool.wait_ge(qk_scaled, t + 1)
                q3 = zQ[:, t, 0:SWA_W].rearrange("p (h d) -> p h d", d=HD)
                k3 = zQ[:, t, SWA_W:QK].rearrange("p (h d) -> p h d", d=HD)
                link(nc.gpsimd.tensor_tensor(q3, q3, bc(qg[:, :].unsqueeze(1), [P, SWA_H, HD]), ALU.mult))
                nc.gpsimd.tensor_tensor(k3, k3, bc(kg[:, :].unsqueeze(1), [P, SWA_KV, HD]),
                                        ALU.mult).then_inc(qk_gained, 1)

            pool.wait_ge(c_late, C_LATE)
            qk_norm(0)
            pool.wait_ge(qk_gained, 1)
            pool.wait_ge(lru_sum, 1)
            nc.gpsimd.tensor_tensor(ra[:], ra[:], half_neg[:, 0:NT], ALU.pow).then_inc(lru_rs, 1)
            pool.wait_ge(lru_rs, 1)
            qk_norm(1)
            pool.wait_ge(qk_gained, 2)

            def yc_rstd(t):
                pool.wait_ge(ysum_out, t + 1)
                nc.gpsimd.tensor_tensor(rc[:, t:t + 1], rc[:, t:t + 1], half_neg[:, 0:1], ALU.pow).then_inc(yc_rs, 1)
                pool.wait_ge(yc_rs, t + 1)

            for s in range(NT):
                if s >= 1:
                    if s >= 2:
                        pool.wait_ge(pv_ps, s - 1)
                    link(nc.gpsimd.tensor_copy(vE[CHUNK:P, s % 2, :], zAV[CHUNK:P, s - 1, GLA_R:AV]))
                nc.gpsimd.tensor_copy(vE[0:CHUNK, s % 2, :], zAV[0:CHUNK, s, GLA_R:AV]).then_inc(vE_ready, 1)
                pool.wait_ge(vE_ready, s + 1)
                if s >= 1:
                    yc_rstd(s - 1)
                if s + 2 < NT:
                    qk_norm(s + 2)
                pool.wait_ge(o_ss, s + 1)
                link(nc.gpsimd.tensor_scalar(gst[:, 1, :], gst[:, 0, :], 1.0 / GLA_DV, EPS, ALU.mult, ALU.add))
                nc.gpsimd.tensor_tensor(gst[:, 1, :], gst[:, 1, :], half_neg[:, 0:GLA_H],
                                        ALU.pow).then_inc(o_rs, 1)
                pool.wait_ge(o_rs, s + 1)
            yc_rstd(NT - 1)

            for t in range(NT):
                pool.wait_ge(x2_ss, t + 1)
                link(nc.gpsimd.tensor_scalar(rs[:, t:t + 1], ss[:, t:t + 1], 1.0 / D, EPS, ALU.mult, ALU.add))
                nc.gpsimd.tensor_tensor(rs[:, t:t + 1], rs[:, t:t + 1], half_neg[:, 0:1],
                                        ALU.pow).then_inc(x2_rs, 1)

                pool.wait_ge(x2_rs, t + 1)

            pool.wait_ge(slot_zero, 16)
            pool.wait_ge(addr_ready, 2)
            for k in range(TOPK):
                for t in range(NT):
                    nc.gpsimd.indirect_dma_start(
                        out=slot_d[:, :], out_offset=bass.IndirectOffsetOnAxis(ap=addr_i[:, k, t:t + 1], axis=0),
                        in_=tokid[:, t:t + 1], in_offset=None).then_inc(slot_put, 16)
            pool.wait_ge(slot_put, 16 * TOPK * NT)
            pool.dma_start(idx[:, :], slot_d[:, :].rearrange("(p b) o -> p (b o)", p=P)).then_inc(slot_back, 16)
            pool.wait_ge(slot_back, 16)
            for b in range(2):
                pool.wait_ge(xn_stored[b], 16 * NT // 2)

            def gather(col, nth, b, s_):
                nc.gpsimd.tensor_copy(idxc[:, b, :], idx[:, bass.ds(col, 1)]).then_inc(e_col, 1)
                pool.wait_ge(e_col, nth)
                pool.sem_inc(turn, 1)
                nc.gpsimd.indirect_dma_start(
                    out=xg[b], out_offset=None, in_=xn_d,
                    in_offset=bass.IndirectOffsetOnAxis(ap=idxc[:, b, :], axis=0)).then_inc(s_, 16)

            for b in range(2):
                gather(b, b + 1, b, e_x[b])
            with pool.Fori(1, NE // 2) as i:
                for b in range(2):
                    e = 2 * i + b
                    pool.wait_ge(e_xps, 2 * e - 2)
                    gather(e, e + 1, b, e_x[b])
            pool.wait_ge(e_xps, 2 * NE - 2)
            gather(NE, NE + 1, 0, e_x[0])
            pool.wait_ge(e_xps, 2 * (NE + 1))
            pool.wait_ge(ctrl_ready, 1)
            n_ovf = pool.value_load(ctrl[0:1, 0:1], min_val=0, max_val=NOVF)
            with pool.Fori(0, NOVF) as j:
                with pool.If(j < n_ovf):
                    gather(j + NE, j + (NE + 2), 1, o_x)
                    pool.wait_ge(o_stored, 16 * j + 16)
                    pool.sem_inc(turn, 1)
                pool.nop()
            pool.wait_ge(e_down, 2 * NE)
            for b in range(2):
                pool.wait_ge(y_stored[b], 16 * (NE // 2) + 16)
            for t in range(NT):
                for k in range(TOPK):
                    nc.gpsimd.indirect_dma_start(
                        out=back[TOPK * t + k], out_offset=None, in_=y_d,
                        in_offset=bass.IndirectOffsetOnAxis(ap=orow_i[:, k, t:t + 1], axis=0)).then_inc(back_in[t], 16)


        @block.scalar
        def _(act):
            n = [0]

            def link(ins):
                n[0] += 1
                ins.then_inc(av, 1)
                act.wait_ge(av, n[0])

            def col(dst, src, k, s=c_late):
                act.dma_start(dst, src.rearrange("(k p) -> p k", p=P), allow_slow_non_contiguous=True).then_inc(s, 16)

            act.wait_ge(const_ready, 1)
            col(g1[:, :], a["norm1_g"][0], KD, c_in)
            act.dma_start(posi[:, :], a["positions"][0].rearrange("(k p) -> p k", p=P),
                          allow_slow_non_contiguous=True).then_inc(c_late, 16)
            for tap in range(CONV_W):
                col(cw[:, tap, :], a["lru_conv_w"][0, tap], 2)
            col(cb[:, :], a["lru_conv_b"][0], 2)
            col(br[:, :], a["lru_br"][0], 2)
            col(bi[:, :], a["lru_bi"][0], 2)
            col(lam[:, :], a["lru_lambda"][0], 2)
            col(lrug[:, :], a["lru_out_g"][0], 2)
            col(ba[:, :], a["gla_ba"][0], 1)
            col(swag[:, :], a["swa_out_g"][0], 4)
            col(g2[:, :], a["norm2_g"][0], KD)

            for t in range(NT):
                act.wait_ge(x_in[t], 16)
                if t:
                    act.wait_ge(x_ss, t)
                nc.scalar.activation(uc[:, 0, :], xs[:, t, :], ACT.Square,
                                     accum_out=ss[:, t:t + 1]).then_inc(x_ss, 1)
            for i in range(2):
                act.dma_start(glag[64 * i:64 * i + 64, :], a["gla_norm_g"][0].rearrange("(p o) -> p o", o=1),
                              allow_slow_non_contiguous=True).then_inc(c_late, 16)
                act.dma_start(sinks[64 * i:64 * i + 64, :],
                              bc(a["swa_sinks"][:, i:SWA_H:2], [64, 4]),
                              allow_slow_non_contiguous=True).then_inc(c_late, 16)
            act.dma_start(qg[:, :], bc(a["swa_q_norm_g"][:, :], [P, HD])).then_inc(c_late, 16)
            act.dma_start(kg[:, :], bc(a["swa_k_norm_g"][:, :], [P, HD])).then_inc(c_late, 16)
            act.dma_start(rb[:, 0:NG], bc(a["moe_bg"][:, :], [P, NG])).then_inc(c_late, 16)
            act.dma_start(rb[:, NG:NR], bc(a["moe_be"][:, :], [P, NE])).then_inc(c_late, 16)
            act.dma_start(wa2[:, :], a["gla_wa2"][0]).then_inc(c_late, 16)
            act.dma_start(rw[:, :, 0:NG], rows(a["moe_wg"][0], 0, NG)).then_inc(c_late, 16)
            act.dma_start(rw[:, :, NG:NR], rows(a["moe_we"][0], 0, NE)).then_inc(c_late, 16)
            act.wait_ge(wbd_zero, 1)
            for blk in range(4):
                j, r = blk // 2, 64 * (blk % 2)
                act.dma_start(wrbd[r:r + 64, j, r:r + 64], a["lru_wr"][0, blk]).then_inc(lam_in, 16)
                act.dma_start(wibd[r:r + 64, j, r:r + 64], a["lru_wi"][0, blk]).then_inc(lam_in, 16)

            def evac(u, dst, src=None):
                act.wait_ge(proj_ps, u + 1)
                nc.scalar.copy(dst, bank[u % 2][:, :] if src is None else src).then_inc(proj_out, 1)

            def evac_q(t):
                u = PROJ_Q + t
                evac(u, zQ[:, t, 0:SWA_W].rearrange("p (h g d) -> p g h d", g=2, d=HD),
                     bank[u % 2][:, :].rearrange("p (g h d) -> p g h d", g=2, d=HD))

            def evac_kv(t):
                b = bank[(PROJ_KV + t) % 2]
                act.wait_ge(proj_ps, PROJ_KV + t + 1)
                nc.scalar.copy(zQ[:, t, SWA_W:QK], b[:, 0:128])
                nc.scalar.copy(zAV[:, t, GLA_R:AV], b[:, 128:256])
                nc.scalar.copy(zAV[:, t, 0:GLA_R], b[:, 256:256 + GLA_R]).then_inc(proj_out, 1)

            for m in range(4):
                evac(m, zA[:, m, 0:BANK])
            act.wait_ge(c_late, C_LATE)
            act.wait_ge(c_in, 16)
            act.wait_ge(rope_arg, 1)
            nc.scalar.activation(sin[:, :, :], zG[:, 0, 0:256].rearrange("p (t d) -> p t d", t=NT), ACT.Sin)
            nc.scalar.activation(cos[:, :, :], zG[:, 1, 0:256].rearrange("p (t d) -> p t d", t=NT),
                                 ACT.Sin).then_inc(rope_ready, 1)
            act.wait_ge(lam_e, 1)
            nc.scalar.activation(sp[:, 1, :], sp[:, 0, :], ACT.Exp).then_inc(lam_e, 1)
            for m in range(4):
                evac(4 + m, zA[:, m, BANK:T])
            for hf in range(2):
                for m in range(2):
                    evac(PROJ_G + 2 * hf + m, zG[:, m, hf * BANK:(hf + 1) * BANK])
            for u in range(8):
                j, g, hf = u // 4, u // 2 % 2, u % 2
                act.wait_ge(lru_ps, u + 1)
                nc.scalar.activation(ri[:, 2 * j + g, hf * BANK:(hf + 1) * BANK], bank[2 + u % 6][:, :], ACT.Sigmoid,
                                     bias=(bi if g else br)[:, j:j + 1]).then_inc(lru_sig, 1)
            act.wait_ge(c8_ready, 1)
            act.wait_ge(lru_sig, 8)
            for j in range(2):
                act.wait_ge(conv_done, j + 1)
                link(nc.scalar.activation(zA[:, j, :], ri[:, 2 * j, :], ACT.Tanh, scale=sp[:, 7, j:j + 1]))
                nc.scalar.activation(ri[:, 2 * j, :], ri[:, 2 * j, :], ACT.Exp,
                                     scale=sp[:, 7, j:j + 1]).then_inc(lru_tanh, 1)
            for t in range(2):
                evac_kv(t)
            for j in range(2):
                nc.scalar.activation(zA[:, 2 + j, :], zA[:, 2 + j, :], ACT.Gelu_apprx_tanh).then_inc(lru_gelu, 1)
            for t in range(2, 4):
                evac_kv(t)
            for j in range(2):
                act.wait_ge(lru_m2, j + 1)
                nc.scalar.activation(zA[:, j, :], zA[:, j, :], ACT.Sqrt).then_inc(lru_sqrt, 1)
            for t in range(4, NT):
                evac_kv(t)
            for hf in range(2):
                act.wait_ge(aT_ps, hf + 1)
                nc.scalar.copy(GB[0:GLA_R, 3, hf * BANK:(hf + 1) * BANK],
                               bank[4 + hf][0:GLA_R, :]).then_inc(aT_out, 1)
            for t in range(2):
                evac_q(t)

            def qk_square(t):
                if t >= 1:
                    act.wait_ge(qk_ready, t)
                nc.scalar.activation(sqs[:, :], zQ[:, t, :], ACT.Square).then_inc(qk_sq, 1)

            act.wait_ge(proj_out, PROJ_Q + 1)
            qk_square(0)
            for j in range(2):
                act.wait_ge(lru_y, j + 1)
                nc.scalar.activation(zA[:, j, :], zA[:, 2 + j, :], ACT.Square).then_inc(lru_ysq, 1)
            for t in range(2, 4):
                evac_q(t)
            act.wait_ge(gla_na, 1)
            link(nc.scalar.activation(GB[:, 1, :], GB[:, 1, :], ACT.Exp))
            nc.scalar.activation(GB[:, 1, :], GB[:, 1, :], ACT.Ln, bias=1.0).then_inc(gla_ln, 1)
            qk_square(1)
            for t in range(4, 6):
                evac_q(t)
            act.wait_ge(gla_b, 1)
            b3 = GB[:, 1, :].rearrange("p (c i) -> p c i", i=CHUNK)
            nc.scalar.activation(GB[:, 3, :], GB[:, 0, :], ACT.Exp, scale=1.0 / GLA_TAU).then_inc(gla_exp, 1)
            act.wait_ge(gla_exp, 1)
            nc.scalar.activation(GB[:, 0, :], GB[:, 0, :], ACT.Exp, scale=-1.0 / GLA_TAU).then_inc(gla_exp, 1)
            nc.scalar.activation(GB[:, 2, :], GB[:, 2, :], ACT.Exp, scale=1.0 / GLA_TAU).then_inc(gla_exp, 1)
            link(nc.scalar.activation(dec[:, :].unsqueeze(2), b3[:, :, CHUNK - 1:CHUNK], ACT.Exp,
                                      scale=1.0 / GLA_TAU))
            nc.scalar.activation(GB[:, 1, :], GB[:, 1, :], ACT.Exp, scale=1.0 / GLA_TAU).then_inc(gla_exp, 1)
            for t in range(6, NT):
                evac_q(t)

            def t1_evac(t):
                act.wait_ge(t1_ps, t + 1)
                if t >= 2:
                    act.wait_ge(s_ps, t - 1)
                    act.wait_ge(kv_ps, 2 * t - 2)
                nc.scalar.copy(qT[:, t % 2].rearrange("p c n q -> p n c q"),
                               bank[2][:, :].rearrange("p (n c q) -> p n c q", n=4, c=2))
                nc.scalar.copy(kT[:, t * P:(t + 1) * P], bank[3][:, 0:P])
                nc.scalar.copy(kdt[:, t % 2, :], bank[3][:, P:2 * P]).then_inc(t1_out, 1)

            t1_evac(0)
            for s in range(NT):
                act.wait_ge(s_negm, s + 1)
                if s >= 1:
                    act.wait_ge(pt_ps, s)
                for m in range(8):
                    g, c, pr = m // 4, m // 2 % 2, m % 2
                    w = CHUNK if s == 0 and c == 0 else P
                    nc.scalar.activation(Pb[:, m, 0:w],
                                         bank[4 + g][:, (m % 4) * P:(m % 4) * P + w], ACT.Exp,
                                         bias=sst[:, 1, m:m + 1], accum_out=sst[:, 3, m:m + 1])
                nc.scalar.activation(sst[:, 4, :], sst[:, 2, :], ACT.Exp).then_inc(p_exp, 1)
                evac(PROJ_VG + s, zVG[:, s, :])
                if s + 2 < NT:
                    qk_square(s + 2)
                if s + 1 < NT:
                    t1_evac(s + 1)
                for g in range(2):
                    act.wait_ge(pt_ps, s + 1)
                    if g == 0 and s >= 1:
                        act.wait_ge(pv_ps, s)
                    nc.scalar.copy(PT[:, 4 * g:4 * g + 4, :],
                                   bank[4 + g][:, :].rearrange("p (n k) -> p n k", n=4)).then_inc(pt_out, 1)
                act.wait_ge(o_ps, s + 1)
                if s >= 1:
                    act.wait_ge(o_ready, s)
                nc.scalar.activation(obuf[:, 0, :], bank[6][:, 0:256], ACT.Square).then_inc(o_sq, 1)
                nc.scalar.activation(obuf[:, 1, :], zVG[:, s, 256:512], ACT.Tanh, scale=0.5).then_inc(o_tanh, 1)
                act.wait_ge(pv_ps, s + 1)
                if s >= 1:
                    act.wait_ge(ysum_ps, s)
                nc.scalar.activation(ysq[:, :, :], bank[2][:, :].rearrange("p (n k) -> p n k", n=4),
                                     ACT.Square).then_inc(yc_sq, 1)

            for t in range(NT):
                act.wait_ge(x2_ready, 2 * t + 2)
                if t:
                    act.wait_ge(x2_ss, t)
                nc.scalar.activation(uc[:, 0, :], x2[:, t, :], ACT.Square,
                                     accum_out=ss[:, t:t + 1]).then_inc(x2_ss, 1)
                act.wait_ge(x2_rs, t + 1)
                if t >= 2:
                    act.wait_ge(xn_ps, 2 * (t - 1))
                    act.wait_ge(xn_stored[t % 2], 16 * (t // 2))
                nc.scalar.mul(xn[t % 2], x2[:, t, :], rs[:, t:t + 1]).then_inc(xn_ready, 1)
            act.wait_ge(rt_arg, 1)
            nc.scalar.activation(kT[:, 328:368], kT[:, 288:328], ACT.Exp).then_inc(rt_exp, 1)

            for b in range(2):
                act.sem_inc(y_stored[b], 16)
            with act.Fori(0, NE // 2) as i:
                for b in range(2):
                    e = 2 * i + b
                    act.wait_ge(e_gate, e + 1)
                    nc.scalar.activation(sg, bank[0][:, :], ACT.Silu).then_inc(e_sg, 1)
                    act.wait_ge(e_hps, e + 1)
                    nc.scalar.copy(hbT, bank[4][:, :].rearrange("p (k t) -> p k t", k=KF)).then_inc(e_hT, 1)
                    act.wait_ge(e_down, 2 * e + 1)
                    act.wait_ge(y_stored[b], 16 * i + 16)
                    nc.scalar.copy(yo[b][:, 0:BANK], bank[5][:, :]).then_inc(e_ya, 1)
                    act.wait_ge(e_ya, e + 1)
                    act.wait_ge(e_yb, e + 1)
                    act.dma_start(y_d[bass.ds(e * P, P), :], yo[b]).then_inc(y_stored[b], 16)
            act.wait_ge(ctrl_ready, 1)
            n_ovf = act.value_load(ctrl[0:1, 0:1], min_val=0, max_val=NOVF)
            with act.Fori(0, NOVF) as j:
                with act.If(j < n_ovf):
                    act.wait_ge(o_gu, j + 1)
                    nc.scalar.activation(sg, bank[0][:, :], ACT.Silu).then_inc(o_sg, 1)
                    act.wait_ge(o_y, j + 1)
                    act.dma_start(y_d[bass.ds((j + NE) * P, P), :], yo[1]).then_inc(o_stored, 16)
                    act.wait_ge(o_stored, 16 * j + 16)
                    act.sem_inc(turn, 1)
                act.nop()

        @block.vector
        def _(dve):
            n = [0]

            def mark(ins):
                n[0] += 1
                ins.then_inc(dv, 1)
                return n[0]

            def link(ins):
                dve.wait_ge(dv, mark(ins))

            V = nc.vector
            ang = zG[:, 0, 0:256].rearrange("p (t d) -> p t d", t=NT)
            ang_c = zG[:, 1, 0:256].rearrange("p (t d) -> p t d", t=NT)
            turn = zG[:, 0, 256:512].rearrange("p (t d) -> p t d", t=NT)
            posf = zG[:, 0, 512:512 + NT]
            invf = zG[:, 0, 544:544 + HALF]

            def hT_evac(u):
                t, h = u // 2, u % 2
                dve.wait_ge(xT_ps, u + 1)
                if u == 0:
                    dve.wait_ge(c_in, 16)
                V.tensor_tensor(hT[:, 4 * h:4 * h + 4, t * P:(t + 1) * P],
                                bank[2 + u % 4][:, :].rearrange("p (k t) -> p k t", k=4),
                                bc(g1[:, 4 * h:4 * h + 4].unsqueeze(2), [P, 4, P]), ALU.mult).then_inc(hT_ready, 1)

            for t in range(NT):
                dve.wait_ge(x_rs, t + 1)
                V.tensor_scalar(xs[:, t, :], xs[:, t, :], rs[:, t:t + 1], None, ALU.mult).then_inc(x_scaled, 1)
                if t:
                    hT_evac(2 * t - 2)
                    hT_evac(2 * t - 1)
            hT_evac(2 * NT - 2)
            hT_evac(2 * NT - 1)

            inv = 1.0 / (10000.0 ** (np.arange(0, HD, 2, dtype=np.float32) / np.float32(HD)))
            for i in range(HALF):
                last = V.memset(invf[:, i:i + 1], float(inv[i]))
            dve.wait_ge(c_late, C_LATE)
            link(last)
            link(V.tensor_copy(posf, posi[:, :]))
            for i in range(NT):
                last = V.tensor_scalar(ang[:, i, :], invf, posf[:, i:i + 1], None, ALU.mult)
            link(last)
            for dst, shift in ((ang_c, 0.25), (ang, 0.0)):
                link(V.tensor_scalar(turn, ang, 1.0 / TWO_PI, shift, ALU.mult, ALU.add))
                link(V.tensor_scalar(turn, turn, ROUND, None, ALU.add))
                link(V.tensor_scalar(turn, turn, -ROUND, None, ALU.add))
                link(V.scalar_tensor_tensor(dst, turn, -PI_A, ang, ALU.mult, ALU.add))
                link(V.scalar_tensor_tensor(dst, turn, -PI_B, dst, ALU.mult, ALU.add))
                link(V.scalar_tensor_tensor(dst, turn, -PI_C, dst, ALU.mult, ALU.add))
                if shift:
                    link(V.tensor_scalar(dst, dst, float(np.pi / 2), None, ALU.add))
                last = V.tensor_scalar(dst, dst, PI_SAFE, -PI_SAFE, ALU.min, ALU.max)
                if shift:
                    link(last)
            last.then_inc(rope_arg, 1)
            link(V.tensor_scalar(sp[:, 2, :], lam[:, :], -1.0, None, ALU.mult))
            V.tensor_tensor(sp[:, 0, :], sp[:, 2, :], lam[:, :], ALU.min).then_inc(lam_e, 1)
            link(V.tensor_scalar(glag[:, :], glag[:, :], 0.5, None, ALU.mult))
            link(V.tensor_copy(desc[:, :], desc_i[:, :]))
            link(V.tensor_scalar(jrow[:, :], desc[:, 0:NOVF], -1.0, float(NE), ALU.mult, ALU.add))
            link(V.tensor_scalar(qg[:, :], qg[:, :], HD ** -0.5, None, ALU.mult))
            dve.wait_ge(lam_e, 2)
            link(V.tensor_scalar(sp[:, 3, :], sp[:, 1, :], 2.0, None, ALU.add))
            link(V.reciprocal(sp[:, 3, :], sp[:, 3, :]))
            link(V.tensor_tensor(sp[:, 3, :], sp[:, 3, :], sp[:, 1, :], ALU.mult))
            link(V.tensor_tensor(sp[:, 4, :], sp[:, 3, :], sp[:, 3, :], ALU.mult))
            link(V.memset(sp[:, 5, :], 1.0 / 19))
            for k in range(17, 0, -2):
                link(V.tensor_tensor(sp[:, 5, :], sp[:, 5, :], sp[:, 4, :], ALU.mult))
                link(V.tensor_scalar(sp[:, 5, :], sp[:, 5, :], 1.0 / k, None, ALU.add))
            link(V.tensor_tensor(sp[:, 5, :], sp[:, 5, :], sp[:, 3, :], ALU.mult))
            link(V.tensor_scalar(sp[:, 2, :], sp[:, 2, :], 0.0, None, ALU.max))
            link(V.scalar_tensor_tensor(sp[:, 6, :], sp[:, 5, :], 2.0, sp[:, 2, :], ALU.mult, ALU.add))
            V.tensor_scalar(sp[:, 7, :], sp[:, 6, :], -8.0, None, ALU.mult).then_inc(c8_ready, 1)

            dve.wait_ge(proj_out, PROJ_G)
            for j in range(2):
                link(V.tensor_scalar(uc[:, j, :], zA[:, j, :], cw[:, 3, j:j + 1], cb[:, j:j + 1], ALU.mult, ALU.add))
                for tap in range(CONV_W - 2, -1, -1):
                    back_ = CONV_W - 1 - tap
                    last = V.scalar_tensor_tensor(uc[:, j, back_:T], zA[:, j, 0:T - back_], cw[:, tap, j:j + 1],
                                                  uc[:, j, back_:T], ALU.mult, ALU.add)
                    if tap:
                        link(last)
                last.then_inc(conv_done, 1)
            for j in range(2):
                dve.wait_ge(lru_sig, 4 * j + 4)
                V.tensor_tensor(ri[:, 2 * j + 1, :], ri[:, 2 * j + 1, :], uc[:, j, :], ALU.mult).then_inc(lru_iu, 1)
            for j in range(2):
                dve.wait_ge(lru_tanh, j + 1)
                dve.wait_ge(lru_iu, j + 1)
                link(V.tensor_scalar(uc[:, j, :], zA[:, j, :], -1.0, 1.0, ALU.mult, ALU.add))
                link(V.reciprocal(uc[:, j, :], uc[:, j, :]))
                V.scalar_tensor_tensor(zA[:, j, :], zA[:, j, :], -2.0, uc[:, j, :], ALU.mult,
                                       ALU.mult).then_inc(lru_m2, 1)
            for j in range(2):
                dve.wait_ge(lru_sqrt, j + 1)
                link(V.tensor_tensor(zA[:, j, :], zA[:, j, :], ri[:, 2 * j + 1, :], ALU.mult))
                link(V.tensor_tensor_scan(uc[:, j, :], ri[:, 2 * j, :], zA[:, j, :], 0.0, ALU.mult, ALU.add))
                dve.wait_ge(lru_gelu, j + 1)
                V.tensor_tensor(zA[:, 2 + j, :], uc[:, j, :], zA[:, 2 + j, :], ALU.mult).then_inc(lru_y, 1)

            for hf in range(2):
                dve.wait_ge(alpha_ps, hf + 1)
                c = slice(hf * BANK, (hf + 1) * BANK)
                link(V.tensor_scalar(GB[:, 0, c], bank[2 + hf][:, :], ba[:, 0:1], None, ALU.add))
            V.scalar_tensor_tensor(GB[:, 1, :], GB[:, 0, :], -1.0, GB[:, 0, :], ALU.mult, ALU.min).then_inc(gla_na, 1)

            def qk_reduce(t):
                dve.wait_ge(qk_sq, t + 1)
                V.tensor_reduce(qst[:, 0, :], sqs[:, :].rearrange("p (h d) -> p h d", d=HD), AX,
                                ALU.add).then_inc(qk_ss, 1)

            def qk_scale(t):
                z3 = zQ[:, t, :].rearrange("p (h d) -> p h d", d=HD)
                dve.wait_ge(qk_rs, t + 1)
                V.tensor_tensor(z3, z3, bc(qst[:, 1, :].unsqueeze(2), [P, NQK, HD]), ALU.mult).then_inc(qk_scaled, 1)

            def qk_rope(t):
                z4 = zQ[:, t, :].rearrange("p (h e d) -> p e h d", e=2, d=HALF)
                c_, s_ = (bc(r[:, t, :].unsqueeze(1), [P, NQK, HALF]) for r in (cos, sin))
                if t == 0:
                    dve.wait_ge(rope_ready, 1)
                dve.wait_ge(qk_gained, t + 1)
                V.tensor_tensor(rt[:, 0], z4[:, 0], s_, ALU.mult)
                a_ = mark(V.tensor_tensor(rt[:, 1], z4[:, 1], s_, ALU.mult))
                dve.wait_ge(dv, a_)
                V.tensor_tensor(z4[:, 0], z4[:, 0], c_, ALU.mult)
                link(V.tensor_tensor(z4[:, 1], z4[:, 1], c_, ALU.mult))
                V.tensor_tensor(z4[:, 0], z4[:, 0], rt[:, 1], ALU.subtract)
                V.tensor_tensor(z4[:, 1], z4[:, 1], rt[:, 0], ALU.add).then_inc(qk_ready, 1)

            qk_reduce(0)
            qk_scale(0)
            dve.wait_ge(gla_ln, 1)
            link(V.scalar_tensor_tensor(GB[:, 0, :], GB[:, 0, :], 0.0, GB[:, 1, :], ALU.min, ALU.subtract))
            for c in range(NCH):
                cc = slice(c * CHUNK, (c + 1) * CHUNK)
                last = V.tensor_tensor_scan(GB[:, 1, cc], bc(ones[:, 0:1], [P, CHUNK]), GB[:, 0, cc], 0.0,
                                            ALU.mult, ALU.add)
            link(last)
            b3, r3, e3 = (GB[:, i, :].rearrange("p (c i) -> p c i", i=CHUNK) for i in (1, 0, 2))
            link(V.tensor_tensor(r3, b3, bc(b3[:, :, CHUNK // 2 - 1:CHUNK // 2], [P, NCH, CHUNK]), ALU.subtract))
            link(V.tensor_tensor(e3, bc(b3[:, :, CHUNK - 1:CHUNK], [P, NCH, CHUNK]), b3, ALU.subtract))
            V.tensor_scalar(GB[:, 0, :], GB[:, 0, :], -GLA_CLAMP * GLA_TAU, GLA_CLAMP * GLA_TAU, ALU.max,
                            ALU.min).then_inc(gla_b, 1)
            qk_rope(0)
            qk_reduce(1)
            dve.wait_ge(lru_ps, 9)
            V.tensor_scalar(ra[:], bank[6][:, 0:NT], 1.0 / LRU_W, EPS, ALU.mult, ALU.add).then_inc(lru_sum, 1)
            for j in range(2):
                V.tensor_scalar(zA[:, 2 + j, :], zA[:, 2 + j, :], lrug[:, j:j + 1], None,
                                ALU.mult).then_inc(lru_done, 1)
            qk_scale(1)
            s_ = GLA_DK ** -0.5
            for i, (dst, src) in enumerate(((3, 0), (0, 1), (2, 1), (1, 0))):
                dve.wait_ge(gla_exp, i + 1)
                V.scalar_tensor_tensor(GB[:, dst, :], GB[:, dst, :], 1.0 if src else s_, zG[:, src, :], ALU.mult,
                                       ALU.mult).then_inc(gla_prep, 1)
            qk_rope(1)
            dve.wait_ge(gla_prep, 4)
            V.memset(St[:, 0, :], 0.0).then_inc(st_ready, 1)

            def expand_q(t):
                if t >= 1:
                    dve.wait_ge(att_ps, t)
                V.tensor_tensor(qx[:, :, :], bc(GB[:, 3, t * P:(t + 1) * P].unsqueeze(1), [P, GLA_H, P]),
                                bc(hm[:, :].unsqueeze(2), [P, GLA_H, P]), ALU.mult).then_inc(qx_ready, 1)

            def yc_mean(t):
                dve.wait_ge(ysum_ps, t + 1)
                V.tensor_scalar(rc[:, t:t + 1], bank[6][:, 256:257], 1.0 / SWA_W, EPS, ALU.mult,
                                ALU.add).then_inc(ysum_out, 1)

            def yb_evac(t):
                dve.wait_ge(yb_ps, t + 1)
                V.tensor_scalar(hT[:, 2:4, t * P:(t + 1) * P],
                                bank[7][:, 256:512].rearrange("p (n k) -> p n k", n=2), glag[:, 0:1], None,
                                ALU.mult).then_inc(yb_ready, 1)

            expand_q(0)
            for s in range(NT):
                dve.wait_ge(s_ps, s + 1)
                if s >= 1:
                    dve.wait_ge(p_ready, s)
                for g in range(2):
                    b_ = bank[4 + g][:, :].rearrange("p (n k) -> p n k", n=4)
                    if s == 0:
                        V.tensor_reduce(sst[:, 0, 4 * g:4 * g + 2], b_[:, 0:2, 0:CHUNK], AX, ALU.max)
                        last = V.tensor_reduce(sst[:, 0, 4 * g + 2:4 * g + 4], b_[:, 2:4, :], AX, ALU.max)
                    else:
                        last = V.tensor_reduce(sst[:, 0, 4 * g:4 * g + 4], b_, AX, ALU.max)
                link(last)
                m4 = sst[:, 0, :].rearrange("p (g c r) -> p g c r", g=2, c=2)
                s4 = bc(sinks[:, :].rearrange("p (g r) -> p g r", g=2).unsqueeze(2), [P, 2, 2, 2])
                link(V.tensor_tensor(m4, m4, s4, ALU.max))
                V.tensor_tensor(sst[:, 2, :].rearrange("p (g c r) -> p g c r", g=2, c=2), s4, m4, ALU.subtract)
                V.tensor_scalar(sst[:, 1, :], sst[:, 0, :], -1.0, None, ALU.mult).then_inc(s_negm, 1)
                if s == 0:
                    V.memset(Pb[:, 0:2, CHUNK:P], 0.0)
                    V.memset(Pb[:, 4:6, CHUNK:P], 0.0)
                if s >= 1:
                    yc_mean(s - 1)
                dve.wait_ge(p_exp, s + 1)
                link(V.tensor_tensor(sst[:, 4, :], sst[:, 4, :], sst[:, 3, :], ALU.add))
                link(V.reciprocal(sst[:, 4, :], sst[:, 4, :]))
                V.tensor_tensor(Pb[:, :, :], Pb[:, :, :], bc(sst[:, 4, :].unsqueeze(2), [P, 8, P]),
                                ALU.mult).then_inc(p_ready, 1)
                dve.wait_ge(att_ps, s + 1)
                if s >= 1:
                    dve.wait_ge(o_ps, s)
                V.tensor_tensor(attT[:, :, :], bank[6][:, :].rearrange("p (h t) -> p h t", h=GLA_H),
                                bc(cmask[:, :].unsqueeze(1), [P, GLA_H, P]), ALU.mult).then_inc(att_out, 1)
                if s + 2 < NT:
                    qk_reduce(s + 2)
                if s >= 1:
                    yb_evac(s - 1)
                for c in range(2):
                    k = 2 * s + c
                    dve.wait_ge(kv_ps, k + 1)
                    if s >= 1 and c == 0:
                        dve.wait_ge(o_ps, s)
                    kv = bank[7][:, 0:256] if c == 0 else bank[3][:, 256:512]
                    link(V.tensor_tensor(vkm[:, :].rearrange("p (h v) -> p h v", h=GLA_H),
                                         kv.rearrange("p (h v) -> p h v", h=GLA_H),
                                         bc(hm[:, :].unsqueeze(2), [P, GLA_H, GLA_DV]), ALU.mult))
                    dve.wait_ge(st_ready, k + 1)
                    V.scalar_tensor_tensor(St[:, (k + 1) % 4, :], St[:, k % 4, :], dec[:, k:k + 1], vkm[:, :],
                                           ALU.mult, ALU.add).then_inc(st_ready, 1)
                    dve.wait_ge(st_ready, k + 2)
                if s + 1 < NT:
                    expand_q(s + 1)
                if s + 2 < NT:
                    qk_scale(s + 2)
                dve.wait_ge(o_sq, s + 1)
                V.tensor_reduce(gst[:, 0, :], obuf[:, 0, :].rearrange("p (h v) -> p h v", h=GLA_H), AX,
                                ALU.add).then_inc(o_ss, 1)
                dve.wait_ge(o_tanh, s + 1)
                link(V.scalar_tensor_tensor(obuf[:, 1, :], obuf[:, 1, :], 1.0, zVG[:, s, 256:512], ALU.add, ALU.mult))
                dve.wait_ge(yc_sq, s + 1)
                V.tensor_tensor(hT[:, 4:8, s * P:(s + 1) * P], bank[2][:, :].rearrange("p (n k) -> p n k", n=4),
                                bc(swag[:, :].unsqueeze(2), [P, 4, P]), ALU.mult).then_inc(yc_raw, 1)
                dve.wait_ge(o_rs, s + 1)
                dve.wait_ge(o_ss, s + 1)
                o3 = obuf[:, 0, :].rearrange("p (h v) -> p h v", h=GLA_H)
                link(V.tensor_tensor(o3, bank[6][:, 0:256].rearrange("p (h v) -> p h v", h=GLA_H),
                                     bc(gst[:, 1, :].unsqueeze(2), [P, GLA_H, GLA_DV]), ALU.mult))
                V.tensor_tensor(zVG[:, s, 0:256], obuf[:, 0, :], obuf[:, 1, :], ALU.mult).then_inc(o_ready, 1)
                if s + 2 < NT:
                    qk_rope(s + 2)
            yc_mean(NT - 1)
            yb_evac(NT - 1)

            L = route[:, 0:NT * NR].rearrange("p (t r) -> p t r", r=NR)

            def h2T_evac(t):
                for h in range(2):
                    dve.wait_ge(xn_ps, 2 * t + h + 1)
                    V.tensor_tensor(h2T[t % 2][:, 4 * h:4 * h + 4, :],
                                    bank[6 + h][:, :].rearrange("p (k t) -> p k t", k=4),
                                    bc(g2[:, 4 * h:4 * h + 4].unsqueeze(2), [P, 4, P]), ALU.mult).then_inc(h2T_ready, 1)

            def logits(t):
                dve.wait_ge(lg_ps, t + 1)
                V.tensor_tensor(L[:, t, :], bank[6][:, 0:NR], rb[:, :], ALU.add).then_inc(lg_out, 1)

            dve.wait_ge(lru_rs, 1)
            for t in range(NT):
                dve.wait_ge(x_in[t], 32)
                dve.wait_ge(yc_rs, t + 1)
                for h in range(2):
                    dve.wait_ge(wo_ps, 2 * t + h + 1)
                    xc = x2[:, t, h * BANK:(h + 1) * BANK]
                    link(V.tensor_tensor(xc, xc, bank[3 * h][:, :], ALU.add))
                    link(V.scalar_tensor_tensor(xc, bank[3 * h + 1][:, :], ra[:, t:t + 1], xc, ALU.mult, ALU.add))
                    V.scalar_tensor_tensor(xc, bank[3 * h + 2][:, :], rc[:, t:t + 1], xc, ALU.mult,
                                           ALU.add).then_inc(x2_ready, 1)
                if t >= 2:
                    logits(t - 2)
                if t >= 1:
                    h2T_evac(t - 1)
            logits(NT - 2)
            h2T_evac(NT - 1)
            logits(NT - 1)

            def small(k, n_):
                return kT[:, k:k + n_]

            U = uc[:, :, :].rearrange("p a b -> p (a b)")
            arg = small(288, NT * NG + NT)
            ex = small(328, NT * NG + NT)
            arg4 = arg[:, 0:NT * NG].rearrange("p (t g) -> p t g", g=NG)
            gmax, gsum, den = small(368, NT), small(376, NT), small(384, NT)
            gt = small(392, NT * NG).rearrange("p (t g) -> p t g", g=NG)
            gfirst = small(424, NT)
            mx = [small(432 + NT * k, NT) for k in range(TOPK)]
            sel16, rk, tb = small(448, 16), small(464, 16), small(480, 16)
            nq, bl, z_ = small(496, 16), small(512, 16), small(528, 16)
            nqi = small(544, 16).bitcast(I32)
            cnt, nb, oend, tab = (small(560 + NE * k, NE) for k in range(4))
            nbi = small(688, NE).bitcast(I32)
            cover = small(0, 16)
            lm = U[:, 0:NT * NE].rearrange("p (t e) -> p t e", e=NE)
            lm4 = U[:, 0:NT * NE].rearrange("p (t g e) -> p t g e", g=NG, e=EPG)
            A = U[:, 256:768].rearrange("p (k t e) -> p k t e", k=TOPK, e=NE)
            A_n = U[:, 256:768].rearrange("p (n e) -> p n e", e=NE)
            rank = U[:, 768:1024].rearrange("p (t e) -> p t e", e=NE)
            tmp = U[:, 1024:1280].rearrange("p (t e) -> p t e", e=NE)
            tmp4 = U[:, 1024:1536].rearrange("p (k t e) -> p k t e", k=TOPK, e=NE)
            tmp_n = U[:, 1024:1536].rearrange("p (n e) -> p n e", e=NE)
            Mb = uc[:, 1, 512:640].bitcast(BF16).rearrange("p (t e) -> p t e", e=NE)
            descb = bc(desc[:, :].unsqueeze(1), [P, NT, NE])
            dg = bc(desc[:, NE - NG:NE].unsqueeze(1), [P, NT, NG])

            def per(c, w):
                return bc(c.unsqueeze(2), [P, NT, w])

            dve.wait_ge(lg_out, NT)
            link(V.tensor_reduce(gmax, L[:, :, 0:NG], AX, ALU.max))
            link(V.tensor_tensor(arg4, L[:, :, 0:NG], per(gmax, NG), ALU.subtract))
            link(V.tensor_tensor(gt, L[:, :, 0:NG], per(gmax, NG), ALU.is_equal))
            link(V.tensor_tensor(gt, gt, dg, ALU.mult))
            link(V.tensor_reduce(gfirst, gt, AX, ALU.max))
            link(V.tensor_tensor(gt, dg, per(gfirst, NG), ALU.is_equal))
            link(V.tensor_scalar(gt, gt, -1.0, BIG, ALU.add, ALU.mult))
            link(V.tensor_tensor(lm4, L[:, :, NG:NR].rearrange("p t (g e) -> p t g e", g=NG),
                                 bc(gt.unsqueeze(3), [P, NT, NG, EPG]), ALU.add))
            for k in range(TOPK):
                sel = sel16[:, k * NT:(k + 1) * NT]
                link(V.tensor_reduce(mx[k], lm, AX, ALU.max))
                if k == 1:
                    V.tensor_tensor(arg[:, NT * NG:], mx[1], mx[0], ALU.subtract).then_inc(rt_arg, 1)
                link(V.tensor_tensor(tmp, lm, per(mx[k], NE), ALU.is_equal))
                link(V.tensor_tensor(tmp, tmp, descb, ALU.mult))
                link(V.tensor_reduce(sel, tmp, AX, ALU.max))
                link(V.tensor_tensor(A[:, k], descb, per(sel, NE), ALU.is_equal))
                if k == 0:
                    link(V.scalar_tensor_tensor(lm, A[:, 0], -3.0 * BIG, lm, ALU.mult, ALU.add))
            V.tensor_tensor(Mb, A[:, 0], A[:, 1], ALU.add).then_inc(hot_ready, 1)
            dve.wait_ge(rt_exp, 1)
            link(V.tensor_reduce(gsum, ex[:, 0:NT * NG].rearrange("p (t g) -> p t g", g=NG), AX, ALU.add))
            link(V.scalar_tensor_tensor(den, ex[:, NT * NG:], 1.0, gsum, ALU.add, ALU.mult))
            link(V.reciprocal(wts[:, 0, :], den))
            link(V.tensor_tensor(wts[:, 1, :], wts[:, 0, :], ex[:, NT * NG:], ALU.mult))
            dve.wait_ge(rank_ps, 1)
            link(V.tensor_copy(rank, bank[5][:, 0:NT * NE].rearrange("p (t e) -> p t e", e=NE)))
            link(V.tensor_copy(cnt, bank[5][:, NT * NE:(NT + 1) * NE]))
            link(V.tensor_scalar(nbi, cnt, float(P - 1), None, ALU.add))
            link(V.tensor_scalar(nbi, nbi, 7, None, ALU.arith_shift_right))
            link(V.tensor_copy(nb, nbi))
            link(V.tensor_scalar(nb, nb, -1.0, 0.0, ALU.add, ALU.max))
            link(V.tensor_tensor_scan(oend, bc(ones[:, 0:1], [P, NE]), nb, 0.0, ALU.mult, ALU.add))
            link(V.scalar_tensor_tensor(tab, desc[:, :], -1.0, oend, ALU.add, ALU.add))
            link(V.tensor_tensor(tab, tab, nb, ALU.subtract))
            link(V.tensor_tensor(tmp4, A, bc(rank.unsqueeze(1), [P, TOPK, NT, NE]), ALU.mult))
            link(V.tensor_reduce(rk, tmp_n, AX, ALU.add))
            link(V.tensor_tensor(tmp_n, A_n, bc(tab.unsqueeze(1), [P, TOPK * NT, NE]), ALU.mult))
            link(V.tensor_reduce(tb, tmp_n, AX, ALU.add))
            link(V.tensor_copy(nqi, rk))
            link(V.tensor_scalar(nqi, nqi, 7, None, ALU.arith_shift_right))
            link(V.tensor_copy(nq, nqi))
            link(V.scalar_tensor_tensor(z_, nq, 1.0, tb, ALU.min, ALU.mult))
            link(V.tensor_tensor(z_, z_, nq, ALU.add))
            link(V.tensor_scalar(bl, sel16, -1.0, float(NE), ALU.mult, ALU.add))
            link(V.tensor_tensor(bl, bl, z_, ALU.add))
            link(V.scalar_tensor_tensor(rk, nq, -float(P), rk, ALU.mult, ALU.add))
            V.scalar_tensor_tensor(addr_i[:, :, :].rearrange("p k t -> p (k t)"), rk, float(NBLK), bl, ALU.mult,
                                   ALU.add).then_inc(addr_ready, 1)
            V.scalar_tensor_tensor(orow_i[:, :, :].rearrange("p k t -> p (k t)"), bl, float(P), rk, ALU.mult,
                                   ALU.add).then_inc(addr_ready, 1)
            ov = U[0:1, 1024:1024 + NOVF * NE].rearrange("p (j e) -> p j e", e=NE)
            link(V.tensor_tensor(ov, bc(oend[0:1, :].unsqueeze(1), [1, NOVF, NE]),
                                 bc(jrow[0:1, :].unsqueeze(2), [1, NOVF, NE]), ALU.is_le))
            link(V.tensor_reduce(cover[0:1, 1:NOVF + 1], ov, AX, ALU.add))
            link(V.tensor_copy(cover[0:1, 0:1], oend[0:1, NE - 1:NE]))
            V.tensor_copy(ctrl[0:1, 0:NOVF + 1], cover[0:1, 0:NOVF + 1]).then_inc(ctrl_ready, 1)

            def xT_evac(b, h, ready):
                V.tensor_tensor(xT[b][:, 4 * h:4 * h + 4, :], bank[2 + h][:, :].rearrange("p (k t) -> p k t", k=4),
                                bc(g2[:, 4 * h:4 * h + 4].unsqueeze(2), [P, 4, P]), ALU.mult).then_inc(ready, 1)

            for h in range(2):
                dve.wait_ge(e_xps, h + 1)
                xT_evac(0, h, e_xT)
            with dve.Fori(0, NE // 2) as i:
                for b in range(2):
                    e = 2 * i + b
                    dve.wait_ge(e_sg, e + 1)
                    dve.wait_ge(e_up, e + 1)
                    V.tensor_tensor(hb, sg, bank[1][:, :], ALU.mult).then_inc(e_hb, 1)
                    for h in range(2):
                        dve.wait_ge(e_xps, 2 * e + (3 + h))
                        xT_evac(1 - b, h, e_xT)
                    dve.wait_ge(e_down, 2 * e + 2)
                    dve.wait_ge(y_stored[b], 16 * i + 16)
                    V.tensor_copy(yo[b][:, BANK:], bank[6][:, :]).then_inc(e_yb, 1)
            dve.wait_ge(ctrl_ready, 1)
            dve.wait_ge(y_stored[1], 16 * (NE // 2) + 16)
            n_ovf = dve.value_load(ctrl[0:1, 0:1], min_val=0, max_val=NOVF)
            with dve.Fori(0, NOVF) as j:
                with dve.If(j < n_ovf):
                    dve.wait_ge(o_xps, j + 1)
                    for h in range(2):
                        xT_evac(1, h, o_xT)
                    dve.wait_ge(o_sg, j + 1)
                    V.tensor_tensor(hb, sg, bank[1][:, :], ALU.mult).then_inc(o_hb, 1)
                    dve.wait_ge(o_hps, j + 1)
                    V.tensor_copy(hbT, bank[4][:, :].rearrange("p (k t) -> p k t", k=KF)).then_inc(o_hT, 1)
                    dve.wait_ge(o_down, j + 1)
                    V.tensor_copy(yo[1][:, 0:BANK], bank[5][:, :])
                    V.tensor_copy(yo[1][:, BANK:], bank[6][:, :]).then_inc(o_y, 1)
                dve.nop()

            for t in range(NT):
                dve.wait_ge(back_in[t], 16 * TOPK)
                for k in range(TOPK):
                    last = V.scalar_tensor_tensor(x2[:, t, :], back[TOPK * t + k], wts[:, k, t:t + 1], x2[:, t, :],
                                                  ALU.mult, ALU.add)
                    if k == 0:
                        link(last)
                last.then_inc(out_ready, 1)

        @block.tensor
        def _(pe):
            M = nc.tensor.matmul

            pe.wait_ge(const_ready, 1)

            def x_transposes(t):
                pe.wait_ge(x_scaled, t + 1)
                for h in range(2):
                    u = 2 * t + h
                    if u >= 4:
                        pe.wait_ge(hT_ready, u - 3)
                    for k in range(4):
                        kk = 4 * h + k
                        last = nc.tensor.transpose(bank[2 + u % 4][:, k * P:(k + 1) * P],
                                                   xs[:, t, kk * P:(kk + 1) * P], ident[:, :])
                    last.then_inc(xT_ps, 1)

            def bank_free(u):
                if u >= 2:
                    pe.wait_ge(proj_out, u - 1)

            def channel_unit(u, w, m, hf):
                bank_free(u)
                for k in range(KD):
                    last = M(bank[u % 2][:, :], w[:, k, m * P:(m + 1) * P], hT[:, k, hf * BANK:(hf + 1) * BANK],
                             start=(k == 0), stop=(k == KD - 1))
                last.then_inc(proj_ps, 1)

            def token_unit(u, w, t):
                bank_free(u)
                for k in range(KD):
                    last = M(bank[u % 2][:, 0:w.shape[2]], hT[:, k, t * P:(t + 1) * P], w[:, k, :],
                             start=(k == 0), stop=(k == KD - 1))
                return last

            for t in range(4):
                x_transposes(t)
            pe.wait_ge(w_in_full[0], 16)
            pe.wait_ge(hT_ready, NT)
            for m in range(4):
                channel_unit(m, wA, m, 0)
            for t in range(4, NT):
                x_transposes(t)
            pe.wait_ge(hT_ready, 2 * NT)
            for m in range(4):
                channel_unit(4 + m, wA, m, 1)
            pe.wait_ge(w_in_full[1], 16)
            pe.wait_ge(rope_ready, 1)
            for hf in range(2):
                for m in range(2):
                    channel_unit(PROJ_G + 2 * hf + m, wQK, m, hf)
            pe.wait_ge(lam_in, 16 * 8)
            for u in range(8):
                j, g, hf = u // 4, u // 2 % 2, u % 2
                pe.wait_ge(conv_done, j + 1)
                if u >= 6:
                    pe.wait_ge(lru_sig, u - 5)
                M(bank[2 + u % 6][:, :], (wibd if g else wrbd)[:, j, :], uc[:, j, hf * BANK:(hf + 1) * BANK],
                  start=True, stop=True).then_inc(lru_ps, 1)
            pe.wait_ge(w_in_full[2], 16)
            pe.wait_ge(w_in_full[3], 16)
            for t in range(NT):
                u = PROJ_KV + t
                token_unit(u, wKV, t)
                for k in range(KD):
                    last = M(bank[u % 2][:, 256:256 + GLA_R], hT[:, k, t * P:(t + 1) * P], wa_sb[:, k, :],
                             start=(k == 0), stop=(k == KD - 1))
                last.then_inc(proj_ps, 1)
            pe.wait_ge(w_in_full[4], 16)
            for t in range(2):
                token_unit(PROJ_Q + t, wQ, t).then_inc(proj_ps, 1)
            pe.wait_ge(lru_sig, 8)
            pe.wait_ge(proj_out, PROJ_Q)
            for t in range(NT):
                last = nc.tensor.transpose(bank[4 + t // 4][0:GLA_R, (t % 4) * P:(t % 4 + 1) * P],
                                           zAV[:, t, 0:GLA_R], ident[:, :])
                if t % 4 == 3:
                    last.then_inc(aT_ps, 1)
            for t in range(2, 3):
                token_unit(PROJ_Q + t, wQ, t).then_inc(proj_ps, 1)
            for hf in range(2):
                pe.wait_ge(aT_out, hf + 1)
                M(bank[2 + hf][:, :], wa2[:, :], GB[0:GLA_R, 3, hf * BANK:(hf + 1) * BANK],
                  start=True, stop=True).then_inc(alpha_ps, 1)
            for t in range(3, 6):
                token_unit(PROJ_Q + t, wQ, t).then_inc(proj_ps, 1)
            pe.wait_ge(lru_ysq, 2)
            for t in range(NT):
                for j in range(2):
                    last = M(bank[6][:, t:t + 1], zA[:, j, t * P:(t + 1) * P], ones[:, 0:1],
                             start=(j == 0), stop=(j == 1))
            last.then_inc(lru_ps, 1)
            for t in range(6, NT):
                token_unit(PROJ_Q + t, wQ, t).then_inc(proj_ps, 1)

            def t1(t):
                pe.wait_ge(qk_ready, t + 1)
                if t == 0:
                    pe.wait_ge(gla_prep, 4)
                else:
                    pe.wait_ge(t1_out, t)
                if t >= 2:
                    pe.wait_ge(yc_raw, t - 1)
                    pe.wait_ge(st_ready, 2 * t - 1)
                for h in range(4):
                    nc.tensor.transpose(bank[2][:, h * P:(h + 1) * P], zQ[:, t, h * P:(h + 1) * P], ident[:, :])
                nc.tensor.transpose(bank[3][:, 0:P], zQ[:, t, SWA_W:QK], ident[:, :])
                nc.tensor.transpose(bank[3][:, P:2 * P], GB[:, 2, t * P:(t + 1) * P], ident[:, :]).then_inc(t1_ps, 1)

            def scores(t):
                pe.wait_ge(t1_out, t + 1)
                if t >= 1:
                    pe.wait_ge(pt_out, 2 * t)
                for c in range(2):
                    for pr in range(2):
                        for g in range(2):
                            rows_ = slice(64 * g, 64 * g + 64)
                            lhs = qT[rows_, t % 2, c, 2 * pr:2 * pr + 2, :]
                            o = (2 * c + pr) * P
                            if c:
                                last = M(bank[4 + g][:, o:o + P], lhs, kT[rows_, t * P:(t + 1) * P],
                                         start=True, stop=True)
                            else:
                                last = M(bank[4 + g][:, o:o + CHUNK], lhs, kT[rows_, t * P:t * P + CHUNK],
                                         start=True, stop=True)
                                if t:
                                    last = M(bank[4 + g][:, o + CHUNK:o + P], lhs,
                                             kT[rows_, t * P - CHUNK:t * P], start=True, stop=True)
                last.then_inc(s_ps, 1)

            def y_sum(t):
                pe.wait_ge(yc_sq, t + 1)
                pe.wait_ge(o_ready, t + 1)
                for m in range(4):
                    last = M(bank[6][:, 256:257], ysq[:, m, :], ones[:, 0:1], start=(m == 0), stop=(m == 3))
                last.then_inc(ysum_ps, 1)

            def yb_transposes(t):
                pe.wait_ge(o_ready, t + 1)
                pe.wait_ge(st_ready, 2 * t + 2)
                for m in range(2):
                    last = nc.tensor.transpose(bank[7][:, 256 + m * P:256 + (m + 1) * P],
                                               zVG[:, t, m * P:(m + 1) * P], ident[:, :])
                last.then_inc(yb_ps, 1)

            pe.wait_ge(lru_sum, 1)
            t1(0)
            pe.wait_ge(w_in_full[5], 16)
            for s in range(NT):
                scores(s)
                token_unit(PROJ_VG + s, wVG, s).then_inc(proj_ps, 1)
                if s >= 1:
                    y_sum(s - 1)
                    yb_transposes(s - 1)
                if s + 1 < NT:
                    t1(s + 1)
                pe.wait_ge(qx_ready, s + 1)
                if s >= 1:
                    pe.wait_ge(ysum_out, s)
                M(bank[6][:, :], GB[:, 0, s * P:(s + 1) * P], qx[:, :, :], start=True, stop=True).then_inc(att_ps, 1)
                pe.wait_ge(p_ready, s + 1)
                for m in range(8):
                    last = nc.tensor.transpose(bank[4 + m // 4][:, (m % 4) * P:(m % 4 + 1) * P],
                                               Pb[:, m, :], ident[:, :])
                last.then_inc(pt_ps, 1)
                pe.wait_ge(proj_out, PROJ_VG + s + 1)
                if s >= 1:
                    pe.wait_ge(yb_ready, s)
                if s + 1 < NT:
                    pe.wait_ge(t1_out, s + 2)
                for c in range(2):
                    r_ = slice(CHUNK * c, CHUNK * (c + 1))
                    kv = bank[7][:, 0:256] if c == 0 else bank[3][:, 256:512]
                    M(kv, kdt[r_, s % 2, :], zVG[r_, s, 0:256], start=True, stop=True).then_inc(kv_ps, 1)
                pe.wait_ge(att_out, s + 1)
                for c in range(2):
                    k = 2 * s + c
                    pe.wait_ge(st_ready, k + 1)
                    M(bank[6][CHUNK * c:CHUNK * (c + 1), 0:256], GB[:, 1, k * CHUNK:(k + 1) * CHUNK],
                      St[:, k % 4, :], start=True, stop=False, skip_group_check=True)
                for h in range(GLA_H):
                    last = M(bank[6][:, h * GLA_DV:(h + 1) * GLA_DV], attT[:, h, :],
                             zVG[:, s, h * GLA_DV:(h + 1) * GLA_DV], start=False, stop=(h == GLA_H - 1),
                             skip_group_check=True)
                last.then_inc(o_ps, 1)
                pe.wait_ge(vE_ready, s + 1)
                pe.wait_ge(pt_out, 2 * s + 2)
                for g in range(2):
                    for c in range(2):
                        v = (zAV[:, s, GLA_R + 64 * g:GLA_R + 64 * g + 64] if c else
                             vE[:, s % 2, 64 * g:64 * g + 64])
                        for i in range(2):
                            o_ = bank[2][64 * i:64 * i + 64, :].rearrange("p (m k) -> p m k", m=4)
                            last = M(o_[:, 2 * g:2 * g + 2, CHUNK * c:CHUNK * (c + 1)], v,
                                     PT[:, 4 * g + 2 * c:4 * g + 2 * c + 2, 64 * i:64 * i + 64],
                                     start=True, stop=True)
                last.then_inc(pv_ps, 1)
            y_sum(NT - 1)
            yb_transposes(NT - 1)

            def xn_transposes(t):
                pe.wait_ge(xn_ready, t + 1)
                if t >= 1:
                    pe.wait_ge(h2T_ready, 2 * t)
                    pe.wait_ge(lg_out, t)
                for h in range(2):
                    for k in range(4):
                        last = nc.tensor.transpose(bank[6 + h][:, k * P:(k + 1) * P],
                                                   xn[t % 2][:, (4 * h + k) * P:(4 * h + k + 1) * P], ident[:, :])
                    last.then_inc(xn_ps, 1)

            def router(t):
                pe.wait_ge(h2T_ready, 2 * t + 2)
                for k in range(KD):
                    last = M(bank[6][:, 0:NR], h2T[t % 2][:, k, :], rw[:, k, :], start=(k == 0), stop=(k == KD - 1))
                last.then_inc(lg_ps, 1)

            pe.wait_ge(lru_done, 2)
            pe.wait_ge(proj_out, PROJ_VG + NT)
            pe.wait_ge(pt_out, 2 * NT)
            pe.wait_ge(ysum_out, NT)
            pe.wait_ge(yc_raw, NT)
            pe.wait_ge(st_ready, 2 * NT + 1)
            pe.wait_ge(yb_ready, NT)
            for t in range(NT):
                for h in range(2):
                    pe.wait_ge(w_out_full[h], 16)
                    if t >= 1:
                        pe.wait_ge(x2_ready, 2 * t - 1 + h)
                    for part, ks in enumerate(((2, 3), (0, 1), (4, 5, 6, 7))):
                        for k in ks:
                            lhs = zA[:, 2 + k, t * P:(t + 1) * P] if k < 2 else hT[:, k, t * P:(t + 1) * P]
                            last = M(bank[3 * h + part][:, :], lhs, wO[h][:, k, :], start=(k == ks[0]),
                                     stop=(k == ks[-1]))
                    last.then_inc(wo_ps, 1)
                if t >= 2:
                    router(t - 2)
                if t >= 1:
                    xn_transposes(t - 1)
            router(NT - 2)
            xn_transposes(NT - 1)
            router(NT - 1)

            pe.wait_ge(hot_ready, 1)
            Mb = uc[:, 1, 512:640].bitcast(BF16).rearrange("p (t e) -> p t e", e=NE)
            for t in range(NT + 1):
                for t0 in range(min(t + 1, NT)):
                    last = M(bank[5][:, t * NE:(t + 1) * NE], (ltri if t0 == t else onesb)[:, :], Mb[:, t0, :],
                             start=(t0 == 0), stop=(t0 == min(t, NT - 1)))
            last.then_inc(rank_ps, 1)

            W = [slots[m].rearrange("p (k n) -> p k n", k=KF if m % 3 == 2 else KD) for m in range(6)]

            def rows_T(b, h):
                for k in range(4):
                    last = nc.tensor.transpose(bank[2 + h][:, k * P:(k + 1) * P],
                                               xg[b][:, (4 * h + k) * P:(4 * h + k + 1) * P], ident[:, :])
                return last

            def first_product(bk, w, b):
                for k in range(KD):
                    last = M(bank[bk][:, :], xT[b][:, k, :], w[:, k, :], start=(k == 0), stop=(k == KD - 1))
                return last

            def hidden_T():
                for k in range(KF):
                    last = nc.tensor.transpose(bank[4][:, k * P:(k + 1) * P], hb[:, k * P:(k + 1) * P], ident[:, :])
                return last

            def down_half(w, h):
                for k in range(KF):
                    last = M(bank[5 + h][:, :], hbT[:, k, :], w[:, k, h * BANK:(h + 1) * BANK], start=(k == 0),
                             stop=(k == KF - 1))
                return last

            pe.wait_ge(addr_ready, 2)
            pe.wait_ge(e_x[0], 16)
            for h in range(2):
                rows_T(0, h).then_inc(e_xps, 1)
            with pe.Fori(0, NE // 2) as i:
                for b in range(2):
                    e = 2 * i + b
                    pe.wait_ge(e_xT, 2 * e + 2)
                    pe.wait_ge(e_w[3 * b], 16 * i + 16)
                    first_product(0, W[3 * b], b).then_inc(e_gate, 1)
                    pe.wait_ge(e_w[3 * b + 1], 16 * i + 16)
                    first_product(1, W[3 * b + 1], b).then_inc(e_up, 1)
                    pe.wait_ge(e_x[1 - b], 16 * i + 16 * (b + 1))
                    rows_T(1 - b, 0).then_inc(e_xps, 1)
                    pe.wait_ge(e_hb, e + 1)
                    hidden_T().then_inc(e_hps, 1)
                    rows_T(1 - b, 1).then_inc(e_xps, 1)
                    pe.wait_ge(e_hT, e + 1)
                    pe.wait_ge(e_w[3 * b + 2], 16 * i + 16)
                    for h in range(2):
                        down_half(W[3 * b + 2], h).then_inc(e_down, 1)
            pe.wait_ge(e_xT, 2 * (NE + 1))
            pe.wait_ge(e_ya, NE)
            pe.wait_ge(e_yb, NE)
            pe.wait_ge(ctrl_ready, 1)
            n_ovf = pe.value_load(ctrl[0:1, 0:1], min_val=0, max_val=NOVF)
            with pe.Fori(0, NOVF) as j:
                with pe.If(j < n_ovf):
                    pe.wait_ge(o_x, 16 * j + 16)
                    for h in range(2):
                        last = rows_T(1, h)
                    last.then_inc(o_xps, 1)
                    pe.wait_ge(o_xT, 2 * j + 2)
                    pe.wait_ge(o_w, 48 * j + 48)
                    first_product(0, W[0], 1)
                    first_product(1, W[1], 1).then_inc(o_gu, 1)
                    pe.wait_ge(o_hb, j + 1)
                    hidden_T().then_inc(o_hps, 1)
                    pe.wait_ge(o_hT, j + 1)
                    for h in range(2):
                        last = down_half(W[2], h)
                    last.then_inc(o_down, 1)
                    pe.wait_ge(o_y, j + 1)
                    pe.sem_inc(turn, 1)
                pe.nop()


_INS = ["x", "positions", "norm1_g", "w_in", "lru_conv_w", "lru_conv_b", "lru_wr", "lru_br", "lru_wi", "lru_bi",
        "lru_lambda", "lru_out_g", "gla_wa2", "gla_ba", "gla_norm_g", "swa_q_norm_g", "swa_k_norm_g", "swa_sinks",
        "swa_out_g", "w_out", "norm2_g", "moe_wg", "moe_bg", "moe_we", "moe_be", "moe_w_gate", "moe_w_up",
        "moe_w_down"]


def kernel(**inputs):
    import numpy as _np
    import concourse.bacc as _bacc
    from concourse import mybir as _mybir
    from concourse.bass_utils import run_bass_kernel_spmd as _run

    nc = _bacc.Bacc("TRN2", target_bir_lowering=False, num_devices=1)
    arrays, args = {}, {}
    for name in _INS:
        x = _np.ascontiguousarray(inputs[name])
        arrays[f"in_{name}_dram"] = x
        args[name] = nc.dram_tensor(f"in_{name}_dram", x.shape, _mybir.dt.from_np(x.dtype), kind="ExternalInput").ap()
    out = nc.dram_tensor("out_0_dram", (1, T, D), F32, kind="ExternalOutput").ap()
    build(nc, args, out)
    r = _run(nc, [arrays], core_ids=[0])
    return r.results[0]["out_0_dram"]
```

```python
from contextlib import ExitStack

import numpy as np

import concourse.bass as bass
from concourse import mybir

ALU = mybir.AluOpType
ACT = mybir.ActivationFunctionType
AX = mybir.AxisListType.X
F32 = mybir.dt.float32
F32R = mybir.dt.float32r
BF16 = mybir.dt.bfloat16
I32 = mybir.dt.int32

P = 128
T = 1024
D = 1024
NT = T // P
KD = D // P
BANK = 512
CHUNK = 64
NCH = T // CHUNK
EPS = 1e-6

LRU_W = 256
LRU_BLK = 64
CONV_W = 4
GLA_H, GLA_DK, GLA_DV, GLA_R = 4, 32, 64, 16
SWA_H, SWA_KV, HD = 8, 2, 64
SWA_W = SWA_H * HD
HALF = HD // 2

C_A = 0
C_BQ = 2 * LRU_W
C_BV = C_BQ + 2 * GLA_H * GLA_DK
C_BA = C_BV + 2 * GLA_H * GLA_DV
C_CQ = C_BA + GLA_R
C_CK = C_CQ + SWA_W
C_CV = C_CK + SWA_KV * HD
QK = SWA_W + SWA_KV * HD
NQK = QK // HD
AV = GLA_R + SWA_KV * HD

NG, EPG, NE, TOPK = 4, 8, 32, 2
FF = 512
KF = FF // P
NR = NG + NE
NOVF = (T * TOPK - 1) // (P + 1)
NBLK = NE + NOVF
BIG = 1.0e30
GLA_CLAMP = 43.0
GLA_TAU = 16.0

TWO_PI = 2.0 * np.pi
PI_A = 6.28125
PI_B = float(np.float32(np.round((TWO_PI - PI_A) * 2.0**21) / 2.0**21))
PI_C = float(TWO_PI - PI_A - PI_B)
ROUND = 12582912.0
PI_SAFE = 3.1415925


def build(nc, a, out):
    with ExitStack() as ctx:
        def sb(name, shape, dt=F32):
            return ctx.enter_context(nc.sbuf_tensor(name, shape, dt))

        def sem(name):
            return ctx.enter_context(nc.semaphore(name))

        x_d = a["x"][0]
        w_in = a["w_in"][0]
        w_out = a["w_out"][0]
        w_gate = a["moe_w_gate"][0]
        w_up = a["moe_w_up"][0]
        w_down = a["moe_w_down"][0]
        out_d = out[0]
        xn_d = nc.dram_tensor("xn_scratch", [T, D], F32)[:, :]
        slot_d = nc.dram_tensor("slot_table", [P * NBLK, 1], I32)
        y_d = nc.dram_tensor("expert_rows", [NBLK * P, D], F32)[:, :]

        def next_place():
            return -(-nc.sbuf_base // 32) * 32

        ring_at = next_place()
        ring = sb("ring", [P, 5, KD * BANK])
        hT_at = next_place()
        hT = sb("hT", [P, KD, T])
        zA_at = next_place()
        zA = sb("zA", [P, 4, T])
        zG_at = next_place()
        zG = sb("zG", [P, 2, T])
        late = sb("late", [P, 9216])
        zAV = sb("zAV", [P, NT, AV])
        uc = sb("uc", [P, 2, T])
        kT = sb("kT", [P, T])
        wa_sb = sb("wa_sb", [P, KD, GLA_R])
        ident = sb("ident", [P, P])
        ones = sb("ones", [P, P])
        cmask = sb("cmask", [P, P])
        ltri = sb("ltri", [P, P], BF16)
        onesb = sb("onesb", [P, P], BF16)
        hm = sb("hm", [P, GLA_H])
        wrbd = sb("wrbd", [P, 2, P])
        wibd = sb("wibd", [P, 2, P])
        wa2 = sb("wa2", [GLA_R, P])
        rw = sb("rw", [P, KD, NR])
        rb = sb("rb", [P, NR])
        qg = sb("qg", [P, HD])
        kg = sb("kg", [P, HD])
        g1 = sb("g1", [P, KD])
        cw = sb("cw", [P, CONV_W, 2])
        cb = sb("cb", [P, 2])
        br = sb("br", [P, 2])
        bi = sb("bi", [P, 2])
        lam = sb("lam", [P, 2])
        lrug = sb("lrug", [P, 2])
        ba = sb("ba", [P, 1])
        glag = sb("glag", [P, 1])
        swag = sb("swag", [P, 4])
        sinks = sb("sinks", [P, 4])
        posi = sb("posi", [P, NT], I32)
        sp = sb("sp", [P, 8, 2])
        cos = sb("cos", [P, NT, HALF])
        sin = sb("sin", [P, NT, HALF])
        eps = sb("eps", [P, 1])
        half_neg = sb("half_neg", [P, NQK])
        ss = sb("ss", [P, NT])
        rs = sb("rs", [P, NT])
        dec = sb("dec", [P, NCH])
        kdt = sb("kdt", [P, 2, P])
        vE = sb("vE", [P, 2, P])
        qst = sb("qst", [P, 2, NQK])
        sst = sb("sst", [P, 6, 8])
        gst = sb("gst", [P, 2, GLA_H])
        ra = sb("ra", [P, NT])
        rc = sb("rc", [P, NT])
        desc_i = sb("desc_i", [P, NE], I32)
        desc = sb("desc", [P, NE])
        jrow = sb("jrow", [P, NOVF])
        addr_i = sb("addr_i", [P, TOPK, NT], I32)
        orow_i = sb("orow_i", [P, TOPK, NT], I32)
        wts = sb("wts", [P, TOPK, NT])
        obuf = sb("obuf", [P, 2, 256])
        idx = sb("idx", [P, NBLK], I32)
        idxc = sb("idxc", [P, 2, 1], I32)
        tokid = sb("tokid", [P, NT], I32)
        ctrl = sb("ctrl", [P, 16], I32)

        xs = late[:, 0:NT * D].rearrange("p (t d) -> p t d", t=NT)
        x2 = xs
        zVG = late[:, 0:NT * 512].rearrange("p (t c) -> p t c", t=NT)
        zQ = late[:, NT * 512:NT * 512 + NT * QK].rearrange("p (t c) -> p t c", t=NT)
        ri = late[:, 0:4 * T].rearrange("p (n t) -> p n t", n=4)
        GB = ring[:, 2, :].rearrange("p (n t) -> p n t", n=4)
        wA = ring[:, 0, :].rearrange("p (k n) -> p k n", k=KD)
        wQK = ring[:, 1, 0:KD * 256].rearrange("p (k n) -> p k n", k=KD)
        wKV = ring[:, 1, KD * 256:KD * 512].rearrange("p (k n) -> p k n", k=KD)
        wQ = ring[:, 3, :].rearrange("p (k n) -> p k n", k=KD)
        wVG = ring[:, 4, :].rearrange("p (k n) -> p k n", k=KD)
        wO = [ring[:, n, :].rearrange("p (k n) -> p k n", k=KD) for n in range(2)]
        Pb = zA[:, 0, :].rearrange("p (n k) -> p n k", n=8)
        ysq = zA[:, 1, 0:512].rearrange("p (n k) -> p n k", n=4)
        vkm = zA[:, 1, 512:768]
        PT = uc[:, 0, :].rearrange("p (n k) -> p n k", n=8)
        qT = uc[:, 1, :].rearrange("p (b c n q) -> p b c n q", b=2, c=2, n=4)
        qx = zG[:, 0, 0:512].rearrange("p (h t) -> p h t", h=GLA_H)
        attT = zG[:, 0, 512:1024].rearrange("p (h t) -> p h t", h=GLA_H)
        St = zG[:, 1, :].rearrange("p (n v) -> p n v", n=4)
        sqs = sb("sqs", [P, QK])
        rt = sqs[:, :].rearrange("p (n h d) -> p n h d", n=2, d=HALF)

        xn = [zG[:, b, :] for b in range(2)]
        h2T = [zA[:, b, :].rearrange("p (k t) -> p k t", k=KD) for b in range(2)]
        route = kT
        slots = [ring[:, 3, :], ring[:, 4, :], ring[:, 2, :]]
        xg = [hT[:, 4 + b, :] for b in range(2)]
        xT = hT[:, 7, :].rearrange("p (k t) -> p k t", k=KD)
        yo = [zA[:, b, :] for b in range(2)]
        sg = zA[:, 2, 0:FF]
        hb = zA[:, 2, FF:2 * FF]
        hbT = zA[:, 3, 0:FF].rearrange("p (k t) -> p k t", k=KF)
        HALF_W = KD * BANK // 2

        def over(name, at, n):
            return nc.alloc_sbuf_tensor_at(name, [P, n], F32R, offset=at)

        raw = [slots[j // 2][:, (j % 2) * HALF_W:(j % 2 + 1) * HALF_W] for j in range(6)]
        raw_at = [ring_at + 4 * (2 * n + h) * HALF_W for n in (3, 4, 2) for h in range(2)]
        hi_at = [hT_at + 4 * h * HALF_W for h in range(2)] + [ring_at + 4 * n * HALF_W for n in range(4)]
        w_lo = [over(f"w_lo{j}", raw_at[j], HALF_W) for j in range(6)]
        w_hi = [over(f"w_hi{j}", hi_at[j], HALF_W) for j in range(6)]
        x_hi = [over(f"x_hi{b}", hT_at + 4 * (6 + b) * T, D) for b in range(2)]
        x_lo = [over(f"x_lo{b}", zG_at + 4 * b * T, D) for b in range(2)]
        h_hi = over("h_hi", zA_at + 4 * 3 * T, FF)
        h_lo = over("h_lo", zA_at + 4 * (3 * T + FF), FF)
        g2b = zAV[:, :, :].rearrange("p t c -> p (t c)")[:, 0:D]
        back = [ring[:, n // 4, (n % 4) * D:(n % 4 + 1) * D] for n in range(16)]

        bank = [ctx.enter_context(nc.psum_tensor(f"bank{i}", [P, BANK], F32)) for i in range(8)]

        x_in = [sem(f"x_in{t}") for t in range(NT)]
        c_in = sem("c_in")
        c_late = sem("c_late")
        w_in_full = [sem(f"w_in_full{n}") for n in range(6)]
        w_out_full = [sem(f"w_out_full{n}") for n in range(2)]
        const_ready = sem("const_ready")
        wbd_zero = sem("wbd_zero")
        x_ss = sem("x_ss")
        x_rs = sem("x_rs")
        x_scaled = sem("x_scaled")
        xT_ps = sem("xT_ps")
        hT_ready = sem("hT_ready")
        proj_ps = sem("proj_ps")
        proj_out = sem("proj_out")
        dv = sem("dv")
        av = sem("av")
        pv_ = sem("pool_chain")
        conv_done = sem("conv_done")
        lru_ps = sem("lru_ps")
        lru_sig = sem("lru_sig")
        lru_iu = sem("lru_iu")
        lru_tanh = sem("lru_tanh")
        lru_m2 = sem("lru_m2")
        lru_sqrt = sem("lru_sqrt")
        lru_gelu = sem("lru_gelu")
        lru_y = sem("lru_y")
        lru_ysq = sem("lru_ysq")
        lru_sum = sem("lru_sum")
        lru_rs = sem("lru_rs")
        lru_done = sem("lru_done")
        lam_e = sem("lam_e")
        lam_in = sem("lam_in")
        c8_ready = sem("c8_ready")
        rope_arg = sem("rope_arg")
        rope_ready = sem("rope_ready")
        aT_ps = sem("aT_ps")
        aT_out = sem("aT_out")
        alpha_ps = sem("alpha_ps")
        gla_na = sem("gla_na")
        gla_ln = sem("gla_ln")
        gla_b = sem("gla_b")
        gla_exp = sem("gla_exp")
        gla_prep = sem("gla_prep")
        qk_sq = sem("qk_sq")
        qk_ss = sem("qk_ss")
        qk_rs = sem("qk_rs")
        qk_scaled = sem("qk_scaled")
        qk_gained = sem("qk_gained")
        qk_ready = sem("qk_ready")
        t1_ps = sem("t1_ps")
        t1_out = sem("t1_out")
        s_ps = sem("s_ps")
        s_negm = sem("s_negm")
        p_exp = sem("p_exp")
        p_ready = sem("p_ready")
        pt_ps = sem("pt_ps")
        pt_out = sem("pt_out")
        vE_ready = sem("vE_ready")
        pv_ps = sem("pv_ps")
        yc_sq = sem("yc_sq")
        yc_raw = sem("yc_raw")
        ysum_ps = sem("ysum_ps")
        ysum_out = sem("ysum_out")
        yc_rs = sem("yc_rs")
        qx_ready = sem("qx_ready")
        att_ps = sem("att_ps")
        att_out = sem("att_out")
        kv_ps = sem("kv_ps")
        st_ready = sem("st_ready")
        o_ps = sem("o_ps")
        o_sq = sem("o_sq")
        o_ss = sem("o_ss")
        o_rs = sem("o_rs")
        o_tanh = sem("o_tanh")
        o_ready = sem("o_ready")
        yb_ps = sem("yb_ps")
        yb_ready = sem("yb_ready")
        wo_ps = sem("wo_ps")
        x2_ready = sem("x2_ready")
        x2_ss = sem("x2_ss")
        x2_rs = sem("x2_rs")
        xn_ready = sem("xn_ready")
        xn_stored = [sem(f"xn_stored{b}") for b in range(2)]
        xn_ps = sem("xn_ps")
        h2T_ready = sem("h2T_ready")
        lg_ps = sem("lg_ps")
        lg_out = sem("lg_out")
        rt_arg = sem("rt_arg")
        rt_exp = sem("rt_exp")
        hot_ready = sem("hot_ready")
        rank_ps = sem("rank_ps")
        addr_ready = sem("addr_ready")
        ctrl_ready = sem("ctrl_ready")
        slot_zero = sem("slot_zero")
        slot_put = sem("slot_put")
        slot_back = sem("slot_back")
        fill_stored = sem("fill_stored")
        e_w = [sem(f"e_w{j}") for j in range(6)]
        e_x = [sem(f"e_x{b}") for b in range(2)]
        y_stored = [sem(f"y_stored{b}") for b in range(2)]
        (xn_scaled, e_xps, e_col, e_xh, e_xT, e_hi, e_lo, e_used, e_sg, e_hb, e_hps, e_hh, e_hT, e_y,
         turn, o_w, o_x, o_xps, o_xT, o_gu, o_hT, o_down, o_y, o_stored, out_ready,
         out_stored) = (sem(n) for n in (
             "xn_scaled", "e_xps", "e_col", "e_xh", "e_xT", "e_hi", "e_lo", "e_used", "e_sg", "e_hb",
             "e_hps", "e_hh", "e_hT", "e_y", "turn", "o_w", "o_x", "o_xps", "o_xT", "o_gu",
             "o_hT", "o_down", "o_y", "o_stored", "out_ready", "out_stored"))
        back_in = [sem(f"back_in{t}") for t in range(NT)]

        block = ctx.enter_context(nc.Block())

        C_LATE = 16 * 23
        PROJ_A, PROJ_G, PROJ_KV, PROJ_Q, PROJ_VG = 0, 8, 12, 20, 28

        def rows(w, c0, n):
            return w[:, c0:c0 + n].rearrange("(k p) n -> p k n", p=P)

        LAST = 6 * NE

        def nth(e, j):
            if isinstance(e, int):
                return j + 1 if e == 0 else min(6 * e + j - 1, 6 * NE + j - 5)
            return 6 * e + (j - 1)

        def loads(e, j):
            return e + 1 if j < 4 else e

        def bc(ap, shape):
            return ap.to_broadcast(shape)

        @block.sync
        def _(sp_):
            for t in range(NT):
                sp_.dma_start(xs[:, t, :], x_d[t * P:(t + 1) * P, :]).then_inc(x_in[t], 16)
                if t == 3:
                    sp_.dma_start(wA, rows(w_in, C_A, 512)).then_inc(w_in_full[0], 16)
            sp_.dma_start(wQK, rows(w_in, C_BQ, 256)).then_inc(w_in_full[1], 16)
            sp_.dma_start(wKV, rows(w_in, C_CK, 256)).then_inc(w_in_full[2], 16)
            sp_.dma_start(wa_sb[:, :, :], rows(w_in, C_BA, GLA_R)).then_inc(w_in_full[3], 16)
            sp_.dma_start(wQ, rows(w_in, C_CQ, 512)).then_inc(w_in_full[4], 16)
            sp_.dma_start(wVG, rows(w_in, C_BV, 512)).then_inc(w_in_full[5], 16)
            sp_.wait_ge(w_in_full[0], 16)
            fills = range(0, NOVF, 4)
            for j in fills:
                m = min(4, NOVF - j)
                sp_.dma_start(y_d[(NE + j) * P:(NE + j + m) * P, :].rearrange("(b p) d -> p b d", p=P),
                              ring[:, 0, 0:m * D].rearrange("p (b d) -> p b d", b=m)).then_inc(fill_stored, 16)
            sp_.wait_ge(fill_stored, 16 * len(fills))
            sp_.wait_ge(proj_ps, PROJ_G)
            sp_.dma_start(wO[0], rows(w_out, 0, 512)).then_inc(w_out_full[0], 16)
            sp_.wait_ge(proj_ps, PROJ_Q)
            sp_.dma_start(wO[1], rows(w_out, 512, 512)).then_inc(w_out_full[1], 16)

            def expert_rows(w, e):
                return w[e] if isinstance(e, int) else w[bass.ds(e, 1)].rearrange("o r c -> (o r) c")

            def expert_half(e, j):
                w, k = ((w_gate, 4), (w_up, 4), (w_down, 2))[j // 2]
                src = expert_rows(w, e - 1 if j >= 4 else e)
                h = j % 2
                sp_.dma_start(raw[j].rearrange("p (k n) -> p k n", k=k),
                              src[h * k * P:(h + 1) * k * P, :].rearrange("(k p) n -> p k n", p=P)
                              ).then_inc(e_w[j], 16)

            def expert_unit(m, e, s_):
                k = KF if m == 2 else KD
                sp_.dma_start(slots[m].rearrange("p (k n) -> p k n", k=k),
                              expert_rows((w_gate, w_up, w_down)[m], e).rearrange("(k p) n -> p k n", p=P)
                              ).then_inc(s_, 16)

            sp_.wait_ge(proj_ps, PROJ_VG)
            for j in range(2):
                expert_half(0, j)
            sp_.wait_ge(yb_ps, NT)
            sp_.wait_ge(qk_ready, NT)
            sp_.wait_ge(t1_ps, NT)
            sp_.wait_ge(yc_sq, NT)
            for t in range(NT):
                sp_.dma_start(x2[:, t, :], x_d[t * P:(t + 1) * P, :]).then_inc(x_in[t], 16)
            sp_.wait_ge(pv_ps, NT)
            sp_.dma_start(g2b, bc(a["norm2_g"][:, :], [P, D])).then_inc(c_in, 16)
            for j in range(2, 4):
                expert_half(0, j)
            for j in range(4, 6):
                expert_half(1, j)
            for t in range(NT):
                sp_.wait_ge(xn_ready, t + 1)
                sp_.dma_start(xn_d[t * P:(t + 1) * P, :], xn[t % 2]).then_inc(xn_stored[t % 2], 16)
            for j in range(4):
                sp_.wait_ge(e_used, nth(0, j))
                expert_half(1, j)
            with sp_.Fori(1, NE // 2) as i:
                for b in range(2):
                    for j in range(6):
                        sp_.wait_ge(e_used, 12 * i + (6 * b + j - 7))
                        expert_half(2 * i + b, j)
            for j in range(4, 6):
                sp_.wait_ge(e_used, nth(NE - 1, j))
                expert_half(NE, j)
            sp_.wait_ge(e_used, LAST)
            sp_.wait_ge(ctrl_ready, 1)
            n_ovf = sp_.value_load(ctrl[0:1, 0:1], min_val=0, max_val=NOVF)
            with sp_.Fori(0, NOVF) as j:
                with sp_.If(j < n_ovf):
                    e = sp_.value_load(ctrl[0:1, bass.ds(j + 1, 1)], min_val=0, max_val=NE - 1)
                    for m in range(3):
                        expert_unit(m, e, o_w)
                    sp_.wait_ge(o_down, j + 1)
                    sp_.sem_inc(turn, 1)
                sp_.nop()
            for t in range(NT):
                sp_.wait_ge(out_ready, t + 1)
                sp_.dma_start(out_d[t * P:(t + 1) * P, :], x2[:, t, :]).then_inc(out_stored, 16)
            sp_.wait_ge(out_stored, 16 * NT)

        @block.gpsimd
        def _(pool):
            n = [0]

            def link(ins):
                n[0] += 1
                ins.then_inc(pv_, 1)
                pool.wait_ge(pv_, n[0])

            link(nc.gpsimd.memset(ident[:], 0.0))
            link(nc.gpsimd.affine_select(out=ident[:], in_=ident[:], compare_op=ALU.not_equal, fill=1.0, base=0,
                                         pattern=[[-1, P]], channel_multiplier=1))
            link(nc.gpsimd.memset(half_neg[:], -0.5))
            link(nc.gpsimd.memset(eps[:], EPS))
            nc.gpsimd.memset(ones[:], 1.0).then_inc(const_ready, 1)
            pool.wait_ge(const_ready, 1)
            link(nc.gpsimd.memset(wrbd[:], 0.0))
            nc.gpsimd.memset(wibd[:], 0.0).then_inc(wbd_zero, 1)
            pool.wait_ge(wbd_zero, 1)
            link(nc.gpsimd.memset(onesb[:], 1.0))
            link(nc.gpsimd.memset(cmask[:], 1.0))
            link(nc.gpsimd.affine_select(out=cmask[:], in_=cmask[:], compare_op=ALU.is_ge, fill=0.0, base=0,
                                         pattern=[[1, P]], channel_multiplier=-1))
            link(nc.gpsimd.memset(cmask[0:CHUNK, CHUNK:P], 0.0))
            link(nc.gpsimd.memset(ltri[:], 1.0))
            link(nc.gpsimd.affine_select(out=ltri[:], in_=ltri[:], compare_op=ALU.is_ge, fill=0.0, base=-1,
                                         pattern=[[1, P]], channel_multiplier=-1))
            link(nc.gpsimd.memset(hm[:], 0.0))
            for h in range(GLA_H):
                link(nc.gpsimd.memset(hm[32 * h:32 * h + 32, h:h + 1], 1.0))
            link(nc.gpsimd.iota(tokid[:], [[P, NT]], base=0, channel_multiplier=1))
            link(nc.gpsimd.iota(desc_i[:], [[-1, NE]], base=NE, channel_multiplier=0))
            link(nc.gpsimd.memset(idx[:], 0))
            nc.gpsimd.memset(vE[CHUNK:P, 0, :], 0.0).then_inc(const_ready, 1)
            pool.wait_ge(const_ready, 2)

            def rstd_x(t):
                pool.wait_ge(x_ss, t + 1)
                link(nc.gpsimd.tensor_scalar(rs[:, t:t + 1], ss[:, t:t + 1], 1.0 / D, EPS, ALU.mult, ALU.add))
                nc.gpsimd.tensor_tensor(rs[:, t:t + 1], rs[:, t:t + 1], half_neg[:, 0:1], ALU.pow).then_inc(x_rs, 1)

            for t in range(NT):
                rstd_x(t)
            pool.dma_start(slot_d[:, :].rearrange("(p b) o -> p (b o)", p=P), idx[:, :]).then_inc(slot_zero, 16)

            def qk_norm(t):
                pool.wait_ge(qk_ss, t + 1)
                link(nc.gpsimd.tensor_scalar(qst[:, 1, :], qst[:, 0, :], 1.0 / HD, EPS, ALU.mult, ALU.add))
                nc.gpsimd.tensor_tensor(qst[:, 1, :], qst[:, 1, :], half_neg[:, 0:NQK], ALU.pow).then_inc(qk_rs, 1)
                pool.wait_ge(qk_scaled, t + 1)
                q3 = zQ[:, t, 0:SWA_W].rearrange("p (h d) -> p h d", d=HD)
                k3 = zQ[:, t, SWA_W:QK].rearrange("p (h d) -> p h d", d=HD)
                link(nc.gpsimd.tensor_tensor(q3, q3, bc(qg[:, :].unsqueeze(1), [P, SWA_H, HD]), ALU.mult))
                nc.gpsimd.tensor_tensor(k3, k3, bc(kg[:, :].unsqueeze(1), [P, SWA_KV, HD]),
                                        ALU.mult).then_inc(qk_gained, 1)

            pool.wait_ge(c_late, C_LATE)
            qk_norm(0)
            pool.wait_ge(qk_gained, 1)
            pool.wait_ge(lru_sum, 1)
            nc.gpsimd.tensor_tensor(ra[:], ra[:], half_neg[:, 0:NT], ALU.pow).then_inc(lru_rs, 1)
            pool.wait_ge(lru_rs, 1)
            qk_norm(1)
            pool.wait_ge(qk_gained, 2)

            def yc_rstd(t):
                pool.wait_ge(ysum_out, t + 1)
                nc.gpsimd.tensor_tensor(rc[:, t:t + 1], rc[:, t:t + 1], half_neg[:, 0:1], ALU.pow).then_inc(yc_rs, 1)
                pool.wait_ge(yc_rs, t + 1)

            for s in range(NT):
                if s >= 1:
                    if s >= 2:
                        pool.wait_ge(pv_ps, s - 1)
                    link(nc.gpsimd.tensor_copy(vE[CHUNK:P, s % 2, :], zAV[CHUNK:P, s - 1, GLA_R:AV]))
                nc.gpsimd.tensor_copy(vE[0:CHUNK, s % 2, :], zAV[0:CHUNK, s, GLA_R:AV]).then_inc(vE_ready, 1)
                pool.wait_ge(vE_ready, s + 1)
                if s >= 1:
                    yc_rstd(s - 1)
                if s + 2 < NT:
                    qk_norm(s + 2)
                pool.wait_ge(o_ss, s + 1)
                link(nc.gpsimd.tensor_scalar(gst[:, 1, :], gst[:, 0, :], 1.0 / GLA_DV, EPS, ALU.mult, ALU.add))
                nc.gpsimd.tensor_tensor(gst[:, 1, :], gst[:, 1, :], half_neg[:, 0:GLA_H],
                                        ALU.pow).then_inc(o_rs, 1)
                pool.wait_ge(o_rs, s + 1)
            yc_rstd(NT - 1)

            for t in range(NT):
                pool.wait_ge(x2_ss, t + 1)
                link(nc.gpsimd.tensor_scalar(rs[:, t:t + 1], ss[:, t:t + 1], 1.0 / D, EPS, ALU.mult, ALU.add))
                nc.gpsimd.tensor_tensor(rs[:, t:t + 1], rs[:, t:t + 1], half_neg[:, 0:1],
                                        ALU.pow).then_inc(x2_rs, 1)

                pool.wait_ge(x2_rs, t + 1)
                pool.wait_ge(xn_scaled, t + 1)
                if t == 0:
                    pool.wait_ge(c_in, 32)
                nc.gpsimd.tensor_tensor(xn[t % 2], xn[t % 2], g2b, ALU.mult).then_inc(xn_ready, 1)
                pool.wait_ge(xn_ready, t + 1)

            pool.wait_ge(slot_zero, 16)
            pool.wait_ge(addr_ready, 2)
            for k in range(TOPK):
                for t in range(NT):
                    nc.gpsimd.indirect_dma_start(
                        out=slot_d[:, :], out_offset=bass.IndirectOffsetOnAxis(ap=addr_i[:, k, t:t + 1], axis=0),
                        in_=tokid[:, t:t + 1], in_offset=None).then_inc(slot_put, 16)
            pool.wait_ge(slot_put, 16 * TOPK * NT)
            pool.dma_start(idx[:, :], slot_d[:, :].rearrange("(p b) o -> p (b o)", p=P)).then_inc(slot_back, 16)
            pool.wait_ge(slot_back, 16)
            for b in range(2):
                pool.wait_ge(xn_stored[b], 16 * NT // 2)

            def gather(col, nth, b, s_):
                nc.gpsimd.tensor_copy(idxc[:, b, :], idx[:, bass.ds(col, 1)]).then_inc(e_col, 1)
                pool.wait_ge(e_col, nth)
                pool.sem_inc(turn, 1)
                nc.gpsimd.indirect_dma_start(
                    out=xg[b], out_offset=None, in_=xn_d,
                    in_offset=bass.IndirectOffsetOnAxis(ap=idxc[:, b, :], axis=0)).then_inc(s_, 16)

            for b in range(2):
                gather(b, b + 1, b, e_x[b])
            with pool.Fori(1, NE // 2) as i:
                for b in range(2):
                    e = 2 * i + b
                    pool.wait_ge(e_xps, 2 * e - 2)
                    gather(e, e + 1, b, e_x[b])
            pool.wait_ge(e_xps, 2 * NE - 2)
            gather(NE, NE + 1, 0, e_x[0])
            pool.wait_ge(e_xps, 2 * (NE + 1))
            pool.wait_ge(ctrl_ready, 1)
            n_ovf = pool.value_load(ctrl[0:1, 0:1], min_val=0, max_val=NOVF)
            with pool.Fori(0, NOVF) as j:
                with pool.If(j < n_ovf):
                    gather(j + NE, j + (NE + 2), 1, o_x)
                    pool.wait_ge(o_stored, 16 * j + 16)
                    pool.sem_inc(turn, 1)
                pool.nop()
            pool.wait_ge(e_used, LAST)
            for b in range(2):
                pool.wait_ge(y_stored[b], 16 * (NE // 2) + 16)
            for t in range(NT):
                for k in range(TOPK):
                    nc.gpsimd.indirect_dma_start(
                        out=back[TOPK * t + k], out_offset=None, in_=y_d,
                        in_offset=bass.IndirectOffsetOnAxis(ap=orow_i[:, k, t:t + 1], axis=0)).then_inc(back_in[t], 16)


        @block.scalar
        def _(act):
            n = [0]

            def link(ins):
                n[0] += 1
                ins.then_inc(av, 1)
                act.wait_ge(av, n[0])

            def col(dst, src, k, s=c_late):
                act.dma_start(dst, src.rearrange("(k p) -> p k", p=P), allow_slow_non_contiguous=True).then_inc(s, 16)

            act.wait_ge(const_ready, 1)
            col(g1[:, :], a["norm1_g"][0], KD, c_in)
            act.dma_start(posi[:, :], a["positions"][0].rearrange("(k p) -> p k", p=P),
                          allow_slow_non_contiguous=True).then_inc(c_late, 16)
            for tap in range(CONV_W):
                col(cw[:, tap, :], a["lru_conv_w"][0, tap], 2)
            col(cb[:, :], a["lru_conv_b"][0], 2)
            col(br[:, :], a["lru_br"][0], 2)
            col(bi[:, :], a["lru_bi"][0], 2)
            col(lam[:, :], a["lru_lambda"][0], 2)
            col(lrug[:, :], a["lru_out_g"][0], 2)
            col(ba[:, :], a["gla_ba"][0], 1)
            col(swag[:, :], a["swa_out_g"][0], 4)

            for t in range(NT):
                act.wait_ge(x_in[t], 16)
                if t:
                    act.wait_ge(x_ss, t)
                nc.scalar.activation(uc[:, 0, :], xs[:, t, :], ACT.Square,
                                     accum_out=ss[:, t:t + 1]).then_inc(x_ss, 1)
            for i in range(2):
                act.dma_start(glag[64 * i:64 * i + 64, :], a["gla_norm_g"][0].rearrange("(p o) -> p o", o=1),
                              allow_slow_non_contiguous=True).then_inc(c_late, 16)
                act.dma_start(sinks[64 * i:64 * i + 64, :],
                              bc(a["swa_sinks"][:, i:SWA_H:2], [64, 4]),
                              allow_slow_non_contiguous=True).then_inc(c_late, 16)
            act.dma_start(qg[:, :], bc(a["swa_q_norm_g"][:, :], [P, HD])).then_inc(c_late, 16)
            act.dma_start(kg[:, :], bc(a["swa_k_norm_g"][:, :], [P, HD])).then_inc(c_late, 16)
            act.dma_start(rb[:, 0:NG], bc(a["moe_bg"][:, :], [P, NG])).then_inc(c_late, 16)
            act.dma_start(rb[:, NG:NR], bc(a["moe_be"][:, :], [P, NE])).then_inc(c_late, 16)
            act.dma_start(wa2[:, :], a["gla_wa2"][0]).then_inc(c_late, 16)
            act.dma_start(rw[:, :, 0:NG], rows(a["moe_wg"][0], 0, NG)).then_inc(c_late, 16)
            act.dma_start(rw[:, :, NG:NR], rows(a["moe_we"][0], 0, NE)).then_inc(c_late, 16)
            act.wait_ge(wbd_zero, 1)
            for blk in range(4):
                j, r = blk // 2, 64 * (blk % 2)
                act.dma_start(wrbd[r:r + 64, j, r:r + 64], a["lru_wr"][0, blk]).then_inc(lam_in, 16)
                act.dma_start(wibd[r:r + 64, j, r:r + 64], a["lru_wi"][0, blk]).then_inc(lam_in, 16)

            def evac(u, dst, src=None):
                act.wait_ge(proj_ps, u + 1)
                nc.scalar.copy(dst, bank[u % 2][:, :] if src is None else src).then_inc(proj_out, 1)

            def evac_q(t):
                u = PROJ_Q + t
                evac(u, zQ[:, t, 0:SWA_W].rearrange("p (h g d) -> p g h d", g=2, d=HD),
                     bank[u % 2][:, :].rearrange("p (g h d) -> p g h d", g=2, d=HD))

            def evac_kv(t):
                b = bank[(PROJ_KV + t) % 2]
                act.wait_ge(proj_ps, PROJ_KV + t + 1)
                nc.scalar.copy(zQ[:, t, SWA_W:QK], b[:, 0:128])
                nc.scalar.copy(zAV[:, t, GLA_R:AV], b[:, 128:256])
                nc.scalar.copy(zAV[:, t, 0:GLA_R], b[:, 256:256 + GLA_R]).then_inc(proj_out, 1)

            for m in range(4):
                evac(m, zA[:, m, 0:BANK])
            act.wait_ge(c_late, C_LATE)
            act.wait_ge(c_in, 16)
            act.wait_ge(rope_arg, 1)
            nc.scalar.activation(sin[:, :, :], zG[:, 0, 0:256].rearrange("p (t d) -> p t d", t=NT), ACT.Sin)
            nc.scalar.activation(cos[:, :, :], zG[:, 1, 0:256].rearrange("p (t d) -> p t d", t=NT),
                                 ACT.Sin).then_inc(rope_ready, 1)
            act.wait_ge(lam_e, 1)
            nc.scalar.activation(sp[:, 1, :], sp[:, 0, :], ACT.Exp).then_inc(lam_e, 1)
            for m in range(4):
                evac(4 + m, zA[:, m, BANK:T])
            for hf in range(2):
                for m in range(2):
                    evac(PROJ_G + 2 * hf + m, zG[:, m, hf * BANK:(hf + 1) * BANK])
            for u in range(8):
                j, g, hf = u // 4, u // 2 % 2, u % 2
                act.wait_ge(lru_ps, u + 1)
                nc.scalar.activation(ri[:, 2 * j + g, hf * BANK:(hf + 1) * BANK], bank[2 + u % 6][:, :], ACT.Sigmoid,
                                     bias=(bi if g else br)[:, j:j + 1]).then_inc(lru_sig, 1)
            act.wait_ge(c8_ready, 1)
            act.wait_ge(lru_sig, 8)
            for j in range(2):
                act.wait_ge(conv_done, j + 1)
                link(nc.scalar.activation(zA[:, j, :], ri[:, 2 * j, :], ACT.Tanh, scale=sp[:, 7, j:j + 1]))
                nc.scalar.activation(ri[:, 2 * j, :], ri[:, 2 * j, :], ACT.Exp,
                                     scale=sp[:, 7, j:j + 1]).then_inc(lru_tanh, 1)
            for t in range(2):
                evac_kv(t)
            for j in range(2):
                nc.scalar.activation(zA[:, 2 + j, :], zA[:, 2 + j, :], ACT.Gelu_apprx_tanh).then_inc(lru_gelu, 1)
            for t in range(2, 4):
                evac_kv(t)
            for j in range(2):
                act.wait_ge(lru_m2, j + 1)
                nc.scalar.activation(zA[:, j, :], zA[:, j, :], ACT.Sqrt).then_inc(lru_sqrt, 1)
            for t in range(4, NT):
                evac_kv(t)
            for hf in range(2):
                act.wait_ge(aT_ps, hf + 1)
                nc.scalar.copy(GB[0:GLA_R, 3, hf * BANK:(hf + 1) * BANK],
                               bank[4 + hf][0:GLA_R, :]).then_inc(aT_out, 1)
            for t in range(2):
                evac_q(t)

            def qk_square(t):
                if t >= 1:
                    act.wait_ge(qk_ready, t)
                nc.scalar.activation(sqs[:, :], zQ[:, t, :], ACT.Square).then_inc(qk_sq, 1)

            act.wait_ge(proj_out, PROJ_Q + 1)
            qk_square(0)
            for j in range(2):
                act.wait_ge(lru_y, j + 1)
                nc.scalar.activation(zA[:, j, :], zA[:, 2 + j, :], ACT.Square).then_inc(lru_ysq, 1)
            for t in range(2, 4):
                evac_q(t)
            act.wait_ge(gla_na, 1)
            link(nc.scalar.activation(GB[:, 1, :], GB[:, 1, :], ACT.Exp))
            nc.scalar.activation(GB[:, 1, :], GB[:, 1, :], ACT.Ln, bias=1.0).then_inc(gla_ln, 1)
            qk_square(1)
            for t in range(4, 6):
                evac_q(t)
            act.wait_ge(gla_b, 1)
            b3 = GB[:, 1, :].rearrange("p (c i) -> p c i", i=CHUNK)
            nc.scalar.activation(GB[:, 3, :], GB[:, 0, :], ACT.Exp, scale=1.0 / GLA_TAU).then_inc(gla_exp, 1)
            act.wait_ge(gla_exp, 1)
            nc.scalar.activation(GB[:, 0, :], GB[:, 0, :], ACT.Exp, scale=-1.0 / GLA_TAU).then_inc(gla_exp, 1)
            nc.scalar.activation(GB[:, 2, :], GB[:, 2, :], ACT.Exp, scale=1.0 / GLA_TAU).then_inc(gla_exp, 1)
            link(nc.scalar.activation(dec[:, :].unsqueeze(2), b3[:, :, CHUNK - 1:CHUNK], ACT.Exp,
                                      scale=1.0 / GLA_TAU))
            nc.scalar.activation(GB[:, 1, :], GB[:, 1, :], ACT.Exp, scale=1.0 / GLA_TAU).then_inc(gla_exp, 1)
            for t in range(6, NT):
                evac_q(t)

            def t1_evac(t):
                act.wait_ge(t1_ps, t + 1)
                if t >= 2:
                    act.wait_ge(s_ps, t - 1)
                    act.wait_ge(kv_ps, 2 * t - 2)
                nc.scalar.copy(qT[:, t % 2].rearrange("p c n q -> p n c q"),
                               bank[2][:, :].rearrange("p (n c q) -> p n c q", n=4, c=2))
                nc.scalar.copy(kT[:, t * P:(t + 1) * P], bank[3][:, 0:P])
                nc.scalar.copy(kdt[:, t % 2, :], bank[3][:, P:2 * P]).then_inc(t1_out, 1)

            t1_evac(0)
            for s in range(NT):
                act.wait_ge(s_negm, s + 1)
                if s >= 1:
                    act.wait_ge(pt_ps, s)
                for m in range(8):
                    g, c, pr = m // 4, m // 2 % 2, m % 2
                    w = CHUNK if s == 0 and c == 0 else P
                    nc.scalar.activation(Pb[:, m, 0:w],
                                         bank[4 + g][:, (m % 4) * P:(m % 4) * P + w], ACT.Exp,
                                         bias=sst[:, 1, m:m + 1], accum_out=sst[:, 3, m:m + 1])
                nc.scalar.activation(sst[:, 4, :], sst[:, 2, :], ACT.Exp).then_inc(p_exp, 1)
                evac(PROJ_VG + s, zVG[:, s, :])
                if s + 2 < NT:
                    qk_square(s + 2)
                if s + 1 < NT:
                    t1_evac(s + 1)
                for g in range(2):
                    act.wait_ge(pt_ps, s + 1)
                    if g == 0 and s >= 1:
                        act.wait_ge(pv_ps, s)
                    nc.scalar.copy(PT[:, 4 * g:4 * g + 4, :],
                                   bank[4 + g][:, :].rearrange("p (n k) -> p n k", n=4)).then_inc(pt_out, 1)
                act.wait_ge(o_ps, s + 1)
                if s >= 1:
                    act.wait_ge(o_ready, s)
                nc.scalar.activation(obuf[:, 0, :], bank[6][:, 0:256], ACT.Square).then_inc(o_sq, 1)
                nc.scalar.activation(obuf[:, 1, :], zVG[:, s, 256:512], ACT.Tanh, scale=0.5).then_inc(o_tanh, 1)
                act.wait_ge(pv_ps, s + 1)
                if s >= 1:
                    act.wait_ge(ysum_ps, s)
                nc.scalar.activation(ysq[:, :, :], bank[2][:, :].rearrange("p (n k) -> p n k", n=4),
                                     ACT.Square).then_inc(yc_sq, 1)

            for t in range(NT):
                act.wait_ge(x2_ready, 2 * t + 2)
                if t:
                    act.wait_ge(x2_ss, t)
                nc.scalar.activation(uc[:, 0, :], x2[:, t, :], ACT.Square,
                                     accum_out=ss[:, t:t + 1]).then_inc(x2_ss, 1)
                act.wait_ge(x2_rs, t + 1)
                if t >= 2:
                    act.wait_ge(xn_ps, 2 * (t - 1))
                    act.wait_ge(xn_stored[t % 2], 16 * (t // 2))
                nc.scalar.mul(xn[t % 2], x2[:, t, :], rs[:, t:t + 1]).then_inc(xn_scaled, 1)

            def hi(e, j):
                act.wait_ge(e_w[j], 16 * loads(e, j))
                nc.scalar.copy(w_hi[j][:, :], raw[j]).then_inc(e_hi, 1)

            def x_hi_evac(e, b):
                for h in range(2):
                    act.wait_ge(e_xps, 2 * e + (h + 1))
                    nc.scalar.copy(x_hi[b][:, h * BANK:(h + 1) * BANK], bank[2 + h][:, :]).then_inc(e_xh, 1)

            def silu(e):
                act.wait_ge(e_used, nth(e, 1))
                if not (isinstance(e, int) and e == 0):
                    act.wait_ge(e_hb, e)
                nc.scalar.activation(sg, bank[0][:, :], ACT.Silu).then_inc(e_sg, 1)

            def hidden_hi(e):
                act.wait_ge(e_hps, e)
                nc.scalar.copy(h_hi[:, :], bank[4][:, :]).then_inc(e_hh, 1)

            def rows_out(e, b, down, stored):
                act.wait_ge(e_used, down)
                act.wait_ge(y_stored[b], stored)
                nc.scalar.copy(yo[b][:, 0:BANK], bank[5][:, :])
                nc.scalar.copy(yo[b][:, BANK:], bank[6][:, :]).then_inc(e_y, 1)
                act.wait_ge(e_y, e - 1)
                act.dma_start(y_d[bass.ds((e - 2) * P, P), :], yo[b]).then_inc(y_stored[b], 16)

            act.wait_ge(wo_ps, 2 * NT)
            for j in range(2):
                hi(0, j)
            act.wait_ge(rt_arg, 1)
            nc.scalar.activation(kT[:, 328:368], kT[:, 288:328], ACT.Exp).then_inc(rt_exp, 1)
            for j in range(2, 4):
                hi(0, j)
            for b in range(2):
                act.sem_inc(y_stored[b], 16)
            x_hi_evac(0, 0)
            silu(0)
            x_hi_evac(1, 1)
            for j in range(6):
                hi(1, j)
                if j == 3:
                    hidden_hi(1)
                if j == 4:
                    silu(1)
            x_hi_evac(2, 0)
            with act.Fori(1, NE // 2) as i:
                for b in range(2):
                    e = 2 * i + b
                    hi(e, 0)
                    hi(e, 1)
                    hi(e, 2)
                    rows_out(e, b, 12 * i + (6 * b - 2), 16 * i)
                    hi(e, 3)
                    hidden_hi(e)
                    hi(e, 4)
                    silu(e)
                    hi(e, 5)
                    x_hi_evac(e + 1, 1 - b)
            hi(NE, 4)
            hi(NE, 5)
            rows_out(NE, 0, nth(NE - 1, 5), 8 * NE)
            hidden_hi(NE)
            rows_out(NE + 1, 1, LAST, 8 * NE)
            act.wait_ge(ctrl_ready, 1)
            n_ovf = act.value_load(ctrl[0:1, 0:1], min_val=0, max_val=NOVF)
            with act.Fori(0, NOVF) as j:
                with act.If(j < n_ovf):
                    act.wait_ge(o_gu, j + 1)
                    nc.scalar.activation(sg, bank[0][:, :], ACT.Silu).then_inc(e_sg, 1)
                    act.wait_ge(o_y, j + 1)
                    act.dma_start(y_d[bass.ds((j + NE) * P, P), :], yo[1]).then_inc(o_stored, 16)
                    act.wait_ge(o_stored, 16 * j + 16)
                    act.sem_inc(turn, 1)
                act.nop()

        @block.vector
        def _(dve):
            n = [0]

            def mark(ins):
                n[0] += 1
                ins.then_inc(dv, 1)
                return n[0]

            def link(ins):
                dve.wait_ge(dv, mark(ins))

            V = nc.vector
            ang = zG[:, 0, 0:256].rearrange("p (t d) -> p t d", t=NT)
            ang_c = zG[:, 1, 0:256].rearrange("p (t d) -> p t d", t=NT)
            turn = zG[:, 0, 256:512].rearrange("p (t d) -> p t d", t=NT)
            posf = zG[:, 0, 512:512 + NT]
            invf = zG[:, 0, 544:544 + HALF]

            def hT_evac(u):
                t, h = u // 2, u % 2
                dve.wait_ge(xT_ps, u + 1)
                if u == 0:
                    dve.wait_ge(c_in, 16)
                V.tensor_tensor(hT[:, 4 * h:4 * h + 4, t * P:(t + 1) * P],
                                bank[2 + u % 4][:, :].rearrange("p (k t) -> p k t", k=4),
                                bc(g1[:, 4 * h:4 * h + 4].unsqueeze(2), [P, 4, P]), ALU.mult).then_inc(hT_ready, 1)

            for t in range(NT):
                dve.wait_ge(x_rs, t + 1)
                V.tensor_scalar(xs[:, t, :], xs[:, t, :], rs[:, t:t + 1], None, ALU.mult).then_inc(x_scaled, 1)
                if t:
                    hT_evac(2 * t - 2)
                    hT_evac(2 * t - 1)
            hT_evac(2 * NT - 2)
            hT_evac(2 * NT - 1)

            inv = 1.0 / (10000.0 ** (np.arange(0, HD, 2, dtype=np.float32) / np.float32(HD)))
            for i in range(HALF):
                last = V.memset(invf[:, i:i + 1], float(inv[i]))
            dve.wait_ge(c_late, C_LATE)
            link(last)
            link(V.tensor_copy(posf, posi[:, :]))
            for i in range(NT):
                last = V.tensor_scalar(ang[:, i, :], invf, posf[:, i:i + 1], None, ALU.mult)
            link(last)
            for dst, shift in ((ang_c, 0.25), (ang, 0.0)):
                link(V.tensor_scalar(turn, ang, 1.0 / TWO_PI, shift, ALU.mult, ALU.add))
                link(V.tensor_scalar(turn, turn, ROUND, None, ALU.add))
                link(V.tensor_scalar(turn, turn, -ROUND, None, ALU.add))
                link(V.scalar_tensor_tensor(dst, turn, -PI_A, ang, ALU.mult, ALU.add))
                link(V.scalar_tensor_tensor(dst, turn, -PI_B, dst, ALU.mult, ALU.add))
                link(V.scalar_tensor_tensor(dst, turn, -PI_C, dst, ALU.mult, ALU.add))
                if shift:
                    link(V.tensor_scalar(dst, dst, float(np.pi / 2), None, ALU.add))
                last = V.tensor_scalar(dst, dst, PI_SAFE, -PI_SAFE, ALU.min, ALU.max)
                if shift:
                    link(last)
            last.then_inc(rope_arg, 1)
            link(V.tensor_scalar(sp[:, 2, :], lam[:, :], -1.0, None, ALU.mult))
            V.tensor_tensor(sp[:, 0, :], sp[:, 2, :], lam[:, :], ALU.min).then_inc(lam_e, 1)
            link(V.tensor_scalar(glag[:, :], glag[:, :], 0.5, None, ALU.mult))
            link(V.tensor_copy(desc[:, :], desc_i[:, :]))
            link(V.tensor_scalar(jrow[:, :], desc[:, 0:NOVF], -1.0, float(NE), ALU.mult, ALU.add))
            link(V.tensor_scalar(qg[:, :], qg[:, :], HD ** -0.5, None, ALU.mult))
            dve.wait_ge(lam_e, 2)
            link(V.tensor_scalar(sp[:, 3, :], sp[:, 1, :], 2.0, None, ALU.add))
            link(V.reciprocal(sp[:, 3, :], sp[:, 3, :]))
            link(V.tensor_tensor(sp[:, 3, :], sp[:, 3, :], sp[:, 1, :], ALU.mult))
            link(V.tensor_tensor(sp[:, 4, :], sp[:, 3, :], sp[:, 3, :], ALU.mult))
            link(V.memset(sp[:, 5, :], 1.0 / 19))
            for k in range(17, 0, -2):
                link(V.tensor_tensor(sp[:, 5, :], sp[:, 5, :], sp[:, 4, :], ALU.mult))
                link(V.tensor_scalar(sp[:, 5, :], sp[:, 5, :], 1.0 / k, None, ALU.add))
            link(V.tensor_tensor(sp[:, 5, :], sp[:, 5, :], sp[:, 3, :], ALU.mult))
            link(V.tensor_scalar(sp[:, 2, :], sp[:, 2, :], 0.0, None, ALU.max))
            link(V.scalar_tensor_tensor(sp[:, 6, :], sp[:, 5, :], 2.0, sp[:, 2, :], ALU.mult, ALU.add))
            V.tensor_scalar(sp[:, 7, :], sp[:, 6, :], -8.0, None, ALU.mult).then_inc(c8_ready, 1)

            dve.wait_ge(proj_out, PROJ_G)
            for j in range(2):
                link(V.tensor_scalar(uc[:, j, :], zA[:, j, :], cw[:, 3, j:j + 1], cb[:, j:j + 1], ALU.mult, ALU.add))
                for tap in range(CONV_W - 2, -1, -1):
                    back_ = CONV_W - 1 - tap
                    last = V.scalar_tensor_tensor(uc[:, j, back_:T], zA[:, j, 0:T - back_], cw[:, tap, j:j + 1],
                                                  uc[:, j, back_:T], ALU.mult, ALU.add)
                    if tap:
                        link(last)
                last.then_inc(conv_done, 1)
            for j in range(2):
                dve.wait_ge(lru_sig, 4 * j + 4)
                V.tensor_tensor(ri[:, 2 * j + 1, :], ri[:, 2 * j + 1, :], uc[:, j, :], ALU.mult).then_inc(lru_iu, 1)
            for j in range(2):
                dve.wait_ge(lru_tanh, j + 1)
                dve.wait_ge(lru_iu, j + 1)
                link(V.tensor_scalar(uc[:, j, :], zA[:, j, :], -1.0, 1.0, ALU.mult, ALU.add))
                link(V.reciprocal(uc[:, j, :], uc[:, j, :]))
                V.scalar_tensor_tensor(zA[:, j, :], zA[:, j, :], -2.0, uc[:, j, :], ALU.mult,
                                       ALU.mult).then_inc(lru_m2, 1)
            for j in range(2):
                dve.wait_ge(lru_sqrt, j + 1)
                link(V.tensor_tensor(zA[:, j, :], zA[:, j, :], ri[:, 2 * j + 1, :], ALU.mult))
                link(V.tensor_tensor_scan(uc[:, j, :], ri[:, 2 * j, :], zA[:, j, :], 0.0, ALU.mult, ALU.add))
                dve.wait_ge(lru_gelu, j + 1)
                V.tensor_tensor(zA[:, 2 + j, :], uc[:, j, :], zA[:, 2 + j, :], ALU.mult).then_inc(lru_y, 1)

            for hf in range(2):
                dve.wait_ge(alpha_ps, hf + 1)
                c = slice(hf * BANK, (hf + 1) * BANK)
                link(V.tensor_scalar(GB[:, 0, c], bank[2 + hf][:, :], ba[:, 0:1], None, ALU.add))
            V.scalar_tensor_tensor(GB[:, 1, :], GB[:, 0, :], -1.0, GB[:, 0, :], ALU.mult, ALU.min).then_inc(gla_na, 1)

            def qk_reduce(t):
                dve.wait_ge(qk_sq, t + 1)
                V.tensor_reduce(qst[:, 0, :], sqs[:, :].rearrange("p (h d) -> p h d", d=HD), AX,
                                ALU.add).then_inc(qk_ss, 1)

            def qk_scale(t):
                z3 = zQ[:, t, :].rearrange("p (h d) -> p h d", d=HD)
                dve.wait_ge(qk_rs, t + 1)
                V.tensor_tensor(z3, z3, bc(qst[:, 1, :].unsqueeze(2), [P, NQK, HD]), ALU.mult).then_inc(qk_scaled, 1)

            def qk_rope(t):
                z4 = zQ[:, t, :].rearrange("p (h e d) -> p e h d", e=2, d=HALF)
                c_, s_ = (bc(r[:, t, :].unsqueeze(1), [P, NQK, HALF]) for r in (cos, sin))
                if t == 0:
                    dve.wait_ge(rope_ready, 1)
                dve.wait_ge(qk_gained, t + 1)
                V.tensor_tensor(rt[:, 0], z4[:, 0], s_, ALU.mult)
                a_ = mark(V.tensor_tensor(rt[:, 1], z4[:, 1], s_, ALU.mult))
                dve.wait_ge(dv, a_)
                V.tensor_tensor(z4[:, 0], z4[:, 0], c_, ALU.mult)
                link(V.tensor_tensor(z4[:, 1], z4[:, 1], c_, ALU.mult))
                V.tensor_tensor(z4[:, 0], z4[:, 0], rt[:, 1], ALU.subtract)
                V.tensor_tensor(z4[:, 1], z4[:, 1], rt[:, 0], ALU.add).then_inc(qk_ready, 1)

            qk_reduce(0)
            qk_scale(0)
            dve.wait_ge(gla_ln, 1)
            link(V.scalar_tensor_tensor(GB[:, 0, :], GB[:, 0, :], 0.0, GB[:, 1, :], ALU.min, ALU.subtract))
            for c in range(NCH):
                cc = slice(c * CHUNK, (c + 1) * CHUNK)
                last = V.tensor_tensor_scan(GB[:, 1, cc], bc(ones[:, 0:1], [P, CHUNK]), GB[:, 0, cc], 0.0,
                                            ALU.mult, ALU.add)
            link(last)
            b3, r3, e3 = (GB[:, i, :].rearrange("p (c i) -> p c i", i=CHUNK) for i in (1, 0, 2))
            link(V.tensor_tensor(r3, b3, bc(b3[:, :, CHUNK // 2 - 1:CHUNK // 2], [P, NCH, CHUNK]), ALU.subtract))
            link(V.tensor_tensor(e3, bc(b3[:, :, CHUNK - 1:CHUNK], [P, NCH, CHUNK]), b3, ALU.subtract))
            V.tensor_scalar(GB[:, 0, :], GB[:, 0, :], -GLA_CLAMP * GLA_TAU, GLA_CLAMP * GLA_TAU, ALU.max,
                            ALU.min).then_inc(gla_b, 1)
            qk_rope(0)
            qk_reduce(1)
            dve.wait_ge(lru_ps, 9)
            V.tensor_scalar(ra[:], bank[6][:, 0:NT], 1.0 / LRU_W, EPS, ALU.mult, ALU.add).then_inc(lru_sum, 1)
            for j in range(2):
                V.tensor_scalar(zA[:, 2 + j, :], zA[:, 2 + j, :], lrug[:, j:j + 1], None,
                                ALU.mult).then_inc(lru_done, 1)
            qk_scale(1)
            s_ = GLA_DK ** -0.5
            for i, (dst, src) in enumerate(((3, 0), (0, 1), (2, 1), (1, 0))):
                dve.wait_ge(gla_exp, i + 1)
                V.scalar_tensor_tensor(GB[:, dst, :], GB[:, dst, :], 1.0 if src else s_, zG[:, src, :], ALU.mult,
                                       ALU.mult).then_inc(gla_prep, 1)
            qk_rope(1)
            dve.wait_ge(gla_prep, 4)
            V.memset(St[:, 0, :], 0.0).then_inc(st_ready, 1)

            def expand_q(t):
                if t >= 1:
                    dve.wait_ge(att_ps, t)
                V.tensor_tensor(qx[:, :, :], bc(GB[:, 3, t * P:(t + 1) * P].unsqueeze(1), [P, GLA_H, P]),
                                bc(hm[:, :].unsqueeze(2), [P, GLA_H, P]), ALU.mult).then_inc(qx_ready, 1)

            def yc_mean(t):
                dve.wait_ge(ysum_ps, t + 1)
                V.tensor_scalar(rc[:, t:t + 1], bank[6][:, 256:257], 1.0 / SWA_W, EPS, ALU.mult,
                                ALU.add).then_inc(ysum_out, 1)

            def yb_evac(t):
                dve.wait_ge(yb_ps, t + 1)
                V.tensor_scalar(hT[:, 2:4, t * P:(t + 1) * P],
                                bank[7][:, 256:512].rearrange("p (n k) -> p n k", n=2), glag[:, 0:1], None,
                                ALU.mult).then_inc(yb_ready, 1)

            expand_q(0)
            for s in range(NT):
                dve.wait_ge(s_ps, s + 1)
                if s >= 1:
                    dve.wait_ge(p_ready, s)
                for g in range(2):
                    b_ = bank[4 + g][:, :].rearrange("p (n k) -> p n k", n=4)
                    if s == 0:
                        V.tensor_reduce(sst[:, 0, 4 * g:4 * g + 2], b_[:, 0:2, 0:CHUNK], AX, ALU.max)
                        last = V.tensor_reduce(sst[:, 0, 4 * g + 2:4 * g + 4], b_[:, 2:4, :], AX, ALU.max)
                    else:
                        last = V.tensor_reduce(sst[:, 0, 4 * g:4 * g + 4], b_, AX, ALU.max)
                link(last)
                m4 = sst[:, 0, :].rearrange("p (g c r) -> p g c r", g=2, c=2)
                s4 = bc(sinks[:, :].rearrange("p (g r) -> p g r", g=2).unsqueeze(2), [P, 2, 2, 2])
                link(V.tensor_tensor(m4, m4, s4, ALU.max))
                V.tensor_tensor(sst[:, 2, :].rearrange("p (g c r) -> p g c r", g=2, c=2), s4, m4, ALU.subtract)
                V.tensor_scalar(sst[:, 1, :], sst[:, 0, :], -1.0, None, ALU.mult).then_inc(s_negm, 1)
                if s == 0:
                    V.memset(Pb[:, 0:2, CHUNK:P], 0.0)
                    V.memset(Pb[:, 4:6, CHUNK:P], 0.0)
                if s >= 1:
                    yc_mean(s - 1)
                dve.wait_ge(p_exp, s + 1)
                link(V.tensor_tensor(sst[:, 4, :], sst[:, 4, :], sst[:, 3, :], ALU.add))
                link(V.reciprocal(sst[:, 4, :], sst[:, 4, :]))
                V.tensor_tensor(Pb[:, :, :], Pb[:, :, :], bc(sst[:, 4, :].unsqueeze(2), [P, 8, P]),
                                ALU.mult).then_inc(p_ready, 1)
                dve.wait_ge(att_ps, s + 1)
                if s >= 1:
                    dve.wait_ge(o_ps, s)
                V.tensor_tensor(attT[:, :, :], bank[6][:, :].rearrange("p (h t) -> p h t", h=GLA_H),
                                bc(cmask[:, :].unsqueeze(1), [P, GLA_H, P]), ALU.mult).then_inc(att_out, 1)
                if s + 2 < NT:
                    qk_reduce(s + 2)
                if s >= 1:
                    yb_evac(s - 1)
                for c in range(2):
                    k = 2 * s + c
                    dve.wait_ge(kv_ps, k + 1)
                    if s >= 1 and c == 0:
                        dve.wait_ge(o_ps, s)
                    kv = bank[7][:, 0:256] if c == 0 else bank[3][:, 256:512]
                    link(V.tensor_tensor(vkm[:, :].rearrange("p (h v) -> p h v", h=GLA_H),
                                         kv.rearrange("p (h v) -> p h v", h=GLA_H),
                                         bc(hm[:, :].unsqueeze(2), [P, GLA_H, GLA_DV]), ALU.mult))
                    dve.wait_ge(st_ready, k + 1)
                    V.scalar_tensor_tensor(St[:, (k + 1) % 4, :], St[:, k % 4, :], dec[:, k:k + 1], vkm[:, :],
                                           ALU.mult, ALU.add).then_inc(st_ready, 1)
                    dve.wait_ge(st_ready, k + 2)
                if s + 1 < NT:
                    expand_q(s + 1)
                if s + 2 < NT:
                    qk_scale(s + 2)
                dve.wait_ge(o_sq, s + 1)
                V.tensor_reduce(gst[:, 0, :], obuf[:, 0, :].rearrange("p (h v) -> p h v", h=GLA_H), AX,
                                ALU.add).then_inc(o_ss, 1)
                dve.wait_ge(o_tanh, s + 1)
                link(V.scalar_tensor_tensor(obuf[:, 1, :], obuf[:, 1, :], 1.0, zVG[:, s, 256:512], ALU.add, ALU.mult))
                dve.wait_ge(yc_sq, s + 1)
                V.tensor_tensor(hT[:, 4:8, s * P:(s + 1) * P], bank[2][:, :].rearrange("p (n k) -> p n k", n=4),
                                bc(swag[:, :].unsqueeze(2), [P, 4, P]), ALU.mult).then_inc(yc_raw, 1)
                dve.wait_ge(o_rs, s + 1)
                dve.wait_ge(o_ss, s + 1)
                o3 = obuf[:, 0, :].rearrange("p (h v) -> p h v", h=GLA_H)
                link(V.tensor_tensor(o3, bank[6][:, 0:256].rearrange("p (h v) -> p h v", h=GLA_H),
                                     bc(gst[:, 1, :].unsqueeze(2), [P, GLA_H, GLA_DV]), ALU.mult))
                V.tensor_tensor(zVG[:, s, 0:256], obuf[:, 0, :], obuf[:, 1, :], ALU.mult).then_inc(o_ready, 1)
                if s + 2 < NT:
                    qk_rope(s + 2)
            yc_mean(NT - 1)
            yb_evac(NT - 1)

            L = route[:, 0:NT * NR].rearrange("p (t r) -> p t r", r=NR)

            def h2T_evac(t):
                for h in range(2):
                    dve.wait_ge(xn_ps, 2 * t + h + 1)
                    V.tensor_copy(h2T[t % 2][:, 4 * h:4 * h + 4, :],
                                  bank[6 + h][:, :].rearrange("p (k t) -> p k t", k=4)).then_inc(h2T_ready, 1)

            def logits(t):
                dve.wait_ge(lg_ps, t + 1)
                V.tensor_tensor(L[:, t, :], bank[6][:, 0:NR], rb[:, :], ALU.add).then_inc(lg_out, 1)

            dve.wait_ge(lru_rs, 1)
            for t in range(NT):
                dve.wait_ge(x_in[t], 32)
                dve.wait_ge(yc_rs, t + 1)
                for h in range(2):
                    dve.wait_ge(wo_ps, 2 * t + h + 1)
                    xc = x2[:, t, h * BANK:(h + 1) * BANK]
                    link(V.tensor_tensor(xc, xc, bank[3 * h][:, :], ALU.add))
                    link(V.scalar_tensor_tensor(xc, bank[3 * h + 1][:, :], ra[:, t:t + 1], xc, ALU.mult, ALU.add))
                    V.scalar_tensor_tensor(xc, bank[3 * h + 2][:, :], rc[:, t:t + 1], xc, ALU.mult,
                                           ALU.add).then_inc(x2_ready, 1)
                if t >= 2:
                    logits(t - 2)
                if t >= 1:
                    h2T_evac(t - 1)
            logits(NT - 2)
            h2T_evac(NT - 1)
            logits(NT - 1)

            def small(k, n_):
                return kT[:, k:k + n_]

            U = uc[:, :, :].rearrange("p a b -> p (a b)")
            arg = small(288, NT * NG + NT)
            ex = small(328, NT * NG + NT)
            arg4 = arg[:, 0:NT * NG].rearrange("p (t g) -> p t g", g=NG)
            gmax, gsum, den = small(368, NT), small(376, NT), small(384, NT)
            gt = small(392, NT * NG).rearrange("p (t g) -> p t g", g=NG)
            gfirst = small(424, NT)
            mx = [small(432 + NT * k, NT) for k in range(TOPK)]
            sel16, rk, tb = small(448, 16), small(464, 16), small(480, 16)
            nq, bl, z_ = small(496, 16), small(512, 16), small(528, 16)
            nqi = small(544, 16).bitcast(I32)
            cnt, nb, oend, tab = (small(560 + NE * k, NE) for k in range(4))
            nbi = small(688, NE).bitcast(I32)
            cover = small(0, 16)
            lm = U[:, 0:NT * NE].rearrange("p (t e) -> p t e", e=NE)
            lm4 = U[:, 0:NT * NE].rearrange("p (t g e) -> p t g e", g=NG, e=EPG)
            A = U[:, 256:768].rearrange("p (k t e) -> p k t e", k=TOPK, e=NE)
            A_n = U[:, 256:768].rearrange("p (n e) -> p n e", e=NE)
            rank = U[:, 768:1024].rearrange("p (t e) -> p t e", e=NE)
            tmp = U[:, 1024:1280].rearrange("p (t e) -> p t e", e=NE)
            tmp4 = U[:, 1024:1536].rearrange("p (k t e) -> p k t e", k=TOPK, e=NE)
            tmp_n = U[:, 1024:1536].rearrange("p (n e) -> p n e", e=NE)
            Mb = uc[:, 1, 512:640].bitcast(BF16).rearrange("p (t e) -> p t e", e=NE)
            descb = bc(desc[:, :].unsqueeze(1), [P, NT, NE])
            dg = bc(desc[:, NE - NG:NE].unsqueeze(1), [P, NT, NG])

            def per(c, w):
                return bc(c.unsqueeze(2), [P, NT, w])

            dve.wait_ge(lg_out, NT)
            link(V.tensor_reduce(gmax, L[:, :, 0:NG], AX, ALU.max))
            link(V.tensor_tensor(arg4, L[:, :, 0:NG], per(gmax, NG), ALU.subtract))
            link(V.tensor_tensor(gt, L[:, :, 0:NG], per(gmax, NG), ALU.is_equal))
            link(V.tensor_tensor(gt, gt, dg, ALU.mult))
            link(V.tensor_reduce(gfirst, gt, AX, ALU.max))
            link(V.tensor_tensor(gt, dg, per(gfirst, NG), ALU.is_equal))
            link(V.tensor_scalar(gt, gt, -1.0, BIG, ALU.add, ALU.mult))
            link(V.tensor_tensor(lm4, L[:, :, NG:NR].rearrange("p t (g e) -> p t g e", g=NG),
                                 bc(gt.unsqueeze(3), [P, NT, NG, EPG]), ALU.add))
            for k in range(TOPK):
                sel = sel16[:, k * NT:(k + 1) * NT]
                link(V.tensor_reduce(mx[k], lm, AX, ALU.max))
                if k == 1:
                    V.tensor_tensor(arg[:, NT * NG:], mx[1], mx[0], ALU.subtract).then_inc(rt_arg, 1)
                link(V.tensor_tensor(tmp, lm, per(mx[k], NE), ALU.is_equal))
                link(V.tensor_tensor(tmp, tmp, descb, ALU.mult))
                link(V.tensor_reduce(sel, tmp, AX, ALU.max))
                link(V.tensor_tensor(A[:, k], descb, per(sel, NE), ALU.is_equal))
                if k == 0:
                    link(V.scalar_tensor_tensor(lm, A[:, 0], -3.0 * BIG, lm, ALU.mult, ALU.add))
            V.tensor_tensor(Mb, A[:, 0], A[:, 1], ALU.add).then_inc(hot_ready, 1)
            dve.wait_ge(rt_exp, 1)
            link(V.tensor_reduce(gsum, ex[:, 0:NT * NG].rearrange("p (t g) -> p t g", g=NG), AX, ALU.add))
            link(V.scalar_tensor_tensor(den, ex[:, NT * NG:], 1.0, gsum, ALU.add, ALU.mult))
            link(V.reciprocal(wts[:, 0, :], den))
            link(V.tensor_tensor(wts[:, 1, :], wts[:, 0, :], ex[:, NT * NG:], ALU.mult))
            dve.wait_ge(rank_ps, 1)
            link(V.tensor_copy(rank, bank[5][:, 0:NT * NE].rearrange("p (t e) -> p t e", e=NE)))
            link(V.tensor_copy(cnt, bank[5][:, NT * NE:(NT + 1) * NE]))
            link(V.tensor_scalar(nbi, cnt, float(P - 1), None, ALU.add))
            link(V.tensor_scalar(nbi, nbi, 7, None, ALU.arith_shift_right))
            link(V.tensor_copy(nb, nbi))
            link(V.tensor_scalar(nb, nb, -1.0, 0.0, ALU.add, ALU.max))
            link(V.tensor_tensor_scan(oend, bc(ones[:, 0:1], [P, NE]), nb, 0.0, ALU.mult, ALU.add))
            link(V.scalar_tensor_tensor(tab, desc[:, :], -1.0, oend, ALU.add, ALU.add))
            link(V.tensor_tensor(tab, tab, nb, ALU.subtract))
            link(V.tensor_tensor(tmp4, A, bc(rank.unsqueeze(1), [P, TOPK, NT, NE]), ALU.mult))
            link(V.tensor_reduce(rk, tmp_n, AX, ALU.add))
            link(V.tensor_tensor(tmp_n, A_n, bc(tab.unsqueeze(1), [P, TOPK * NT, NE]), ALU.mult))
            link(V.tensor_reduce(tb, tmp_n, AX, ALU.add))
            link(V.tensor_copy(nqi, rk))
            link(V.tensor_scalar(nqi, nqi, 7, None, ALU.arith_shift_right))
            link(V.tensor_copy(nq, nqi))
            link(V.scalar_tensor_tensor(z_, nq, 1.0, tb, ALU.min, ALU.mult))
            link(V.tensor_tensor(z_, z_, nq, ALU.add))
            link(V.tensor_scalar(bl, sel16, -1.0, float(NE), ALU.mult, ALU.add))
            link(V.tensor_tensor(bl, bl, z_, ALU.add))
            link(V.scalar_tensor_tensor(rk, nq, -float(P), rk, ALU.mult, ALU.add))
            V.scalar_tensor_tensor(addr_i[:, :, :].rearrange("p k t -> p (k t)"), rk, float(NBLK), bl, ALU.mult,
                                   ALU.add).then_inc(addr_ready, 1)
            V.scalar_tensor_tensor(orow_i[:, :, :].rearrange("p k t -> p (k t)"), bl, float(P), rk, ALU.mult,
                                   ALU.add).then_inc(addr_ready, 1)
            ov = U[0:1, 1024:1024 + NOVF * NE].rearrange("p (j e) -> p j e", e=NE)
            link(V.tensor_tensor(ov, bc(oend[0:1, :].unsqueeze(1), [1, NOVF, NE]),
                                 bc(jrow[0:1, :].unsqueeze(2), [1, NOVF, NE]), ALU.is_le))
            link(V.tensor_reduce(cover[0:1, 1:NOVF + 1], ov, AX, ALU.add))
            link(V.tensor_copy(cover[0:1, 0:1], oend[0:1, NE - 1:NE]))
            V.tensor_copy(ctrl[0:1, 0:NOVF + 1], cover[0:1, 0:NOVF + 1]).then_inc(ctrl_ready, 1)

            def lo(e, j):
                dve.wait_ge(e_hi, nth(e, j))
                V.tensor_tensor(w_lo[j][:, :], raw[j], w_hi[j][:, :].bitcast(F32), ALU.subtract).then_inc(e_lo, 1)

            def x_lo_evac(e, b):
                for h in range(2):
                    dve.wait_ge(e_xh, 2 * e + (h + 1))
                    c = slice(h * BANK, (h + 1) * BANK)
                    V.tensor_tensor(x_lo[b][:, c], bank[2 + h][:, :], x_hi[b][:, c].bitcast(F32),
                                    ALU.subtract).then_inc(e_xT, 1)

            def hidden(e, up):
                dve.wait_ge(e_sg, e)
                dve.wait_ge(e_used, up)
                V.tensor_tensor(hb, sg, bank[1][:, :], ALU.mult).then_inc(e_hb, 1)

            def hidden_lo(e):
                dve.wait_ge(e_hh, e)
                V.tensor_tensor(h_lo[:, :], bank[4][:, :], h_hi[:, :].bitcast(F32), ALU.subtract).then_inc(e_hT, 1)

            for j in range(4):
                lo(0, j)
            x_lo_evac(0, 0)
            x_lo_evac(1, 1)
            for j in range(6):
                lo(1, j)
                if j == 0:
                    hidden(1, nth(0, 3))
                if j == 3:
                    hidden_lo(1)
            x_lo_evac(2, 0)
            with dve.Fori(1, NE // 2) as i:
                for b in range(2):
                    e = 2 * i + b
                    lo(e, 0)
                    hidden(e, 12 * i + (6 * b - 4))
                    lo(e, 1)
                    lo(e, 2)
                    lo(e, 3)
                    hidden_lo(e)
                    lo(e, 4)
                    lo(e, 5)
                    x_lo_evac(e + 1, 1 - b)
            hidden(NE, nth(NE - 1, 3))
            lo(NE, 4)
            lo(NE, 5)
            hidden_lo(NE)
            dve.wait_ge(ctrl_ready, 1)
            dve.wait_ge(y_stored[1], 16 * (NE // 2) + 16)
            n_ovf = dve.value_load(ctrl[0:1, 0:1], min_val=0, max_val=NOVF)
            with dve.Fori(0, NOVF) as j:
                with dve.If(j < n_ovf):
                    dve.wait_ge(o_xps, j + 1)
                    for h in range(2):
                        V.tensor_copy(xT[:, 4 * h:4 * h + 4, :],
                                      bank[2 + h][:, :].rearrange("p (k t) -> p k t", k=4)).then_inc(o_xT, 1)
                    dve.wait_ge(e_sg, j + (NE + 1))
                    V.tensor_tensor(hb, sg, bank[1][:, :], ALU.mult).then_inc(e_hb, 1)
                    dve.wait_ge(e_hps, j + (NE + 1))
                    V.tensor_copy(hbT, bank[4][:, :].rearrange("p (k t) -> p k t", k=KF)).then_inc(o_hT, 1)
                    dve.wait_ge(o_down, j + 1)
                    V.tensor_copy(yo[1][:, 0:BANK], bank[5][:, :])
                    V.tensor_copy(yo[1][:, BANK:], bank[6][:, :]).then_inc(o_y, 1)
                dve.nop()

            for t in range(NT):
                dve.wait_ge(back_in[t], 16 * TOPK)
                for k in range(TOPK):
                    last = V.scalar_tensor_tensor(x2[:, t, :], back[TOPK * t + k], wts[:, k, t:t + 1], x2[:, t, :],
                                                  ALU.mult, ALU.add)
                    if k == 0:
                        link(last)
                last.then_inc(out_ready, 1)

        @block.tensor
        def _(pe):
            M = nc.tensor.matmul

            pe.wait_ge(const_ready, 1)

            def x_transposes(t):
                pe.wait_ge(x_scaled, t + 1)
                for h in range(2):
                    u = 2 * t + h
                    if u >= 4:
                        pe.wait_ge(hT_ready, u - 3)
                    for k in range(4):
                        kk = 4 * h + k
                        last = nc.tensor.transpose(bank[2 + u % 4][:, k * P:(k + 1) * P],
                                                   xs[:, t, kk * P:(kk + 1) * P], ident[:, :])
                    last.then_inc(xT_ps, 1)

            def bank_free(u):
                if u >= 2:
                    pe.wait_ge(proj_out, u - 1)

            def channel_unit(u, w, m, hf):
                bank_free(u)
                for k in range(KD):
                    last = M(bank[u % 2][:, :], w[:, k, m * P:(m + 1) * P], hT[:, k, hf * BANK:(hf + 1) * BANK],
                             start=(k == 0), stop=(k == KD - 1))
                last.then_inc(proj_ps, 1)

            def token_unit(u, w, t):
                bank_free(u)
                for k in range(KD):
                    last = M(bank[u % 2][:, 0:w.shape[2]], hT[:, k, t * P:(t + 1) * P], w[:, k, :],
                             start=(k == 0), stop=(k == KD - 1))
                return last

            for t in range(4):
                x_transposes(t)
            pe.wait_ge(w_in_full[0], 16)
            pe.wait_ge(hT_ready, NT)
            for m in range(4):
                channel_unit(m, wA, m, 0)
            for t in range(4, NT):
                x_transposes(t)
            pe.wait_ge(hT_ready, 2 * NT)
            for m in range(4):
                channel_unit(4 + m, wA, m, 1)
            pe.wait_ge(w_in_full[1], 16)
            pe.wait_ge(rope_ready, 1)
            for hf in range(2):
                for m in range(2):
                    channel_unit(PROJ_G + 2 * hf + m, wQK, m, hf)
            pe.wait_ge(lam_in, 16 * 8)
            for u in range(8):
                j, g, hf = u // 4, u // 2 % 2, u % 2
                pe.wait_ge(conv_done, j + 1)
                if u >= 6:
                    pe.wait_ge(lru_sig, u - 5)
                M(bank[2 + u % 6][:, :], (wibd if g else wrbd)[:, j, :], uc[:, j, hf * BANK:(hf + 1) * BANK],
                  start=True, stop=True).then_inc(lru_ps, 1)
            pe.wait_ge(w_in_full[2], 16)
            pe.wait_ge(w_in_full[3], 16)
            for t in range(NT):
                u = PROJ_KV + t
                token_unit(u, wKV, t)
                for k in range(KD):
                    last = M(bank[u % 2][:, 256:256 + GLA_R], hT[:, k, t * P:(t + 1) * P], wa_sb[:, k, :],
                             start=(k == 0), stop=(k == KD - 1))
                last.then_inc(proj_ps, 1)
            pe.wait_ge(w_in_full[4], 16)
            for t in range(2):
                token_unit(PROJ_Q + t, wQ, t).then_inc(proj_ps, 1)
            pe.wait_ge(lru_sig, 8)
            pe.wait_ge(proj_out, PROJ_Q)
            for t in range(NT):
                last = nc.tensor.transpose(bank[4 + t // 4][0:GLA_R, (t % 4) * P:(t % 4 + 1) * P],
                                           zAV[:, t, 0:GLA_R], ident[:, :])
                if t % 4 == 3:
                    last.then_inc(aT_ps, 1)
            for t in range(2, 3):
                token_unit(PROJ_Q + t, wQ, t).then_inc(proj_ps, 1)
            for hf in range(2):
                pe.wait_ge(aT_out, hf + 1)
                M(bank[2 + hf][:, :], wa2[:, :], GB[0:GLA_R, 3, hf * BANK:(hf + 1) * BANK],
                  start=True, stop=True).then_inc(alpha_ps, 1)
            for t in range(3, 6):
                token_unit(PROJ_Q + t, wQ, t).then_inc(proj_ps, 1)
            pe.wait_ge(lru_ysq, 2)
            for t in range(NT):
                for j in range(2):
                    last = M(bank[6][:, t:t + 1], zA[:, j, t * P:(t + 1) * P], ones[:, 0:1],
                             start=(j == 0), stop=(j == 1))
            last.then_inc(lru_ps, 1)
            for t in range(6, NT):
                token_unit(PROJ_Q + t, wQ, t).then_inc(proj_ps, 1)

            def t1(t):
                pe.wait_ge(qk_ready, t + 1)
                if t == 0:
                    pe.wait_ge(gla_prep, 4)
                else:
                    pe.wait_ge(t1_out, t)
                if t >= 2:
                    pe.wait_ge(yc_raw, t - 1)
                    pe.wait_ge(st_ready, 2 * t - 1)
                for h in range(4):
                    nc.tensor.transpose(bank[2][:, h * P:(h + 1) * P], zQ[:, t, h * P:(h + 1) * P], ident[:, :])
                nc.tensor.transpose(bank[3][:, 0:P], zQ[:, t, SWA_W:QK], ident[:, :])
                nc.tensor.transpose(bank[3][:, P:2 * P], GB[:, 2, t * P:(t + 1) * P], ident[:, :]).then_inc(t1_ps, 1)

            def scores(t):
                pe.wait_ge(t1_out, t + 1)
                if t >= 1:
                    pe.wait_ge(pt_out, 2 * t)
                for c in range(2):
                    for pr in range(2):
                        for g in range(2):
                            rows_ = slice(64 * g, 64 * g + 64)
                            lhs = qT[rows_, t % 2, c, 2 * pr:2 * pr + 2, :]
                            o = (2 * c + pr) * P
                            if c:
                                last = M(bank[4 + g][:, o:o + P], lhs, kT[rows_, t * P:(t + 1) * P],
                                         start=True, stop=True)
                            else:
                                last = M(bank[4 + g][:, o:o + CHUNK], lhs, kT[rows_, t * P:t * P + CHUNK],
                                         start=True, stop=True)
                                if t:
                                    last = M(bank[4 + g][:, o + CHUNK:o + P], lhs,
                                             kT[rows_, t * P - CHUNK:t * P], start=True, stop=True)
                last.then_inc(s_ps, 1)

            def y_sum(t):
                pe.wait_ge(yc_sq, t + 1)
                pe.wait_ge(o_ready, t + 1)
                for m in range(4):
                    last = M(bank[6][:, 256:257], ysq[:, m, :], ones[:, 0:1], start=(m == 0), stop=(m == 3))
                last.then_inc(ysum_ps, 1)

            def yb_transposes(t):
                pe.wait_ge(o_ready, t + 1)
                pe.wait_ge(st_ready, 2 * t + 2)
                for m in range(2):
                    last = nc.tensor.transpose(bank[7][:, 256 + m * P:256 + (m + 1) * P],
                                               zVG[:, t, m * P:(m + 1) * P], ident[:, :])
                last.then_inc(yb_ps, 1)

            pe.wait_ge(lru_sum, 1)
            t1(0)
            pe.wait_ge(w_in_full[5], 16)
            for s in range(NT):
                scores(s)
                token_unit(PROJ_VG + s, wVG, s).then_inc(proj_ps, 1)
                if s >= 1:
                    y_sum(s - 1)
                    yb_transposes(s - 1)
                if s + 1 < NT:
                    t1(s + 1)
                pe.wait_ge(qx_ready, s + 1)
                if s >= 1:
                    pe.wait_ge(ysum_out, s)
                M(bank[6][:, :], GB[:, 0, s * P:(s + 1) * P], qx[:, :, :], start=True, stop=True).then_inc(att_ps, 1)
                pe.wait_ge(p_ready, s + 1)
                for m in range(8):
                    last = nc.tensor.transpose(bank[4 + m // 4][:, (m % 4) * P:(m % 4 + 1) * P],
                                               Pb[:, m, :], ident[:, :])
                last.then_inc(pt_ps, 1)
                pe.wait_ge(proj_out, PROJ_VG + s + 1)
                if s >= 1:
                    pe.wait_ge(yb_ready, s)
                if s + 1 < NT:
                    pe.wait_ge(t1_out, s + 2)
                for c in range(2):
                    r_ = slice(CHUNK * c, CHUNK * (c + 1))
                    kv = bank[7][:, 0:256] if c == 0 else bank[3][:, 256:512]
                    M(kv, kdt[r_, s % 2, :], zVG[r_, s, 0:256], start=True, stop=True).then_inc(kv_ps, 1)
                pe.wait_ge(att_out, s + 1)
                for c in range(2):
                    k = 2 * s + c
                    pe.wait_ge(st_ready, k + 1)
                    M(bank[6][CHUNK * c:CHUNK * (c + 1), 0:256], GB[:, 1, k * CHUNK:(k + 1) * CHUNK],
                      St[:, k % 4, :], start=True, stop=False, skip_group_check=True)
                for h in range(GLA_H):
                    last = M(bank[6][:, h * GLA_DV:(h + 1) * GLA_DV], attT[:, h, :],
                             zVG[:, s, h * GLA_DV:(h + 1) * GLA_DV], start=False, stop=(h == GLA_H - 1),
                             skip_group_check=True)
                last.then_inc(o_ps, 1)
                pe.wait_ge(vE_ready, s + 1)
                pe.wait_ge(pt_out, 2 * s + 2)
                for g in range(2):
                    for c in range(2):
                        v = (zAV[:, s, GLA_R + 64 * g:GLA_R + 64 * g + 64] if c else
                             vE[:, s % 2, 64 * g:64 * g + 64])
                        for i in range(2):
                            o_ = bank[2][64 * i:64 * i + 64, :].rearrange("p (m k) -> p m k", m=4)
                            last = M(o_[:, 2 * g:2 * g + 2, CHUNK * c:CHUNK * (c + 1)], v,
                                     PT[:, 4 * g + 2 * c:4 * g + 2 * c + 2, 64 * i:64 * i + 64],
                                     start=True, stop=True)
                last.then_inc(pv_ps, 1)
            y_sum(NT - 1)
            yb_transposes(NT - 1)

            def xn_transposes(t):
                pe.wait_ge(xn_ready, t + 1)
                if t >= 1:
                    pe.wait_ge(h2T_ready, 2 * t)
                    pe.wait_ge(lg_out, t)
                for h in range(2):
                    for k in range(4):
                        last = nc.tensor.transpose(bank[6 + h][:, k * P:(k + 1) * P],
                                                   xn[t % 2][:, (4 * h + k) * P:(4 * h + k + 1) * P], ident[:, :])
                    last.then_inc(xn_ps, 1)

            def router(t):
                pe.wait_ge(h2T_ready, 2 * t + 2)
                for k in range(KD):
                    last = M(bank[6][:, 0:NR], h2T[t % 2][:, k, :], rw[:, k, :], start=(k == 0), stop=(k == KD - 1))
                last.then_inc(lg_ps, 1)

            pe.wait_ge(lru_done, 2)
            pe.wait_ge(proj_out, PROJ_VG + NT)
            pe.wait_ge(pt_out, 2 * NT)
            pe.wait_ge(ysum_out, NT)
            pe.wait_ge(yc_raw, NT)
            pe.wait_ge(st_ready, 2 * NT + 1)
            pe.wait_ge(yb_ready, NT)
            for t in range(NT):
                for h in range(2):
                    pe.wait_ge(w_out_full[h], 16)
                    if t >= 1:
                        pe.wait_ge(x2_ready, 2 * t - 1 + h)
                    for part, ks in enumerate(((2, 3), (0, 1), (4, 5, 6, 7))):
                        for k in ks:
                            lhs = zA[:, 2 + k, t * P:(t + 1) * P] if k < 2 else hT[:, k, t * P:(t + 1) * P]
                            last = M(bank[3 * h + part][:, :], lhs, wO[h][:, k, :], start=(k == ks[0]),
                                     stop=(k == ks[-1]))
                    last.then_inc(wo_ps, 1)
                if t >= 2:
                    router(t - 2)
                if t >= 1:
                    xn_transposes(t - 1)
            router(NT - 2)
            xn_transposes(NT - 1)
            router(NT - 1)

            pe.wait_ge(hot_ready, 1)
            Mb = uc[:, 1, 512:640].bitcast(BF16).rearrange("p (t e) -> p t e", e=NE)
            for t in range(NT + 1):
                for t0 in range(min(t + 1, NT)):
                    last = M(bank[5][:, t * NE:(t + 1) * NE], (ltri if t0 == t else onesb)[:, :], Mb[:, t0, :],
                             start=(t0 == 0), stop=(t0 == min(t, NT - 1)))
            last.then_inc(rank_ps, 1)

            W = [slots[m].rearrange("p (k n) -> p k n", k=KF if m == 2 else KD) for m in range(3)]

            def rows_T(b, h):
                for k in range(4):
                    last = nc.tensor.transpose(bank[2 + h][:, k * P:(k + 1) * P],
                                               xg[b][:, (4 * h + k) * P:(4 * h + k + 1) * P], ident[:, :])
                return last

            def first_half(bk, j, b):
                for k in range(4):
                    kk = 4 * (j % 2) + k
                    xk, wk = slice(kk * P, (kk + 1) * P), slice(k * FF, (k + 1) * FF)
                    for n, (l, w) in enumerate(((x_hi, w_hi), (x_hi, w_lo), (x_lo, w_hi))):
                        last = M(bank[bk][:, :], l[b][:, xk], w[j][:, wk], start=(kk == 0 and n == 0),
                                 stop=(kk == KD - 1 and n == 2))
                last.then_inc(e_used, 1)

            def down_half(j):
                for k in range(2):
                    kk = 2 * (j - 4) + k
                    for n, (l, w) in enumerate(((h_hi, w_hi), (h_hi, w_lo), (h_lo, w_hi))):
                        for h in range(2):
                            last = M(bank[5 + h][:, :], l[:, kk * P:(kk + 1) * P],
                                     w[j][:, k * D + h * BANK:k * D + (h + 1) * BANK],
                                     start=(kk == 0 and n == 0), stop=(kk == KF - 1 and n == 2))
                last.then_inc(e_used, 1)

            def product(bk, w):
                for k in range(KD):
                    last = M(bank[bk][:, :], xT[:, k, :], w[:, k, :], start=(k == 0), stop=(k == KD - 1))
                return last

            def hidden_T():
                for k in range(KF):
                    last = nc.tensor.transpose(bank[4][:, k * P:(k + 1) * P], hb[:, k * P:(k + 1) * P], ident[:, :])
                return last

            def step(e, b, has, first=False, second=False):
                pe.wait_ge(e_xT, 2 * e + 2)
                if not first:
                    pe.wait_ge(e_sg, e)
                pe.wait_ge(e_lo, nth(e, 0))
                first_half(0, 0, b)
                if not first:
                    pe.wait_ge(e_hb, e)
                    hidden_T().then_inc(e_hps, 1)
                pe.wait_ge(e_lo, nth(e, 1))
                first_half(0, 1, b)
                pe.wait_ge(e_x[1 - b], has)
                rows_T(1 - b, 0).then_inc(e_xps, 1)
                pe.wait_ge(e_lo, nth(e, 2))
                first_half(1, 2, b)
                rows_T(1 - b, 1).then_inc(e_xps, 1)
                pe.wait_ge(e_lo, nth(e, 3))
                first_half(1, 3, b)
                if not first:
                    pe.wait_ge(e_hT, e)
                    if not second:
                        pe.wait_ge(e_y, e - 1)
                    for j in (4, 5):
                        pe.wait_ge(e_lo, nth(e, j))
                        down_half(j)

            pe.wait_ge(addr_ready, 2)
            pe.wait_ge(e_x[0], 16)
            for h in range(2):
                rows_T(0, h).then_inc(e_xps, 1)
            step(0, 0, 16, first=True)
            step(1, 1, 32, second=True)
            with pe.Fori(1, NE // 2) as i:
                for b in range(2):
                    step(2 * i + b, b, 16 * i + 16 * (b + 1))
            pe.wait_ge(e_hb, NE)
            hidden_T().then_inc(e_hps, 1)
            pe.wait_ge(e_hT, NE)
            pe.wait_ge(e_y, NE - 1)
            for j in (4, 5):
                pe.wait_ge(e_lo, nth(NE, j))
                down_half(j)
            pe.wait_ge(e_xT, 2 * (NE + 1))
            pe.wait_ge(e_y, NE)
            pe.wait_ge(ctrl_ready, 1)
            n_ovf = pe.value_load(ctrl[0:1, 0:1], min_val=0, max_val=NOVF)
            with pe.Fori(0, NOVF) as j:
                with pe.If(j < n_ovf):
                    pe.wait_ge(o_x, 16 * j + 16)
                    for h in range(2):
                        last = rows_T(1, h)
                    last.then_inc(o_xps, 1)
                    pe.wait_ge(o_xT, 2 * j + 2)
                    pe.wait_ge(o_w, 48 * j + 48)
                    product(0, W[0])
                    product(1, W[1]).then_inc(o_gu, 1)
                    pe.wait_ge(e_hb, j + (NE + 1))
                    hidden_T().then_inc(e_hps, 1)
                    pe.wait_ge(o_hT, j + 1)
                    for h in range(2):
                        for k in range(KF):
                            last = M(bank[5 + h][:, :], hbT[:, k, :], W[2][:, k, h * BANK:(h + 1) * BANK],
                                     start=(k == 0), stop=(k == KF - 1))
                    last.then_inc(o_down, 1)
                    pe.wait_ge(o_y, j + 1)
                    pe.sem_inc(turn, 1)
                pe.nop()


_INS = ["x", "positions", "norm1_g", "w_in", "lru_conv_w", "lru_conv_b", "lru_wr", "lru_br", "lru_wi", "lru_bi",
        "lru_lambda", "lru_out_g", "gla_wa2", "gla_ba", "gla_norm_g", "swa_q_norm_g", "swa_k_norm_g", "swa_sinks",
        "swa_out_g", "w_out", "norm2_g", "moe_wg", "moe_bg", "moe_we", "moe_be", "moe_w_gate", "moe_w_up",
        "moe_w_down"]


def kernel(**inputs):
    import numpy as _np
    import concourse.bacc as _bacc
    from concourse import mybir as _mybir
    from concourse.bass_utils import run_bass_kernel_spmd as _run

    nc = _bacc.Bacc("TRN2", target_bir_lowering=False, num_devices=1)
    arrays, args = {}, {}
    for name in _INS:
        x = _np.ascontiguousarray(inputs[name])
        arrays[f"in_{name}_dram"] = x
        args[name] = nc.dram_tensor(f"in_{name}_dram", x.shape, _mybir.dt.from_np(x.dtype), kind="ExternalInput").ap()
    out = nc.dram_tensor("out_0_dram", (1, T, D), F32, kind="ExternalOutput").ap()
    build(nc, args, out)
    r = _run(nc, [arrays], core_ids=[0])
    return r.results[0]["out_0_dram"]
```

```python
from contextlib import ExitStack

import numpy as np

import concourse.bass as bass
from concourse import mybir

ALU = mybir.AluOpType
ACT = mybir.ActivationFunctionType
AX = mybir.AxisListType.X
F32 = mybir.dt.float32
F32R = mybir.dt.float32r
BF16 = mybir.dt.bfloat16
I32 = mybir.dt.int32

P = 128
T = 1024
D = 1024
NT = T // P
KD = D // P
BANK = 512
CHUNK = 64
NCH = T // CHUNK
EPS = 1e-6

LRU_W = 256
CONV_W = 4
GLA_H, GLA_DK, GLA_DV, GLA_R = 4, 32, 64, 16
SWA_H, SWA_KV, HD = 8, 2, 64
SWA_W = SWA_H * HD
HALF = HD // 2

C_A = 0
C_BQ = 2 * LRU_W
C_BV = C_BQ + 2 * GLA_H * GLA_DK
C_BA = C_BV + 2 * GLA_H * GLA_DV
C_CQ = C_BA + GLA_R
C_CK = C_CQ + SWA_W
QK = SWA_W + SWA_KV * HD
NQK = QK // HD
AV = GLA_R + SWA_KV * HD

NG, EPG, NE, TOPK = 4, 8, 32, 2
FF = 512
KF = FF // P
NR = NG + NE
NOVF = (T * TOPK - 1) // (P + 1)
NBLK = NE + NOVF
BIG = 1.0e30
GLA_CLAMP = 43.0
GLA_TAU = 16.0

TWO_PI = 2.0 * np.pi
PI_A = 6.28125
PI_B = float(np.float32(np.round((TWO_PI - PI_A) * 2.0**21) / 2.0**21))
PI_C = float(TWO_PI - PI_A - PI_B)
ROUND = 12582912.0
PI_SAFE = 3.1415925


def build(nc, a, out):
    with ExitStack() as ctx:
        def sb(name, shape, dt=F32):
            return ctx.enter_context(nc.sbuf_tensor(name, shape, dt))

        def sem(name):
            return ctx.enter_context(nc.semaphore(name))

        x_d = a["x"][0]
        w_in = a["w_in"][0]
        w_out = a["w_out"][0]
        w_gate = a["moe_w_gate"][0]
        w_up = a["moe_w_up"][0]
        w_down = a["moe_w_down"][0]
        out_d = out[0]
        xn_d = nc.dram_tensor("xn_scratch", [T, D], F32)[:, :]
        y_d = nc.dram_tensor("assignment_rows", [TOPK * T, D], F32)[:, :]

        def next_place():
            return -(-nc.sbuf_base // 32) * 32

        ring_at = next_place()
        ring = sb("ring", [P, 5, KD * BANK])
        hT_at = next_place()
        hT = sb("hT", [P, KD, T])
        zA_at = next_place()
        zA = sb("zA", [P, 4, T])
        zG_at = next_place()
        zG = sb("zG", [P, 2, T])
        late = sb("late", [P, 9216])
        zAV = sb("zAV", [P, NT, AV])
        uc = sb("uc", [P, 2, T])
        kT = sb("kT", [P, T])
        ident = sb("ident", [P, P])
        ones = sb("ones", [P, P])
        cmask = sb("cmask", [P, P])
        ltri = sb("ltri", [P, P], BF16)
        onesb = sb("onesb", [P, P], BF16)
        hm = sb("hm", [P, GLA_H])
        wrbd = sb("wrbd", [P, 2, P])
        wibd = sb("wibd", [P, 2, P])
        wa2 = sb("wa2", [GLA_R, P])
        rw = sb("rw", [P, KD, NR])
        rb = sb("rb", [P, NR])
        qg = sb("qg", [P, HD])
        kg = sb("kg", [P, HD])
        g1 = sb("g1", [P, KD])
        cw = sb("cw", [P, CONV_W, 2])
        cb = sb("cb", [P, 2])
        br = sb("br", [P, 2])
        bi = sb("bi", [P, 2])
        lam = sb("lam", [P, 2])
        lrug = sb("lrug", [P, 2])
        ba = sb("ba", [P, 1])
        glag = sb("glag", [P, 1])
        swag = sb("swag", [P, 4])
        sinks = sb("sinks", [P, 4])
        posi = sb("posi", [P, NT], I32)
        sp = sb("sp", [P, 8, 2])
        cos = sb("cos", [P, NT, HALF])
        sin = sb("sin", [P, NT, HALF])
        half_neg = sb("half_neg", [P, NQK])
        ss = sb("ss", [P, NT])
        rs = sb("rs", [P, NT])
        dec = sb("dec", [P, NCH])
        kdt = sb("kdt", [P, 2, P])
        vE = sb("vE", [P, 2, P])
        qst = sb("qst", [P, 2, NQK])
        sst = sb("sst", [P, 6, 8])
        gst = sb("gst", [P, 2, GLA_H])
        ra = sb("ra", [P, NT])
        rc = sb("rc", [P, NT])
        desc_i = sb("desc_i", [P, NE], I32)
        desc = sb("desc", [P, NE])
        jrow = sb("jrow", [P, NOVF])
        asg = sb("asg", [P, NBLK], I32)
        asgc = sb("asgc", [P, 2, 1], I32)
        asgf = sb("asgf", [P, TOPK, NT])
        wts = sb("wts", [P, TOPK, NT])
        obuf = sb("obuf", [P, 2, 256])
        idx = sb("idx", [P, NBLK], I32)
        idxc = sb("idxc", [P, 2, 1], I32)
        tokid = sb("tokid", [P, NT], I32)
        ctrl = sb("ctrl", [P, 16], I32)

        xs = late[:, 0:NT * D].rearrange("p (t d) -> p t d", t=NT)
        x2 = xs
        zVG = late[:, 0:NT * 512].rearrange("p (t c) -> p t c", t=NT)
        zQ = late[:, NT * 512:NT * 512 + NT * QK].rearrange("p (t c) -> p t c", t=NT)
        ri = late[:, 0:4 * T].rearrange("p (n t) -> p n t", n=4)
        GB = ring[:, 2, :].rearrange("p (n t) -> p n t", n=4)
        wA = ring[:, 0, :].rearrange("p (k n) -> p k n", k=KD)
        wQK = ring[:, 1, 0:KD * 256].rearrange("p (k n) -> p k n", k=KD)
        wKVA = ring[:, 2, 0:KD * (256 + GLA_R)].rearrange("p (k n) -> p k n", k=KD)
        wQ = ring[:, 3, :].rearrange("p (k n) -> p k n", k=KD)
        wVG = ring[:, 4, :].rearrange("p (k n) -> p k n", k=KD)
        wO = [ring[:, n, :] for n in range(2)]
        Pb = zA[:, 0, :].rearrange("p (n k) -> p n k", n=8)
        ysq = zA[:, 1, 0:512].rearrange("p (n k) -> p n k", n=4)
        vkm = zA[:, 1, 512:768]
        PT = uc[:, 0, :].rearrange("p (n k) -> p n k", n=8)
        qT = uc[:, 1, :].rearrange("p (b c n q) -> p b c n q", b=2, c=2, n=4)
        qx = zG[:, 0, 0:512].rearrange("p (h t) -> p h t", h=GLA_H)
        attT = zG[:, 0, 512:1024].rearrange("p (h t) -> p h t", h=GLA_H)
        St = zG[:, 1, :].rearrange("p (n v) -> p n v", n=4)
        sqs = sb("sqs", [P, QK])
        rt = sqs[:, :].rearrange("p (n h d) -> p n h d", n=2, d=HALF)

        xn = [zG[:, b, :] for b in range(2)]
        h2T = [zA[:, b, :].rearrange("p (k t) -> p k t", k=KD) for b in range(2)]
        route = kT
        slots = [ring[:, 3, :], ring[:, 4, :], ring[:, 2, :]]
        xg = [hT[:, 4 + b, :] for b in range(2)]
        xT = hT[:, 7, :].rearrange("p (k t) -> p k t", k=KD)
        yo = [zA[:, b, :] for b in range(2)]
        sg = zA[:, 2, 0:FF]
        hb = zA[:, 2, FF:2 * FF]
        hbT = zA[:, 3, 0:FF].rearrange("p (k t) -> p k t", k=KF)
        HALF_W = KD * BANK // 2

        def over(name, at, n):
            return nc.alloc_sbuf_tensor_at(name, [P, n], F32R, offset=at)

        SLOT_B = 4 * KD * BANK
        o_hi = [over(f"o_hi{h}", ring_at + (3 + h) * SLOT_B, KD * BANK) for h in range(2)]
        o_lo = [over(f"o_lo{h}", ring_at + h * SLOT_B, KD * BANK) for h in range(2)]
        y_hi = [over(f"y_hi{b}", ring_at + 2 * SLOT_B + 4 * b * D, D) for b in range(2)]
        y_lo = [over(f"y_lo{b}", ring_at + 2 * SLOT_B + 4 * (2 + b) * D, D) for b in range(2)]

        raw = [slots[j // 2][:, (j % 2) * HALF_W:(j % 2 + 1) * HALF_W] for j in range(6)]
        raw_at = [ring_at + 4 * (2 * n + h) * HALF_W for n in (3, 4, 2) for h in range(2)]
        hi_at = [hT_at + 4 * h * HALF_W for h in range(2)] + [ring_at + 4 * n * HALF_W for n in range(4)]
        w_lo = [over(f"w_lo{j}", raw_at[j], HALF_W) for j in range(6)]
        w_hi = [over(f"w_hi{j}", hi_at[j], HALF_W) for j in range(6)]
        x_hi = [over(f"x_hi{b}", hT_at + 4 * (6 + b) * T, D) for b in range(2)]
        x_lo = [over(f"x_lo{b}", zG_at + 4 * b * T, D) for b in range(2)]
        h_hi = over("h_hi", zA_at + 4 * 3 * T, FF)
        h_lo = over("h_lo", zA_at + 4 * (3 * T + FF), FF)
        slot_hots = uc[:, :, :].rearrange("p a b -> p (a b)").rearrange("p (n s) -> p n s", s=P)
        blk_hots = zAV[:, :, :].rearrange("p t c -> p (t c)")[:, 0:TOPK * NT * NBLK].rearrange(
            "p (n b) -> p n b", b=NBLK)
        count = sqs[:, 0:P]
        g2b = zAV[:, :, :].rearrange("p t c -> p (t c)")[:, 0:D]
        back = [ring[:, n // 4, (n % 4) * D:(n % 4 + 1) * D] for n in range(16)]

        bank = [ctx.enter_context(nc.psum_tensor(f"bank{i}", [P, BANK], F32)) for i in range(8)]

        x_in = [sem(f"x_in{t}") for t in range(NT)]
        c_in = sem("c_in")
        c_late = sem("c_late")
        w_in_full = [sem(f"w_in_full{n}") for n in range(6)]
        const_ready = sem("const_ready")
        wbd_zero = sem("wbd_zero")
        x_ss = sem("x_ss")
        x_rs = sem("x_rs")
        x_scaled = sem("x_scaled")
        xT_ps = sem("xT_ps")
        hT_ready = sem("hT_ready")
        proj_ps = sem("proj_ps")
        proj_out = sem("proj_out")
        dv = sem("dv")
        av = sem("av")
        pv_ = sem("pool_chain")
        conv_done = sem("conv_done")
        lru_ps = sem("lru_ps")
        lru_sig = sem("lru_sig")
        lru_iu = sem("lru_iu")
        lru_tanh = sem("lru_tanh")
        lru_m2 = sem("lru_m2")
        lru_sqrt = sem("lru_sqrt")
        lru_gelu = sem("lru_gelu")
        lru_y = sem("lru_y")
        lru_ysq = sem("lru_ysq")
        lru_sum = sem("lru_sum")
        lru_rs = sem("lru_rs")
        lru_done = sem("lru_done")
        lam_e = sem("lam_e")
        c8_ready = sem("c8_ready")
        rope_arg = sem("rope_arg")
        rope_ready = sem("rope_ready")
        aT_ps = sem("aT_ps")
        aT_out = sem("aT_out")
        alpha_ps = sem("alpha_ps")
        gla_na = sem("gla_na")
        gla_ln = sem("gla_ln")
        gla_b = sem("gla_b")
        gla_exp = sem("gla_exp")
        gla_prep = sem("gla_prep")
        qk_sq = sem("qk_sq")
        qk_ss = sem("qk_ss")
        qk_rs = sem("qk_rs")
        qk_scaled = sem("qk_scaled")
        qk_gained = sem("qk_gained")
        qk_ready = sem("qk_ready")
        t1_ps = sem("t1_ps")
        t1_out = sem("t1_out")
        s_ps = sem("s_ps")
        s_negm = sem("s_negm")
        p_exp = sem("p_exp")
        p_ready = sem("p_ready")
        pt_ps = sem("pt_ps")
        pt_out = sem("pt_out")
        vE_ready = sem("vE_ready")
        pv_ps = sem("pv_ps")
        yc_sq = sem("yc_sq")
        yc_raw = sem("yc_raw")
        ysum_ps = sem("ysum_ps")
        ysum_out = sem("ysum_out")
        yc_rs = sem("yc_rs")
        qx_ready = sem("qx_ready")
        att_ps = sem("att_ps")
        att_out = sem("att_out")
        kv_ps = sem("kv_ps")
        st_ready = sem("st_ready")
        o_ps = sem("o_ps")
        o_sq = sem("o_sq")
        o_ss = sem("o_ss")
        o_rs = sem("o_rs")
        o_tanh = sem("o_tanh")
        o_ready = sem("o_ready")
        yb_ps = sem("yb_ps")
        yb_ready = sem("yb_ready")
        wo_ps = sem("wo_ps")
        x2_ready = sem("x2_ready")
        wo_hi = sem("wo_hi")
        wo_lo = sem("wo_lo")
        y_hi_ready = sem("y_hi_ready")
        y_lo_ready = sem("y_lo_ready")
        x2_ss = sem("x2_ss")
        x2_rs = sem("x2_rs")
        xn_ready = sem("xn_ready")
        xn_stored = [sem(f"xn_stored{b}") for b in range(2)]
        xn_ps = sem("xn_ps")
        h2T_ready = sem("h2T_ready")
        lg_ps = sem("lg_ps")
        lg_out = sem("lg_out")
        rt_arg = sem("rt_arg")
        rt_exp = sem("rt_exp")
        hot_ready = sem("hot_ready")
        rank_ps = sem("rank_ps")
        ctrl_ready = sem("ctrl_ready")
        slot_hot = sem("slot_hot")
        slot_ps = sem("slot_ps")
        slot_ready = sem("slot_ready")
        e_w = [sem(f"e_w{j}") for j in range(6)]
        e_x = [sem(f"e_x{b}") for b in range(2)]
        y_stored = [sem(f"y_stored{b}") for b in range(2)]
        (xn_scaled, e_xps, e_col, e_xh, e_xT, e_hi, e_lo, e_used, e_sg, e_hb, e_hps, e_hh, e_hT, e_y,
         turn, o_w, o_x, o_xps, o_xT, o_gu, o_hT, o_down, o_y, o_stored, out_ready,
         out_stored) = (sem(n) for n in (
             "xn_scaled", "e_xps", "e_col", "e_xh", "e_xT", "e_hi", "e_lo", "e_used", "e_sg", "e_hb",
             "e_hps", "e_hh", "e_hT", "e_y", "turn", "o_w", "o_x", "o_xps", "o_xT", "o_gu",
             "o_hT", "o_down", "o_y", "o_stored", "out_ready", "out_stored"))
        back_in = [sem(f"back_in{t}") for t in range(NT)]

        block = ctx.enter_context(nc.Block())

        C_LATE = 16 * 31
        PROJ_A, PROJ_G, PROJ_KV, PROJ_Q = 0, 8, 12, 20
        PROJ_ALL = 36
        Q_AHEAD = 6

        def unit_q(t):
            return PROJ_Q + t if t < Q_AHEAD else PROJ_Q + Q_AHEAD + 1 + 2 * (t - Q_AHEAD)

        def unit_vg(t):
            return PROJ_Q + Q_AHEAD + t + min(t, NT - Q_AHEAD)

        def rows(w, c0, n):
            return w[:, c0:c0 + n].rearrange("(k p) n -> p k n", p=P)

        LAST = 6 * NE

        def nth(e, j):
            if isinstance(e, int):
                return j + 1 if e == 0 else min(6 * e + j - 1, 6 * NE + j - 5)
            return 6 * e + (j - 1)

        def y_parts(t, dst):
            c = slice(t * P, (t + 1) * P)
            return ((zA[:, 2:4, c], dst[:, 0:2 * P].rearrange("p (k t) -> p k t", t=P)),
                    (hT[:, 2:8, c], dst[:, 2 * P:D].rearrange("p (k t) -> p k t", t=P)))

        def place(e, j):
            return j - 4 if isinstance(e, int) and e == NE else j

        def loads(e, j):
            return e + 1 if place(e, j) < 4 else e

        def bc(ap, shape):
            return ap.to_broadcast(shape)

        @block.sync
        def _(sp_):
            def col(dst, src, k, s=c_late):
                sp_.dma_start(dst, src.rearrange("(k p) -> p k", p=P), allow_slow_non_contiguous=True).then_inc(s, 16)

            for t in range(NT):
                sp_.dma_start(xs[:, t, :], x_d[t * P:(t + 1) * P, :]).then_inc(x_in[t], 16)
                if t == 3:
                    sp_.dma_start(wA, rows(w_in, C_A, 512)).then_inc(w_in_full[0], 16)
            sp_.dma_start(posi[:, :], a["positions"][0].rearrange("(k p) -> p k", p=P),
                          allow_slow_non_contiguous=True).then_inc(c_late, 16)
            for tap in range(CONV_W):
                col(cw[:, tap, :], a["lru_conv_w"][0, tap], 2)
            col(cb[:, :], a["lru_conv_b"][0], 2)
            col(br[:, :], a["lru_br"][0], 2)
            col(bi[:, :], a["lru_bi"][0], 2)
            col(lam[:, :], a["lru_lambda"][0], 2)
            col(lrug[:, :], a["lru_out_g"][0], 2)
            col(ba[:, :], a["gla_ba"][0], 1)
            col(swag[:, :], a["swa_out_g"][0], 4)

            for i in range(2):
                sp_.dma_start(glag[64 * i:64 * i + 64, :], a["gla_norm_g"][0].rearrange("(p o) -> p o", o=1),
                              allow_slow_non_contiguous=True).then_inc(c_late, 16)
                sp_.dma_start(sinks[64 * i:64 * i + 64, :],
                              bc(a["swa_sinks"][:, i:SWA_H:2], [64, 4]),
                              allow_slow_non_contiguous=True).then_inc(c_late, 16)
            sp_.dma_start(qg[:, :], bc(a["swa_q_norm_g"][:, :], [P, HD])).then_inc(c_late, 16)
            sp_.dma_start(kg[:, :], bc(a["swa_k_norm_g"][:, :], [P, HD])).then_inc(c_late, 16)
            sp_.dma_start(rb[:, 0:NG], bc(a["moe_bg"][:, :], [P, NG])).then_inc(c_late, 16)
            sp_.dma_start(rb[:, NG:NR], bc(a["moe_be"][:, :], [P, NE])).then_inc(c_late, 16)
            sp_.dma_start(wa2[:, :], a["gla_wa2"][0]).then_inc(c_late, 16)
            sp_.dma_start(rw[:, :, 0:NG], rows(a["moe_wg"][0], 0, NG)).then_inc(c_late, 16)
            sp_.dma_start(rw[:, :, NG:NR], rows(a["moe_we"][0], 0, NE)).then_inc(c_late, 16)
            sp_.wait_ge(wbd_zero, 1)
            for blk in range(4):
                j, r = blk // 2, 64 * (blk % 2)
                sp_.dma_start(wrbd[r:r + 64, j, r:r + 64], a["lru_wr"][0, blk]).then_inc(c_late, 16)
                sp_.dma_start(wibd[r:r + 64, j, r:r + 64], a["lru_wi"][0, blk]).then_inc(c_late, 16)
            sp_.dma_start(wQK, rows(w_in, C_BQ, 256)).then_inc(w_in_full[1], 16)
            sp_.dma_start(wKVA[:, :, 0:256], rows(w_in, C_CK, 256)).then_inc(w_in_full[2], 16)
            sp_.dma_start(wKVA[:, :, 256:], rows(w_in, C_BA, GLA_R)).then_inc(w_in_full[3], 16)
            sp_.dma_start(wQ, rows(w_in, C_CQ, 512)).then_inc(w_in_full[4], 16)
            sp_.dma_start(wVG, rows(w_in, C_BV, 512)).then_inc(w_in_full[5], 16)
            sp_.wait_ge(proj_ps, PROJ_G)
            sp_.dma_start(wO[0].rearrange("p (k n) -> p k n", k=KD), rows(w_out, 0, 512)).then_inc(w_in_full[0], 16)
            sp_.wait_ge(proj_ps, PROJ_Q)
            sp_.dma_start(wO[1].rearrange("p (k n) -> p k n", k=KD), rows(w_out, 512, 512)).then_inc(w_in_full[1], 16)

            def expert_rows(w, e):
                return w[e] if isinstance(e, int) else w[bass.ds(e, 1)].rearrange("o r c -> (o r) c")

            def expert_half(e, j):
                w, k = ((w_gate, 4), (w_up, 4), (w_down, 2))[j // 2]
                src = expert_rows(w, e - 1 if j >= 4 else e)
                h = j % 2
                m = place(e, j)
                sp_.dma_start(raw[m].rearrange("p (k n) -> p k n", k=k),
                              src[h * k * P:(h + 1) * k * P, :].rearrange("(k p) n -> p k n", p=P)
                              ).then_inc(e_w[m], 16)

            def expert_unit(m, e, s_):
                k = KF if m == 2 else KD
                sp_.dma_start(slots[m].rearrange("p (k n) -> p k n", k=k),
                              expert_rows((w_gate, w_up, w_down)[m], e).rearrange("(k p) n -> p k n", p=P)
                              ).then_inc(s_, 16)

            sp_.wait_ge(yb_ps, NT)
            sp_.wait_ge(qk_ready, NT)
            sp_.wait_ge(t1_ps, NT)
            sp_.wait_ge(yc_sq, NT)
            for t in range(NT):
                sp_.dma_start(x2[:, t, :], x_d[t * P:(t + 1) * P, :]).then_inc(x_in[t], 16)
            sp_.wait_ge(pv_ps, NT)
            sp_.dma_start(g2b, bc(a["norm2_g"][:, :], [P, D])).then_inc(c_in, 16)
            for t in range(NT):
                if t == NT - 1:
                    sp_.wait_ge(wo_ps, 2 * NT)
                    for j in range(4):
                        expert_half(0, j)
                sp_.wait_ge(xn_ready, t + 1)
                sp_.dma_start(xn_d[t * P:(t + 1) * P, :], xn[t % 2]).then_inc(xn_stored[t % 2], 16)
            for j in range(4, 6):
                expert_half(1, j)
            for j in range(4):
                sp_.wait_ge(e_used, nth(0, j))
                expert_half(1, j)
            with sp_.Fori(1, NE // 2) as i:
                for b in range(2):
                    for j in range(6):
                        sp_.wait_ge(e_used, 12 * i + (6 * b + j - 7))
                        expert_half(2 * i + b, j)
            for j in range(4, 6):
                sp_.wait_ge(e_used, nth(NE - 1, place(NE, j)))
                expert_half(NE, j)
            sp_.wait_ge(e_used, LAST)
            sp_.wait_ge(ctrl_ready, 1)
            n_ovf = sp_.value_load(ctrl[0:1, 0:1], min_val=0, max_val=NOVF)
            with sp_.If(0 < n_ovf):
                with sp_.Fori(0, NOVF) as j:
                    with sp_.If(j < n_ovf):
                        e = sp_.value_load(ctrl[0:1, bass.ds(j + 1, 1)], min_val=0, max_val=NE - 1)
                        for m in range(3):
                            expert_unit(m, e, o_w)
                        sp_.wait_ge(o_stored, 16 * j + 16)
                        sp_.sem_inc(turn, 1)
                    sp_.nop()
            for b in range(2):
                sp_.wait_ge(y_stored[b], 16 * (NE // 2))
            for t in range(NT):
                if t >= 2:
                    sp_.wait_ge(back_in[t - 2], 16 * TOPK)
                for k in range(TOPK):
                    r0 = k * T + t * P
                    sp_.dma_start(back[TOPK * t + k], y_d[r0:r0 + P, :]).then_inc(back_in[t], 16)

        @block.gpsimd
        def _(pool):
            n = [0]

            def link(ins):
                n[0] += 1
                ins.then_inc(pv_, 1)
                pool.wait_ge(pv_, n[0])

            link(nc.gpsimd.memset(ident[:], 0.0))
            link(nc.gpsimd.affine_select(out=ident[:], in_=ident[:], compare_op=ALU.not_equal, fill=1.0, base=0,
                                         pattern=[[-1, P]], channel_multiplier=1))
            link(nc.gpsimd.memset(half_neg[:], -0.5))
            nc.gpsimd.memset(ones[:], 1.0).then_inc(const_ready, 1)
            pool.wait_ge(const_ready, 1)
            link(nc.gpsimd.memset(wrbd[:], 0.0))
            nc.gpsimd.memset(wibd[:], 0.0).then_inc(wbd_zero, 1)
            pool.wait_ge(wbd_zero, 1)
            link(nc.gpsimd.memset(onesb[:], 1.0))
            link(nc.gpsimd.memset(cmask[:], 1.0))
            link(nc.gpsimd.affine_select(out=cmask[:], in_=cmask[:], compare_op=ALU.is_ge, fill=0.0, base=0,
                                         pattern=[[1, P]], channel_multiplier=-1))
            link(nc.gpsimd.memset(cmask[0:CHUNK, CHUNK:P], 0.0))
            link(nc.gpsimd.memset(ltri[:], 1.0))
            link(nc.gpsimd.affine_select(out=ltri[:], in_=ltri[:], compare_op=ALU.is_ge, fill=0.0, base=-1,
                                         pattern=[[1, P]], channel_multiplier=-1))
            link(nc.gpsimd.memset(hm[:], 0.0))
            for h in range(GLA_H):
                link(nc.gpsimd.memset(hm[32 * h:32 * h + 32, h:h + 1], 1.0))
            link(nc.gpsimd.iota(tokid[:], [[P, NT]], base=0, channel_multiplier=1))
            link(nc.gpsimd.iota(desc_i[:], [[-1, NE]], base=NE, channel_multiplier=0))
            nc.gpsimd.memset(vE[CHUNK:P, 0, :], 0.0).then_inc(const_ready, 1)
            pool.wait_ge(const_ready, 2)

            def rstd_x(t):
                pool.wait_ge(x_ss, t + 1)
                link(nc.gpsimd.tensor_scalar(rs[:, t:t + 1], ss[:, t:t + 1], 1.0 / D, EPS, ALU.mult, ALU.add))
                nc.gpsimd.tensor_tensor(rs[:, t:t + 1], rs[:, t:t + 1], half_neg[:, 0:1], ALU.pow).then_inc(x_rs, 1)

            for t in range(NT):
                rstd_x(t)
            def qk_norm(t):
                pool.wait_ge(qk_ss, t + 1)
                link(nc.gpsimd.tensor_scalar(qst[:, 1, :], qst[:, 0, :], 1.0 / HD, EPS, ALU.mult, ALU.add))
                nc.gpsimd.tensor_tensor(qst[:, 1, :], qst[:, 1, :], half_neg[:, 0:NQK], ALU.pow).then_inc(qk_rs, 1)
                pool.wait_ge(qk_scaled, t + 1)
                q3 = zQ[:, t, 0:SWA_W].rearrange("p (h d) -> p h d", d=HD)
                k3 = zQ[:, t, SWA_W:QK].rearrange("p (h d) -> p h d", d=HD)
                link(nc.gpsimd.tensor_tensor(q3, q3, bc(qg[:, :].unsqueeze(1), [P, SWA_H, HD]), ALU.mult))
                nc.gpsimd.tensor_tensor(k3, k3, bc(kg[:, :].unsqueeze(1), [P, SWA_KV, HD]),
                                        ALU.mult).then_inc(qk_gained, 1)

            pool.wait_ge(c_late, C_LATE)
            qk_norm(0)
            pool.wait_ge(qk_gained, 1)
            pool.wait_ge(lru_sum, 1)
            nc.gpsimd.tensor_tensor(ra[:], ra[:], half_neg[:, 0:NT], ALU.pow).then_inc(lru_rs, 1)
            pool.wait_ge(lru_rs, 1)
            qk_norm(1)
            pool.wait_ge(qk_gained, 2)

            def yc_rstd(t):
                pool.wait_ge(ysum_out, t + 1)
                nc.gpsimd.tensor_tensor(rc[:, t:t + 1], rc[:, t:t + 1], half_neg[:, 0:1], ALU.pow).then_inc(yc_rs, 1)
                pool.wait_ge(yc_rs, t + 1)

            for s in range(NT):
                if s >= 1:
                    if s >= 2:
                        pool.wait_ge(pv_ps, s - 1)
                    link(nc.gpsimd.tensor_copy(vE[CHUNK:P, s % 2, :], zAV[CHUNK:P, s - 1, GLA_R:AV]))
                nc.gpsimd.tensor_copy(vE[0:CHUNK, s % 2, :], zAV[0:CHUNK, s, GLA_R:AV]).then_inc(vE_ready, 1)
                pool.wait_ge(vE_ready, s + 1)
                if s >= 1:
                    yc_rstd(s - 1)
                if s + 2 < NT:
                    qk_norm(s + 2)
                pool.wait_ge(o_ss, s + 1)
                link(nc.gpsimd.tensor_scalar(gst[:, 1, :], gst[:, 0, :], 1.0 / GLA_DV, EPS, ALU.mult, ALU.add))
                nc.gpsimd.tensor_tensor(gst[:, 1, :], gst[:, 1, :], half_neg[:, 0:GLA_H],
                                        ALU.pow).then_inc(o_rs, 1)
                pool.wait_ge(o_rs, s + 1)
            yc_rstd(NT - 1)

            for t in range(NT):
                pool.wait_ge(x2_ss, t + 1)
                link(nc.gpsimd.tensor_scalar(rs[:, t:t + 1], ss[:, t:t + 1], 1.0 / D, EPS, ALU.mult, ALU.add))
                nc.gpsimd.tensor_tensor(rs[:, t:t + 1], rs[:, t:t + 1], half_neg[:, 0:1],
                                        ALU.pow).then_inc(x2_rs, 1)

                pool.wait_ge(x2_rs, t + 1)
                pool.wait_ge(xn_scaled, t + 1)
                if t == 0:
                    pool.wait_ge(c_in, 32)
                nc.gpsimd.tensor_tensor(xn[t % 2], xn[t % 2], g2b, ALU.mult).then_inc(xn_ready, 1)
                pool.wait_ge(xn_ready, t + 1)

            pool.wait_ge(slot_ready, 2)
            for b in range(2):
                pool.wait_ge(xn_stored[b], 16 * NT // 2)

            def gather_at(at, b, s_):
                nc.gpsimd.indirect_dma_start(
                    out=xg[b], out_offset=None, in_=xn_d, in_offset=bass.IndirectOffsetOnAxis(ap=at, axis=0),
                    bounds_check=T - 1, oob_is_err=False).then_inc(s_, 16)

            def gather(col, copies, b, s_):
                nc.gpsimd.tensor_copy(idxc[:, b, :], idx[:, bass.ds(col, 1)]).then_inc(e_col, 1)
                pool.wait_ge(e_col, copies)
                pool.sem_inc(turn, 1)
                gather_at(idxc[:, b, :], b, s_)

            for b in range(2):
                gather_at(idx[:, b:b + 1], b, e_x[b])
            def scatter_at(at, b, s_):
                nc.gpsimd.indirect_dma_start(
                    out=y_d, out_offset=bass.IndirectOffsetOnAxis(ap=at, axis=0), in_=yo[b], in_offset=None,
                    bounds_check=TOPK * T - 1, oob_is_err=False).then_inc(s_, 16)

            def scatter(col, copies, b, s_):
                nc.gpsimd.tensor_copy(asgc[:, b, :], asg[:, bass.ds(col, 1)]).then_inc(e_col, 1)
                pool.wait_ge(e_col, copies)
                pool.sem_inc(turn, 1)
                scatter_at(asgc[:, b, :], b, s_)

            for b in range(2):
                pool.wait_ge(e_xps, 2 * b + 2)
                gather_at(idx[:, b + 2:b + 3], b, e_x[b])
            with pool.Fori(2, NE // 2) as i:
                for b in range(2):
                    e = 2 * i + b
                    pool.wait_ge(e_xps, 2 * e - 2)
                    gather(e, 4 * i + (2 * b - 7), b, e_x[b])
                    pool.wait_ge(e_y, e - 3)
                    scatter(2 * i + (b - 4), 4 * i + (2 * b - 6), b, y_stored[b])
            pool.wait_ge(e_xps, 2 * NE - 2)
            gather_at(idx[:, 0:1], 0, e_x[0])
            for e in range(NE - 4, NE):
                pool.wait_ge(e_y, e + 1)
                scatter_at(asg[:, e:e + 1], e % 2, y_stored[e % 2])
            COPIES = 2 * (NE - 4)
            pool.wait_ge(e_xps, 2 * (NE + 1))
            pool.wait_ge(ctrl_ready, 1)
            n_ovf = pool.value_load(ctrl[0:1, 0:1], min_val=0, max_val=NOVF)
            with pool.If(0 < n_ovf):
                with pool.Fori(0, NOVF) as j:
                    with pool.If(j < n_ovf):
                        gather(j + NE, 2 * j + (COPIES + 1), 1, o_x)
                        pool.wait_ge(o_y, j + 1)
                        scatter(j + NE, 2 * j + (COPIES + 2), 1, o_stored)
                        pool.wait_ge(o_stored, 16 * j + 16)
                        pool.sem_inc(turn, 1)
                    pool.nop()


        @block.scalar
        def _(act):
            n = [0]

            def link(ins):
                n[0] += 1
                ins.then_inc(av, 1)
                act.wait_ge(av, n[0])

            act.wait_ge(const_ready, 1)
            act.dma_start(g1[:, :], a["norm1_g"][0].rearrange("(k p) -> p k", p=P),
                          allow_slow_non_contiguous=True).then_inc(c_in, 16)
            for t in range(NT):
                act.wait_ge(x_in[t], 16)
                if t:
                    act.wait_ge(x_ss, t)
                nc.scalar.activation(uc[:, 0, :], xs[:, t, :], ACT.Square,
                                     accum_out=ss[:, t:t + 1]).then_inc(x_ss, 1)
            def evac(u, dst, src=None):
                act.wait_ge(proj_ps, u + 1)
                nc.scalar.copy(dst, bank[u % 2][:, :] if src is None else src).then_inc(proj_out, 1)

            def evac_q(t):
                u = unit_q(t)
                evac(u, zQ[:, t, 0:SWA_W].rearrange("p (h g d) -> p g h d", g=2, d=HD),
                     bank[u % 2][:, :].rearrange("p (g h d) -> p g h d", g=2, d=HD))

            def evac_kv(t):
                b = bank[(PROJ_KV + t) % 2]
                act.wait_ge(proj_ps, PROJ_KV + t + 1)
                nc.scalar.copy(zQ[:, t, SWA_W:QK], b[:, 0:128])
                nc.scalar.copy(zAV[:, t, GLA_R:AV], b[:, 128:256])
                nc.scalar.copy(zAV[:, t, 0:GLA_R], b[:, 256:256 + GLA_R]).then_inc(proj_out, 1)

            for m in range(4):
                evac(m, zA[:, m, 0:BANK])
            act.wait_ge(c_late, C_LATE)
            act.wait_ge(c_in, 16)
            act.wait_ge(rope_arg, 1)
            nc.scalar.activation(sin[:, :, :], zG[:, 0, 0:256].rearrange("p (t d) -> p t d", t=NT), ACT.Sin)
            nc.scalar.activation(cos[:, :, :], zG[:, 1, 0:256].rearrange("p (t d) -> p t d", t=NT),
                                 ACT.Sin).then_inc(rope_ready, 1)
            act.wait_ge(lam_e, 1)
            nc.scalar.activation(sp[:, 1, :], sp[:, 0, :], ACT.Exp).then_inc(lam_e, 1)
            for m in range(4):
                evac(4 + m, zA[:, m, BANK:T])
            for hf in range(2):
                for m in range(2):
                    evac(PROJ_G + 2 * hf + m, zG[:, m, hf * BANK:(hf + 1) * BANK])
            for u in range(8):
                j, g, hf = u // 4, u // 2 % 2, u % 2
                act.wait_ge(lru_ps, u + 1)
                nc.scalar.activation(ri[:, 2 * j + g, hf * BANK:(hf + 1) * BANK], bank[2 + u % 6][:, :], ACT.Sigmoid,
                                     bias=(bi if g else br)[:, j:j + 1]).then_inc(lru_sig, 1)
            act.wait_ge(c8_ready, 1)
            act.wait_ge(lru_sig, 8)
            for j in range(2):
                act.wait_ge(conv_done, j + 1)
                link(nc.scalar.activation(zA[:, j, :], ri[:, 2 * j, :], ACT.Tanh, scale=sp[:, 7, j:j + 1]))
                nc.scalar.activation(ri[:, 2 * j, :], ri[:, 2 * j, :], ACT.Exp,
                                     scale=sp[:, 7, j:j + 1]).then_inc(lru_tanh, 1)
            for t in range(2):
                evac_kv(t)
            for j in range(2):
                nc.scalar.activation(zA[:, 2 + j, :], zA[:, 2 + j, :], ACT.Gelu_apprx_tanh).then_inc(lru_gelu, 1)
            for t in range(2, 4):
                evac_kv(t)
            for j in range(2):
                act.wait_ge(lru_m2, j + 1)
                nc.scalar.activation(zA[:, j, :], zA[:, j, :], ACT.Sqrt).then_inc(lru_sqrt, 1)
            for t in range(4, NT):
                evac_kv(t)
            for hf in range(2):
                act.wait_ge(aT_ps, hf + 1)
                nc.scalar.copy(GB[0:GLA_R, 3, hf * BANK:(hf + 1) * BANK],
                               bank[4 + hf][0:GLA_R, :]).then_inc(aT_out, 1)
            for t in range(2):
                evac_q(t)

            def qk_square(t):
                if t >= 1:
                    act.wait_ge(qk_ready, t)
                nc.scalar.activation(sqs[:, :], zQ[:, t, :], ACT.Square).then_inc(qk_sq, 1)

            act.wait_ge(proj_out, PROJ_Q + 1)
            qk_square(0)
            for j in range(2):
                act.wait_ge(lru_y, j + 1)
                nc.scalar.activation(zA[:, j, :], zA[:, 2 + j, :], ACT.Square).then_inc(lru_ysq, 1)
            act.wait_ge(gla_na, 1)
            link(nc.scalar.activation(GB[:, 1, :], GB[:, 1, :], ACT.Exp))
            nc.scalar.activation(GB[:, 1, :], GB[:, 1, :], ACT.Ln, bias=1.0).then_inc(gla_ln, 1)
            for t in range(2, 4):
                evac_q(t)
            qk_square(1)
            act.wait_ge(gla_b, 1)
            b3 = GB[:, 1, :].rearrange("p (c i) -> p c i", i=CHUNK)
            nc.scalar.activation(GB[:, 3, :], GB[:, 0, :], ACT.Exp, scale=1.0 / GLA_TAU).then_inc(gla_exp, 1)
            act.wait_ge(gla_exp, 1)
            nc.scalar.activation(GB[:, 0, :], GB[:, 0, :], ACT.Exp, scale=-1.0 / GLA_TAU).then_inc(gla_exp, 1)
            nc.scalar.activation(GB[:, 2, :], GB[:, 2, :], ACT.Exp, scale=1.0 / GLA_TAU).then_inc(gla_exp, 1)
            link(nc.scalar.activation(dec[:, :].unsqueeze(2), b3[:, :, CHUNK - 1:CHUNK], ACT.Exp,
                                      scale=1.0 / GLA_TAU))
            nc.scalar.activation(GB[:, 1, :], GB[:, 1, :], ACT.Exp, scale=1.0 / GLA_TAU).then_inc(gla_exp, 1)

            for t in range(4, Q_AHEAD):
                evac_q(t)

            def t1_evac(t):
                act.wait_ge(t1_ps, t + 1)
                if t >= 2:
                    act.wait_ge(s_ps, t - 1)
                    act.wait_ge(kv_ps, 2 * t - 2)
                nc.scalar.copy(qT[:, t % 2].rearrange("p c n q -> p n c q"),
                               bank[2][:, :].rearrange("p (n c q) -> p n c q", n=4, c=2))
                nc.scalar.copy(kT[:, t * P:(t + 1) * P], bank[3][:, 0:P])
                nc.scalar.copy(kdt[:, t % 2, :], bank[3][:, P:2 * P]).then_inc(t1_out, 1)

            def wo_round(h, q):
                c = slice(q * 2 * BANK, (q + 1) * 2 * BANK)
                nc.scalar.copy(o_hi[h][:, c], wO[h][:, c]).then_inc(wo_hi, 1)

            t1_evac(0)
            for s in range(NT):
                act.wait_ge(s_negm, s + 1)
                if s >= 1:
                    act.wait_ge(pt_ps, s)
                for m in range(8):
                    g, c, pr = m // 4, m // 2 % 2, m % 2
                    w = CHUNK if s == 0 and c == 0 else P
                    nc.scalar.activation(Pb[:, m, 0:w],
                                         bank[4 + g][:, (m % 4) * P:(m % 4) * P + w], ACT.Exp,
                                         bias=sst[:, 1, m:m + 1], accum_out=sst[:, 3, m:m + 1])
                nc.scalar.activation(sst[:, 4, :], sst[:, 2, :], ACT.Exp).then_inc(p_exp, 1)
                evac(unit_vg(s), zVG[:, s, :])
                if s + 2 < NT:
                    qk_square(s + 2)
                if s + 1 < NT:
                    t1_evac(s + 1)
                for g in range(2):
                    act.wait_ge(pt_ps, s + 1)
                    if g == 0 and s >= 1:
                        act.wait_ge(pv_ps, s)
                    nc.scalar.copy(PT[:, 4 * g:4 * g + 4, :],
                                   bank[4 + g][:, :].rearrange("p (n k) -> p n k", n=4)).then_inc(pt_out, 1)
                if s + Q_AHEAD < NT:
                    evac_q(s + Q_AHEAD)
                act.wait_ge(o_ps, s + 1)
                if s >= 1:
                    act.wait_ge(o_ready, s)
                nc.scalar.activation(obuf[:, 0, :], bank[6][:, 0:256], ACT.Square).then_inc(o_sq, 1)
                nc.scalar.activation(obuf[:, 1, :], zVG[:, s, 256:512], ACT.Tanh, scale=0.5).then_inc(o_tanh, 1)
                act.wait_ge(pv_ps, s + 1)
                if s >= 1:
                    act.wait_ge(ysum_ps, s)
                nc.scalar.activation(ysq[:, :, :], bank[2][:, :].rearrange("p (n k) -> p n k", n=4),
                                     ACT.Square).then_inc(yc_sq, 1)
                if s >= NT - 4:
                    if s == NT - 4:
                        act.wait_ge(w_in_full[0], 32)
                        act.wait_ge(proj_ps, unit_q(NT - 1) + 1)
                    wo_round(0, s - (NT - 4))

            def y_round(t):
                if t >= 2:
                    act.wait_ge(wo_ps, 2 * t - 2)
                act.wait_ge(yb_ready, t + 1)
                (s0, d0), (s1, d1) = y_parts(t, y_hi[t % 2])
                nc.scalar.copy(d0, s0)
                nc.scalar.copy(d1, s1).then_inc(y_hi_ready, 1)

            act.wait_ge(lru_done, 2)
            act.wait_ge(yc_raw, NT)
            y_round(0)
            act.wait_ge(w_in_full[1], 32)
            act.wait_ge(proj_ps, PROJ_ALL)
            for q in range(4):
                wo_round(1, q)
            y_round(1)

            for t in range(NT):
                if t + 2 < NT:
                    y_round(t + 2)
                act.wait_ge(x2_ready, 2 * t + 2)
                if t:
                    act.wait_ge(x2_ss, t)
                nc.scalar.activation(uc[:, 0, :], x2[:, t, :], ACT.Square,
                                     accum_out=ss[:, t:t + 1]).then_inc(x2_ss, 1)
                act.wait_ge(x2_rs, t + 1)
                if t >= 2:
                    act.wait_ge(xn_ps, 2 * (t - 1))
                    act.wait_ge(xn_stored[t % 2], 16 * (t // 2))
                nc.scalar.mul(xn[t % 2], x2[:, t, :], rs[:, t:t + 1]).then_inc(xn_scaled, 1)

            def hi(e, j):
                m = place(e, j)
                act.wait_ge(e_w[m], 16 * loads(e, j))
                nc.scalar.copy(w_hi[m][:, :], raw[m]).then_inc(e_hi, 1)

            def x_hi_evac(e, b):
                for h in range(2):
                    act.wait_ge(e_xps, 2 * e + (h + 1))
                    nc.scalar.copy(x_hi[b][:, h * BANK:(h + 1) * BANK], bank[2 + h][:, :]).then_inc(e_xh, 1)

            def silu(e):
                act.wait_ge(e_used, nth(e, 1))
                if not (isinstance(e, int) and e == 0):
                    act.wait_ge(e_hb, e)
                nc.scalar.activation(sg, bank[0][:, :], ACT.Silu).then_inc(e_sg, 1)

            def hidden_hi(e):
                act.wait_ge(e_hps, e)
                nc.scalar.copy(h_hi[:, :], bank[4][:, :]).then_inc(e_hh, 1)

            def rows_out(e, b, down, stored):
                act.wait_ge(e_used, down)
                if stored is not None:
                    act.wait_ge(y_stored[b], stored)
                nc.scalar.copy(yo[b][:, 0:BANK], bank[5][:, :])
                nc.scalar.copy(yo[b][:, BANK:], bank[6][:, :]).then_inc(e_y, 1)

            act.wait_ge(wo_ps, 2 * NT)
            for j in range(2):
                hi(0, j)
            act.wait_ge(rt_arg, 1)
            nc.scalar.activation(kT[:, 328:368], kT[:, 288:328], ACT.Exp).then_inc(rt_exp, 1)
            for j in range(2, 4):
                hi(0, j)
            x_hi_evac(0, 0)
            silu(0)
            x_hi_evac(1, 1)
            for j in range(6):
                hi(1, j)
                if j == 3:
                    hidden_hi(1)
                if j == 4:
                    silu(1)
            x_hi_evac(2, 0)

            def step(e, b, down, stored):
                for j in range(6):
                    hi(e, j)
                    if j == 2:
                        rows_out(e, b, down, stored)
                    if j == 3:
                        hidden_hi(e)
                    if j == 4:
                        silu(e)
                x_hi_evac(e + 1, 1 - b)

            for b in range(2):
                step(2 + b, b, nth(1 + b, 5), None)
            with act.Fori(2, NE // 2) as i:
                for b in range(2):
                    step(2 * i + b, b, 12 * i + (6 * b - 2), 16 * i - 16)
            hi(NE, 4)
            hi(NE, 5)
            hidden_hi(NE)
            rows_out(NE, 0, nth(NE - 1, 5), 8 * NE - 16)
            rows_out(NE + 1, 1, LAST, 8 * NE - 16)
            act.wait_ge(ctrl_ready, 1)
            n_ovf = act.value_load(ctrl[0:1, 0:1], min_val=0, max_val=NOVF)
            with act.If(0 < n_ovf):
                with act.Fori(0, NOVF) as j:
                    with act.If(j < n_ovf):
                        act.wait_ge(o_gu, j + 1)
                        nc.scalar.activation(sg, bank[0][:, :], ACT.Silu).then_inc(e_sg, 1)
                    act.nop()

            for t in range(NT):
                act.wait_ge(out_ready, t + 1)
                act.dma_start(out_d[t * P:(t + 1) * P, :], x2[:, t, :]).then_inc(out_stored, 16)
            act.wait_ge(out_stored, 16 * NT)

        @block.vector
        def _(dve):
            n = [0]

            def mark(ins):
                n[0] += 1
                ins.then_inc(dv, 1)
                return n[0]

            def link(ins):
                dve.wait_ge(dv, mark(ins))

            V = nc.vector
            ang = zG[:, 0, 0:256].rearrange("p (t d) -> p t d", t=NT)
            ang_c = zG[:, 1, 0:256].rearrange("p (t d) -> p t d", t=NT)
            turn = zG[:, 0, 256:512].rearrange("p (t d) -> p t d", t=NT)
            posf = zG[:, 0, 512:512 + NT]
            invf = zG[:, 0, 544:544 + HALF]

            def hT_evac(u):
                t, h = u // 2, u % 2
                dve.wait_ge(xT_ps, u + 1)
                if u == 0:
                    dve.wait_ge(c_in, 16)
                V.tensor_tensor(hT[:, 4 * h:4 * h + 4, t * P:(t + 1) * P],
                                bank[2 + u % 4][:, :].rearrange("p (k t) -> p k t", k=4),
                                bc(g1[:, 4 * h:4 * h + 4].unsqueeze(2), [P, 4, P]), ALU.mult).then_inc(hT_ready, 1)

            for t in range(NT):
                dve.wait_ge(x_rs, t + 1)
                V.tensor_scalar(xs[:, t, :], xs[:, t, :], rs[:, t:t + 1], None, ALU.mult).then_inc(x_scaled, 1)
                if t:
                    hT_evac(2 * t - 2)
                    hT_evac(2 * t - 1)
            hT_evac(2 * NT - 2)
            hT_evac(2 * NT - 1)

            inv = 1.0 / (10000.0 ** (np.arange(0, HD, 2, dtype=np.float32) / np.float32(HD)))
            for i in range(HALF):
                last = V.memset(invf[:, i:i + 1], float(inv[i]))
            dve.wait_ge(c_late, C_LATE)
            link(last)
            link(V.tensor_copy(posf, posi[:, :]))
            for i in range(NT):
                last = V.tensor_scalar(ang[:, i, :], invf, posf[:, i:i + 1], None, ALU.mult)
            link(last)
            for dst, shift in ((ang_c, 0.25), (ang, 0.0)):
                link(V.tensor_scalar(turn, ang, 1.0 / TWO_PI, shift, ALU.mult, ALU.add))
                link(V.tensor_scalar(turn, turn, ROUND, None, ALU.add))
                link(V.tensor_scalar(turn, turn, -ROUND, None, ALU.add))
                link(V.scalar_tensor_tensor(dst, turn, -PI_A, ang, ALU.mult, ALU.add))
                link(V.scalar_tensor_tensor(dst, turn, -PI_B, dst, ALU.mult, ALU.add))
                link(V.scalar_tensor_tensor(dst, turn, -PI_C, dst, ALU.mult, ALU.add))
                if shift:
                    link(V.tensor_scalar(dst, dst, float(np.pi / 2), None, ALU.add))
                last = V.tensor_scalar(dst, dst, PI_SAFE, -PI_SAFE, ALU.min, ALU.max)
                if shift:
                    link(last)
            last.then_inc(rope_arg, 1)
            link(V.tensor_scalar(sp[:, 2, :], lam[:, :], -1.0, None, ALU.mult))
            V.tensor_tensor(sp[:, 0, :], sp[:, 2, :], lam[:, :], ALU.min).then_inc(lam_e, 1)
            link(V.tensor_scalar(glag[:, :], glag[:, :], 0.5, None, ALU.mult))
            link(V.tensor_copy(desc[:, :], desc_i[:, :]))
            link(V.tensor_scalar(jrow[:, :], desc[:, 0:NOVF], -1.0, float(NE), ALU.mult, ALU.add))
            link(V.tensor_scalar(qg[:, :], qg[:, :], HD ** -0.5, None, ALU.mult))
            dve.wait_ge(lam_e, 2)
            link(V.tensor_scalar(sp[:, 3, :], sp[:, 1, :], 2.0, None, ALU.add))
            link(V.reciprocal(sp[:, 3, :], sp[:, 3, :]))
            link(V.tensor_tensor(sp[:, 3, :], sp[:, 3, :], sp[:, 1, :], ALU.mult))
            link(V.tensor_tensor(sp[:, 4, :], sp[:, 3, :], sp[:, 3, :], ALU.mult))
            link(V.memset(sp[:, 5, :], 1.0 / 19))
            for k in range(17, 0, -2):
                link(V.tensor_tensor(sp[:, 5, :], sp[:, 5, :], sp[:, 4, :], ALU.mult))
                link(V.tensor_scalar(sp[:, 5, :], sp[:, 5, :], 1.0 / k, None, ALU.add))
            link(V.tensor_tensor(sp[:, 5, :], sp[:, 5, :], sp[:, 3, :], ALU.mult))
            link(V.tensor_scalar(sp[:, 2, :], sp[:, 2, :], 0.0, None, ALU.max))
            link(V.scalar_tensor_tensor(sp[:, 6, :], sp[:, 5, :], 2.0, sp[:, 2, :], ALU.mult, ALU.add))
            V.tensor_scalar(sp[:, 7, :], sp[:, 6, :], -8.0, None, ALU.mult).then_inc(c8_ready, 1)

            dve.wait_ge(proj_out, PROJ_G)
            for j in range(2):
                link(V.tensor_scalar(uc[:, j, :], zA[:, j, :], cw[:, 3, j:j + 1], cb[:, j:j + 1], ALU.mult, ALU.add))
                for tap in range(CONV_W - 2, -1, -1):
                    back_ = CONV_W - 1 - tap
                    last = V.scalar_tensor_tensor(uc[:, j, back_:T], zA[:, j, 0:T - back_], cw[:, tap, j:j + 1],
                                                  uc[:, j, back_:T], ALU.mult, ALU.add)
                    if tap:
                        link(last)
                last.then_inc(conv_done, 1)
            for j in range(2):
                dve.wait_ge(lru_sig, 4 * j + 4)
                V.tensor_tensor(ri[:, 2 * j + 1, :], ri[:, 2 * j + 1, :], uc[:, j, :], ALU.mult).then_inc(lru_iu, 1)
            for j in range(2):
                dve.wait_ge(lru_tanh, j + 1)
                dve.wait_ge(lru_iu, j + 1)
                link(V.tensor_scalar(uc[:, j, :], zA[:, j, :], -1.0, 1.0, ALU.mult, ALU.add))
                link(V.reciprocal(uc[:, j, :], uc[:, j, :]))
                V.scalar_tensor_tensor(zA[:, j, :], zA[:, j, :], -2.0, uc[:, j, :], ALU.mult,
                                       ALU.mult).then_inc(lru_m2, 1)
            for j in range(2):
                dve.wait_ge(lru_sqrt, j + 1)
                link(V.tensor_tensor(zA[:, j, :], zA[:, j, :], ri[:, 2 * j + 1, :], ALU.mult))
                link(V.tensor_tensor_scan(uc[:, j, :], ri[:, 2 * j, :], zA[:, j, :], 0.0, ALU.mult, ALU.add))
                dve.wait_ge(lru_gelu, j + 1)
                V.tensor_tensor(zA[:, 2 + j, :], uc[:, j, :], zA[:, 2 + j, :], ALU.mult).then_inc(lru_y, 1)

            for hf in range(2):
                dve.wait_ge(alpha_ps, hf + 1)
                c = slice(hf * BANK, (hf + 1) * BANK)
                link(V.tensor_scalar(GB[:, 0, c], bank[2 + hf][:, :], ba[:, 0:1], None, ALU.add))
            V.scalar_tensor_tensor(GB[:, 1, :], GB[:, 0, :], -1.0, GB[:, 0, :], ALU.mult, ALU.min).then_inc(gla_na, 1)

            def qk_reduce(t):
                dve.wait_ge(qk_sq, t + 1)
                V.tensor_reduce(qst[:, 0, :], sqs[:, :].rearrange("p (h d) -> p h d", d=HD), AX,
                                ALU.add).then_inc(qk_ss, 1)

            def qk_scale(t):
                z3 = zQ[:, t, :].rearrange("p (h d) -> p h d", d=HD)
                dve.wait_ge(qk_rs, t + 1)
                V.tensor_tensor(z3, z3, bc(qst[:, 1, :].unsqueeze(2), [P, NQK, HD]), ALU.mult).then_inc(qk_scaled, 1)

            def qk_rope(t):
                z4 = zQ[:, t, :].rearrange("p (h e d) -> p e h d", e=2, d=HALF)
                c_, s_ = (bc(r[:, t, :].unsqueeze(1), [P, NQK, HALF]) for r in (cos, sin))
                if t == 0:
                    dve.wait_ge(rope_ready, 1)
                dve.wait_ge(qk_gained, t + 1)
                V.tensor_tensor(rt[:, 0], z4[:, 0], s_, ALU.mult)
                a_ = mark(V.tensor_tensor(rt[:, 1], z4[:, 1], s_, ALU.mult))
                dve.wait_ge(dv, a_)
                V.tensor_tensor(z4[:, 0], z4[:, 0], c_, ALU.mult)
                link(V.tensor_tensor(z4[:, 1], z4[:, 1], c_, ALU.mult))
                V.tensor_tensor(z4[:, 0], z4[:, 0], rt[:, 1], ALU.subtract)
                V.tensor_tensor(z4[:, 1], z4[:, 1], rt[:, 0], ALU.add).then_inc(qk_ready, 1)

            qk_reduce(0)
            qk_scale(0)
            dve.wait_ge(gla_ln, 1)
            link(V.scalar_tensor_tensor(GB[:, 0, :], GB[:, 0, :], 0.0, GB[:, 1, :], ALU.min, ALU.subtract))
            for c in range(NCH):
                cc = slice(c * CHUNK, (c + 1) * CHUNK)
                last = V.tensor_tensor_scan(GB[:, 1, cc], bc(ones[:, 0:1], [P, CHUNK]), GB[:, 0, cc], 0.0,
                                            ALU.mult, ALU.add)
            link(last)
            b3, r3, e3 = (GB[:, i, :].rearrange("p (c i) -> p c i", i=CHUNK) for i in (1, 0, 2))
            link(V.tensor_tensor(r3, b3, bc(b3[:, :, CHUNK // 2 - 1:CHUNK // 2], [P, NCH, CHUNK]), ALU.subtract))
            link(V.tensor_tensor(e3, bc(b3[:, :, CHUNK - 1:CHUNK], [P, NCH, CHUNK]), b3, ALU.subtract))
            V.tensor_scalar(GB[:, 0, :], GB[:, 0, :], -GLA_CLAMP * GLA_TAU, GLA_CLAMP * GLA_TAU, ALU.max,
                            ALU.min).then_inc(gla_b, 1)
            qk_rope(0)
            qk_reduce(1)
            dve.wait_ge(lru_ps, 9)
            V.tensor_scalar(ra[:], bank[6][:, 0:NT], 1.0 / LRU_W, EPS, ALU.mult, ALU.add).then_inc(lru_sum, 1)
            for j in range(2):
                V.tensor_scalar(zA[:, 2 + j, :], zA[:, 2 + j, :], lrug[:, j:j + 1], None,
                                ALU.mult).then_inc(lru_done, 1)
            qk_scale(1)
            s_ = GLA_DK ** -0.5
            for i, (dst, src) in enumerate(((3, 0), (0, 1), (2, 1), (1, 0))):
                dve.wait_ge(gla_exp, i + 1)
                V.scalar_tensor_tensor(GB[:, dst, :], GB[:, dst, :], 1.0 if src else s_, zG[:, src, :], ALU.mult,
                                       ALU.mult).then_inc(gla_prep, 1)
            qk_rope(1)
            dve.wait_ge(gla_prep, 4)
            V.memset(St[:, 0, :], 0.0).then_inc(st_ready, 1)

            def expand_q(t):
                if t >= 1:
                    dve.wait_ge(att_ps, t)
                V.tensor_tensor(qx[:, :, :], bc(GB[:, 3, t * P:(t + 1) * P].unsqueeze(1), [P, GLA_H, P]),
                                bc(hm[:, :].unsqueeze(2), [P, GLA_H, P]), ALU.mult).then_inc(qx_ready, 1)

            def yc_mean(t):
                dve.wait_ge(ysum_ps, t + 1)
                V.tensor_scalar(rc[:, t:t + 1], bank[6][:, 256:257], 1.0 / SWA_W, EPS, ALU.mult,
                                ALU.add).then_inc(ysum_out, 1)

            def yb_evac(t):
                dve.wait_ge(yb_ps, t + 1)
                V.tensor_scalar(hT[:, 2:4, t * P:(t + 1) * P],
                                bank[7][:, 256:512].rearrange("p (n k) -> p n k", n=2), glag[:, 0:1], None,
                                ALU.mult).then_inc(yb_ready, 1)

            def wo_rest(h, q):
                c = slice(q * 2 * BANK, (q + 1) * 2 * BANK)
                dve.wait_ge(wo_hi, 4 * h + q + 1)
                V.tensor_tensor(o_lo[h][:, c], wO[h][:, c], o_hi[h][:, c].bitcast(F32),
                                ALU.subtract).then_inc(wo_lo, 1)

            def y_rest(t):
                dve.wait_ge(y_hi_ready, t + 1)
                for (src, hi_), (_, lo_) in zip(y_parts(t, y_hi[t % 2][:, :].bitcast(F32)), y_parts(t, y_lo[t % 2])):
                    last = V.tensor_tensor(lo_, src, hi_, ALU.subtract)
                last.then_inc(y_lo_ready, 1)

            expand_q(0)
            for s in range(NT):
                dve.wait_ge(s_ps, s + 1)
                if s >= 1:
                    dve.wait_ge(p_ready, s)
                for g in range(2):
                    b_ = bank[4 + g][:, :].rearrange("p (n k) -> p n k", n=4)
                    if s == 0:
                        V.tensor_reduce(sst[:, 0, 4 * g:4 * g + 2], b_[:, 0:2, 0:CHUNK], AX, ALU.max)
                        last = V.tensor_reduce(sst[:, 0, 4 * g + 2:4 * g + 4], b_[:, 2:4, :], AX, ALU.max)
                    else:
                        last = V.tensor_reduce(sst[:, 0, 4 * g:4 * g + 4], b_, AX, ALU.max)
                link(last)
                m4 = sst[:, 0, :].rearrange("p (g c r) -> p g c r", g=2, c=2)
                s4 = bc(sinks[:, :].rearrange("p (g r) -> p g r", g=2).unsqueeze(2), [P, 2, 2, 2])
                link(V.tensor_tensor(m4, m4, s4, ALU.max))
                V.tensor_tensor(sst[:, 2, :].rearrange("p (g c r) -> p g c r", g=2, c=2), s4, m4, ALU.subtract)
                V.tensor_scalar(sst[:, 1, :], sst[:, 0, :], -1.0, None, ALU.mult).then_inc(s_negm, 1)
                if 1 <= s < NT - 1:
                    qk_rope(s + 1)
                if s == 0:
                    V.memset(Pb[:, 0:2, CHUNK:P], 0.0)
                    V.memset(Pb[:, 4:6, CHUNK:P], 0.0)
                if s >= 1:
                    yc_mean(s - 1)
                dve.wait_ge(p_exp, s + 1)
                link(V.tensor_tensor(sst[:, 4, :], sst[:, 4, :], sst[:, 3, :], ALU.add))
                link(V.reciprocal(sst[:, 4, :], sst[:, 4, :]))
                V.tensor_tensor(Pb[:, :, :], Pb[:, :, :], bc(sst[:, 4, :].unsqueeze(2), [P, 8, P]),
                                ALU.mult).then_inc(p_ready, 1)
                dve.wait_ge(att_ps, s + 1)
                if s >= 1:
                    dve.wait_ge(o_ps, s)
                V.tensor_tensor(attT[:, :, :], bank[6][:, :].rearrange("p (h t) -> p h t", h=GLA_H),
                                bc(cmask[:, :].unsqueeze(1), [P, GLA_H, P]), ALU.mult).then_inc(att_out, 1)
                if s + 2 < NT:
                    qk_reduce(s + 2)
                if s >= 1:
                    yb_evac(s - 1)
                for c in range(2):
                    k = 2 * s + c
                    dve.wait_ge(kv_ps, k + 1)
                    if s >= 1 and c == 0:
                        dve.wait_ge(o_ps, s)
                    kv = bank[7][:, 0:256] if c == 0 else bank[3][:, 256:512]
                    link(V.tensor_tensor(vkm[:, :].rearrange("p (h v) -> p h v", h=GLA_H),
                                         kv.rearrange("p (h v) -> p h v", h=GLA_H),
                                         bc(hm[:, :].unsqueeze(2), [P, GLA_H, GLA_DV]), ALU.mult))
                    dve.wait_ge(st_ready, k + 1)
                    V.scalar_tensor_tensor(St[:, (k + 1) % 4, :], St[:, k % 4, :], dec[:, k:k + 1], vkm[:, :],
                                           ALU.mult, ALU.add).then_inc(st_ready, 1)
                    dve.wait_ge(st_ready, k + 2)
                if s + 1 < NT:
                    expand_q(s + 1)
                if s + 2 < NT:
                    qk_scale(s + 2)
                dve.wait_ge(o_sq, s + 1)
                V.tensor_reduce(gst[:, 0, :], obuf[:, 0, :].rearrange("p (h v) -> p h v", h=GLA_H), AX,
                                ALU.add).then_inc(o_ss, 1)
                dve.wait_ge(o_tanh, s + 1)
                link(V.scalar_tensor_tensor(obuf[:, 1, :], obuf[:, 1, :], 1.0, zVG[:, s, 256:512], ALU.add, ALU.mult))
                dve.wait_ge(yc_sq, s + 1)
                V.tensor_tensor(hT[:, 4:8, s * P:(s + 1) * P], bank[2][:, :].rearrange("p (n k) -> p n k", n=4),
                                bc(swag[:, :].unsqueeze(2), [P, 4, P]), ALU.mult).then_inc(yc_raw, 1)
                dve.wait_ge(o_rs, s + 1)
                dve.wait_ge(o_ss, s + 1)
                o3 = obuf[:, 0, :].rearrange("p (h v) -> p h v", h=GLA_H)
                link(V.tensor_tensor(o3, bank[6][:, 0:256].rearrange("p (h v) -> p h v", h=GLA_H),
                                     bc(gst[:, 1, :].unsqueeze(2), [P, GLA_H, GLA_DV]), ALU.mult))
                V.tensor_tensor(zVG[:, s, 0:256], obuf[:, 0, :], obuf[:, 1, :], ALU.mult).then_inc(o_ready, 1)
                if s >= NT - 3:
                    wo_rest(0, s - (NT - 3))
            yc_mean(NT - 1)
            yb_evac(NT - 1)
            wo_rest(0, 3)
            y_rest(0)
            for q in range(4):
                wo_rest(1, q)
            y_rest(1)

            L = route[:, 0:NT * NR].rearrange("p (t r) -> p t r", r=NR)

            def h2T_evac(t):
                for h in range(2):
                    dve.wait_ge(xn_ps, 2 * t + h + 1)
                    V.tensor_copy(h2T[t % 2][:, 4 * h:4 * h + 4, :],
                                  bank[6 + h][:, :].rearrange("p (k t) -> p k t", k=4)).then_inc(h2T_ready, 1)

            def logits(t):
                dve.wait_ge(lg_ps, t + 1)
                V.tensor_tensor(L[:, t, :], bank[6][:, 0:NR], rb[:, :], ALU.add).then_inc(lg_out, 1)

            def lo(e, j):
                m = place(e, j)
                dve.wait_ge(e_hi, nth(e, j))
                V.tensor_tensor(w_lo[m][:, :], raw[m], w_hi[m][:, :].bitcast(F32), ALU.subtract).then_inc(e_lo, 1)

            one = bc(ones[:, 0:1], [P, P])
            link(V.tensor_tensor_scan(count, one, one, -1.0, ALU.mult, ALU.add))
            for k in range(TOPK):
                V.tensor_scalar(asgf[:, k, :], tokid[:, :], -1.0, float((TOPK - k) * T), ALU.mult, ALU.add)
            dve.wait_ge(lru_rs, 1)
            for t in range(NT):
                dve.wait_ge(x_in[t], 32)
                dve.wait_ge(yc_rs, t + 1)
                for h in range(2):
                    if t >= 2 and h == 1:
                        h2T_evac(t - 2)
                    dve.wait_ge(wo_ps, 2 * t + h + 1)
                    xc = x2[:, t, h * BANK:(h + 1) * BANK]
                    link(V.tensor_tensor(xc, xc, bank[3 * h][:, :], ALU.add))
                    link(V.scalar_tensor_tensor(xc, bank[3 * h + 1][:, :], ra[:, t:t + 1], xc, ALU.mult, ALU.add))
                    V.scalar_tensor_tensor(xc, bank[3 * h + 2][:, :], rc[:, t:t + 1], xc, ALU.mult,
                                           ALU.add).then_inc(x2_ready, 1)
                if t + 2 < NT:
                    y_rest(t + 2)
                if t >= 2:
                    logits(t - 2)
            h2T_evac(NT - 2)
            logits(NT - 2)
            lo(0, 0)
            h2T_evac(NT - 1)
            lo(0, 1)
            logits(NT - 1)

            def small(k, n_):
                return kT[:, k:k + n_]

            U = uc[:, :, :].rearrange("p a b -> p (a b)")
            arg = small(288, NT * NG + NT)
            ex = small(328, NT * NG + NT)
            arg4 = arg[:, 0:NT * NG].rearrange("p (t g) -> p t g", g=NG)
            gmax, gsum, den = small(368, NT), small(376, NT), small(384, NT)
            gt = small(392, NT * NG).rearrange("p (t g) -> p t g", g=NG)
            gfirst = small(424, NT)
            mx = [small(432 + NT * k, NT) for k in range(TOPK)]
            sel16, rk, tb = small(448, 16), small(464, 16), small(480, 16)
            nq, bl, z_ = small(496, 16), small(512, 16), small(528, 16)
            nqi = small(544, 16).bitcast(I32)
            cnt, nb, oend, tab = (small(560 + NE * k, NE) for k in range(4))
            nbi = small(688, NE).bitcast(I32)
            cover = small(0, 16)
            lm = U[:, 0:NT * NE].rearrange("p (t e) -> p t e", e=NE)
            lm4 = U[:, 0:NT * NE].rearrange("p (t g e) -> p t g e", g=NG, e=EPG)
            A = U[:, 256:768].rearrange("p (k t e) -> p k t e", k=TOPK, e=NE)
            A_n = U[:, 256:768].rearrange("p (n e) -> p n e", e=NE)
            rank = U[:, 768:1024].rearrange("p (t e) -> p t e", e=NE)
            tmp = U[:, 1024:1280].rearrange("p (t e) -> p t e", e=NE)
            tmp4 = U[:, 1024:1536].rearrange("p (k t e) -> p k t e", k=TOPK, e=NE)
            tmp_n = U[:, 1024:1536].rearrange("p (n e) -> p n e", e=NE)
            Mb = uc[:, 1, 512:640].bitcast(BF16).rearrange("p (t e) -> p t e", e=NE)
            descb = bc(desc[:, :].unsqueeze(1), [P, NT, NE])
            dg = bc(desc[:, NE - NG:NE].unsqueeze(1), [P, NT, NG])

            def per(c, w):
                return bc(c.unsqueeze(2), [P, NT, w])

            dve.wait_ge(lg_out, NT)
            link(V.tensor_reduce(gmax, L[:, :, 0:NG], AX, ALU.max))
            link(V.tensor_tensor(arg4, L[:, :, 0:NG], per(gmax, NG), ALU.subtract))
            link(V.tensor_tensor(gt, L[:, :, 0:NG], per(gmax, NG), ALU.is_equal))
            link(V.tensor_tensor(gt, gt, dg, ALU.mult))
            link(V.tensor_reduce(gfirst, gt, AX, ALU.max))
            link(V.tensor_tensor(gt, dg, per(gfirst, NG), ALU.is_equal))
            link(V.tensor_scalar(gt, gt, -1.0, BIG, ALU.add, ALU.mult))
            link(V.tensor_tensor(lm4, L[:, :, NG:NR].rearrange("p t (g e) -> p t g e", g=NG),
                                 bc(gt.unsqueeze(3), [P, NT, NG, EPG]), ALU.add))
            for k in range(TOPK):
                sel = sel16[:, k * NT:(k + 1) * NT]
                link(V.tensor_reduce(mx[k], lm, AX, ALU.max))
                if k == 1:
                    V.tensor_tensor(arg[:, NT * NG:], mx[1], mx[0], ALU.subtract).then_inc(rt_arg, 1)
                link(V.tensor_tensor(tmp, lm, per(mx[k], NE), ALU.is_equal))
                link(V.tensor_tensor(tmp, tmp, descb, ALU.mult))
                link(V.tensor_reduce(sel, tmp, AX, ALU.max))
                link(V.tensor_tensor(A[:, k], descb, per(sel, NE), ALU.is_equal))
                if k == 0:
                    link(V.scalar_tensor_tensor(lm, A[:, 0], -3.0 * BIG, lm, ALU.mult, ALU.add))
            V.tensor_tensor(Mb, A[:, 0], A[:, 1], ALU.add).then_inc(hot_ready, 1)
            dve.wait_ge(rt_exp, 1)
            link(V.tensor_reduce(gsum, ex[:, 0:NT * NG].rearrange("p (t g) -> p t g", g=NG), AX, ALU.add))
            link(V.scalar_tensor_tensor(den, ex[:, NT * NG:], 1.0, gsum, ALU.add, ALU.mult))
            link(V.reciprocal(wts[:, 0, :], den))
            link(V.tensor_tensor(wts[:, 1, :], wts[:, 0, :], ex[:, NT * NG:], ALU.mult))
            dve.wait_ge(rank_ps, 1)
            link(V.tensor_copy(rank, bank[5][:, 0:NT * NE].rearrange("p (t e) -> p t e", e=NE)))
            link(V.tensor_copy(cnt, bank[5][:, NT * NE:(NT + 1) * NE]))
            link(V.tensor_scalar(nbi, cnt, float(P - 1), None, ALU.add))
            link(V.tensor_scalar(nbi, nbi, 7, None, ALU.arith_shift_right))
            link(V.tensor_copy(nb, nbi))
            link(V.tensor_scalar(nb, nb, -1.0, 0.0, ALU.add, ALU.max))
            link(V.tensor_tensor_scan(oend, bc(ones[:, 0:1], [P, NE]), nb, 0.0, ALU.mult, ALU.add))
            link(V.scalar_tensor_tensor(tab, desc[:, :], -1.0, oend, ALU.add, ALU.add))
            link(V.tensor_tensor(tab, tab, nb, ALU.subtract))
            link(V.tensor_tensor(tmp4, A, bc(rank.unsqueeze(1), [P, TOPK, NT, NE]), ALU.mult))
            link(V.tensor_reduce(rk, tmp_n, AX, ALU.add))
            link(V.tensor_tensor(tmp_n, A_n, bc(tab.unsqueeze(1), [P, TOPK * NT, NE]), ALU.mult))
            link(V.tensor_reduce(tb, tmp_n, AX, ALU.add))
            link(V.tensor_copy(nqi, rk))
            link(V.tensor_scalar(nqi, nqi, 7, None, ALU.arith_shift_right))
            link(V.tensor_copy(nq, nqi))
            link(V.scalar_tensor_tensor(z_, nq, 1.0, tb, ALU.min, ALU.mult))
            link(V.tensor_tensor(z_, z_, nq, ALU.add))
            link(V.tensor_scalar(bl, sel16, -1.0, float(NE), ALU.mult, ALU.add))
            link(V.tensor_tensor(bl, bl, z_, ALU.add))
            link(V.scalar_tensor_tensor(rk, nq, -float(P), rk, ALU.mult, ALU.add))
            for k in range(TOPK):
                n_ = slice(k * NT, (k + 1) * NT)
                bh = blk_hots[:, n_, :]
                a_ = mark(V.tensor_tensor(bh, bc(count[:, 0:NBLK].unsqueeze(1), [P, NT, NBLK]), per(bl[:, n_], NBLK),
                                          ALU.is_equal))
                V.tensor_tensor(slot_hots[:, n_, :], bc(count.unsqueeze(1), [P, NT, P]), per(rk[:, n_], P),
                                ALU.is_equal)
                dve.wait_ge(dv, a_)
                V.tensor_tensor(bh, bh, per(asgf[:, k, :], NBLK), ALU.mult).then_inc(slot_hot, 1)
            dve.wait_ge(slot_ps, 1)
            dstf, over_T = small(704, NBLK), small(752, NBLK)
            link(V.tensor_scalar(dstf, bank[7][:, 0:NBLK], -1.0, float(TOPK * T), ALU.mult, ALU.add))
            link(V.tensor_scalar(over_T, dstf, float(T), -float(T), ALU.is_ge, ALU.mult))
            V.tensor_tensor(idx[:, :], dstf, over_T, ALU.add).then_inc(slot_ready, 1)
            V.tensor_copy(asg[:, :], dstf).then_inc(slot_ready, 1)
            ov = sqs[0:1, P:P + NOVF * NE].rearrange("p (j e) -> p j e", e=NE)
            link(V.tensor_tensor(ov, bc(oend[0:1, :].unsqueeze(1), [1, NOVF, NE]),
                                 bc(jrow[0:1, :].unsqueeze(2), [1, NOVF, NE]), ALU.is_le))
            link(V.tensor_reduce(cover[0:1, 1:NOVF + 1], ov, AX, ALU.add))
            link(V.tensor_copy(cover[0:1, 0:1], oend[0:1, NE - 1:NE]))
            V.tensor_copy(ctrl[0:1, 0:NOVF + 1], cover[0:1, 0:NOVF + 1]).then_inc(ctrl_ready, 1)

            def x_lo_evac(e, b):
                for h in range(2):
                    dve.wait_ge(e_xh, 2 * e + (h + 1))
                    c = slice(h * BANK, (h + 1) * BANK)
                    V.tensor_tensor(x_lo[b][:, c], bank[2 + h][:, :], x_hi[b][:, c].bitcast(F32),
                                    ALU.subtract).then_inc(e_xT, 1)

            def hidden(e, up):
                dve.wait_ge(e_sg, e)
                dve.wait_ge(e_used, up)
                V.tensor_tensor(hb, sg, bank[1][:, :], ALU.mult).then_inc(e_hb, 1)

            def hidden_lo(e):
                dve.wait_ge(e_hh, e)
                V.tensor_tensor(h_lo[:, :], bank[4][:, :], h_hi[:, :].bitcast(F32), ALU.subtract).then_inc(e_hT, 1)

            for j in range(2, 4):
                lo(0, j)
            x_lo_evac(0, 0)
            x_lo_evac(1, 1)
            for j in range(6):
                lo(1, j)
                if j == 0:
                    hidden(1, nth(0, 3))
                if j == 3:
                    hidden_lo(1)
            x_lo_evac(2, 0)
            with dve.Fori(1, NE // 2) as i:
                for b in range(2):
                    e = 2 * i + b
                    lo(e, 0)
                    hidden(e, 12 * i + (6 * b - 4))
                    lo(e, 1)
                    lo(e, 2)
                    lo(e, 3)
                    hidden_lo(e)
                    lo(e, 4)
                    lo(e, 5)
                    x_lo_evac(e + 1, 1 - b)
            hidden(NE, nth(NE - 1, 3))
            lo(NE, 4)
            lo(NE, 5)
            hidden_lo(NE)
            dve.wait_ge(ctrl_ready, 1)
            n_ovf = dve.value_load(ctrl[0:1, 0:1], min_val=0, max_val=NOVF)
            with dve.If(0 < n_ovf):
                with dve.Fori(0, NOVF) as j:
                    with dve.If(j < n_ovf):
                        dve.wait_ge(o_xps, j + 1)
                        for h in range(2):
                            V.tensor_copy(xT[:, 4 * h:4 * h + 4, :],
                                          bank[2 + h][:, :].rearrange("p (k t) -> p k t", k=4)).then_inc(o_xT, 1)
                        dve.wait_ge(e_sg, j + (NE + 1))
                        V.tensor_tensor(hb, sg, bank[1][:, :], ALU.mult).then_inc(e_hb, 1)
                        dve.wait_ge(e_hps, j + (NE + 1))
                        V.tensor_copy(hbT, bank[4][:, :].rearrange("p (k t) -> p k t", k=KF)).then_inc(o_hT, 1)
                        dve.wait_ge(o_down, j + 1)
                        dve.wait_ge(y_stored[1], 16 * (NE // 2))
                        V.tensor_copy(yo[1][:, 0:BANK], bank[5][:, :])
                        V.tensor_copy(yo[1][:, BANK:], bank[6][:, :]).then_inc(o_y, 1)
                    dve.nop()

            for t in range(NT):
                dve.wait_ge(back_in[t], 16 * TOPK)
                for k in range(TOPK):
                    last = V.scalar_tensor_tensor(x2[:, t, :], back[TOPK * t + k], wts[:, k, t:t + 1], x2[:, t, :],
                                                  ALU.mult, ALU.add)
                    if k == 0:
                        link(last)
                last.then_inc(out_ready, 1)

        @block.tensor
        def _(pe):
            M = nc.tensor.matmul

            pe.wait_ge(const_ready, 1)

            def x_transposes(t):
                pe.wait_ge(x_scaled, t + 1)
                for h in range(2):
                    u = 2 * t + h
                    if u >= 4:
                        pe.wait_ge(hT_ready, u - 3)
                    for k in range(4):
                        kk = 4 * h + k
                        last = nc.tensor.transpose(bank[2 + u % 4][:, k * P:(k + 1) * P],
                                                   xs[:, t, kk * P:(kk + 1) * P], ident[:, :])
                    last.then_inc(xT_ps, 1)

            def bank_free(u):
                if u >= 2:
                    pe.wait_ge(proj_out, u - 1)

            def channel_unit(u, w, m, hf):
                bank_free(u)
                for k in range(KD):
                    last = M(bank[u % 2][:, :], w[:, k, m * P:(m + 1) * P], hT[:, k, hf * BANK:(hf + 1) * BANK],
                             start=(k == 0), stop=(k == KD - 1))
                last.then_inc(proj_ps, 1)

            def token_unit(u, w, t):
                bank_free(u)
                for k in range(KD):
                    last = M(bank[u % 2][:, 0:w.shape[2]], hT[:, k, t * P:(t + 1) * P], w[:, k, :],
                             start=(k == 0), stop=(k == KD - 1))
                return last

            for t in range(4):
                x_transposes(t)
            pe.wait_ge(w_in_full[0], 16)
            pe.wait_ge(hT_ready, NT)
            for m in range(4):
                channel_unit(m, wA, m, 0)
            for t in range(4, NT):
                x_transposes(t)
            pe.wait_ge(hT_ready, 2 * NT)
            for m in range(4):
                channel_unit(4 + m, wA, m, 1)
            pe.wait_ge(w_in_full[1], 16)
            pe.wait_ge(rope_ready, 1)
            for hf in range(2):
                for m in range(2):
                    channel_unit(PROJ_G + 2 * hf + m, wQK, m, hf)
            pe.wait_ge(c_late, C_LATE)
            for u in range(8):
                j, g, hf = u // 4, u // 2 % 2, u % 2
                pe.wait_ge(conv_done, j + 1)
                if u >= 6:
                    pe.wait_ge(lru_sig, u - 5)
                M(bank[2 + u % 6][:, :], (wibd if g else wrbd)[:, j, :], uc[:, j, hf * BANK:(hf + 1) * BANK],
                  start=True, stop=True).then_inc(lru_ps, 1)
            pe.wait_ge(w_in_full[2], 16)
            pe.wait_ge(w_in_full[3], 16)
            for t in range(NT):
                u = PROJ_KV + t
                token_unit(u, wKVA, t).then_inc(proj_ps, 1)
            pe.wait_ge(w_in_full[4], 16)
            token_unit(unit_q(0), wQ, 0).then_inc(proj_ps, 1)
            pe.wait_ge(lru_sig, 8)
            pe.wait_ge(proj_out, PROJ_Q)
            for t in range(NT):
                last = nc.tensor.transpose(bank[4 + t // 4][0:GLA_R, (t % 4) * P:(t % 4 + 1) * P],
                                           zAV[:, t, 0:GLA_R], ident[:, :])
                if t % 4 == 3:
                    last.then_inc(aT_ps, 1)
            token_unit(unit_q(1), wQ, 1).then_inc(proj_ps, 1)
            for hf in range(2):
                pe.wait_ge(aT_out, hf + 1)
                M(bank[2 + hf][:, :], wa2[:, :], GB[0:GLA_R, 3, hf * BANK:(hf + 1) * BANK],
                  start=True, stop=True).then_inc(alpha_ps, 1)
            for t in range(2, 4):
                token_unit(unit_q(t), wQ, t).then_inc(proj_ps, 1)
            pe.wait_ge(lru_ysq, 2)
            for t in range(NT):
                for j in range(2):
                    last = M(bank[6][:, t:t + 1], zA[:, j, t * P:(t + 1) * P], ones[:, 0:1],
                             start=(j == 0), stop=(j == 1))
            last.then_inc(lru_ps, 1)
            for t in range(4, Q_AHEAD):
                token_unit(unit_q(t), wQ, t).then_inc(proj_ps, 1)

            def t1(t):
                pe.wait_ge(qk_ready, t + 1)
                if t == 0:
                    pe.wait_ge(gla_prep, 4)
                else:
                    pe.wait_ge(t1_out, t)
                if t >= 2:
                    pe.wait_ge(yc_raw, t - 1)
                    pe.wait_ge(st_ready, 2 * t - 1)
                for h in range(4):
                    nc.tensor.transpose(bank[2][:, h * P:(h + 1) * P], zQ[:, t, h * P:(h + 1) * P], ident[:, :])
                nc.tensor.transpose(bank[3][:, 0:P], zQ[:, t, SWA_W:QK], ident[:, :])
                nc.tensor.transpose(bank[3][:, P:2 * P], GB[:, 2, t * P:(t + 1) * P], ident[:, :]).then_inc(t1_ps, 1)

            def scores(t):
                pe.wait_ge(t1_out, t + 1)
                if t >= 1:
                    pe.wait_ge(pt_out, 2 * t)
                for c in range(2):
                    for pr in range(2):
                        for g in range(2):
                            rows_ = slice(64 * g, 64 * g + 64)
                            lhs = qT[rows_, t % 2, c, 2 * pr:2 * pr + 2, :]
                            o = (2 * c + pr) * P
                            if c:
                                last = M(bank[4 + g][:, o:o + P], lhs, kT[rows_, t * P:(t + 1) * P],
                                         start=True, stop=True)
                            else:
                                last = M(bank[4 + g][:, o:o + CHUNK], lhs, kT[rows_, t * P:t * P + CHUNK],
                                         start=True, stop=True)
                                if t:
                                    last = M(bank[4 + g][:, o + CHUNK:o + P], lhs,
                                             kT[rows_, t * P - CHUNK:t * P], start=True, stop=True)
                last.then_inc(s_ps, 1)

            def y_sum(t):
                pe.wait_ge(yc_sq, t + 1)
                pe.wait_ge(o_ready, t + 1)
                for m in range(4):
                    last = M(bank[6][:, 256:257], ysq[:, m, :], ones[:, 0:1], start=(m == 0), stop=(m == 3))
                last.then_inc(ysum_ps, 1)

            def yb_transposes(t):
                pe.wait_ge(o_ready, t + 1)
                pe.wait_ge(st_ready, 2 * t + 2)
                for m in range(2):
                    last = nc.tensor.transpose(bank[7][:, 256 + m * P:256 + (m + 1) * P],
                                               zVG[:, t, m * P:(m + 1) * P], ident[:, :])
                last.then_inc(yb_ps, 1)

            pe.wait_ge(lru_sum, 1)
            t1(0)
            pe.wait_ge(w_in_full[5], 16)
            for s in range(NT):
                scores(s)
                token_unit(unit_vg(s), wVG, s).then_inc(proj_ps, 1)
                if s >= 1:
                    y_sum(s - 1)
                    yb_transposes(s - 1)
                if s + 1 < NT:
                    t1(s + 1)
                pe.wait_ge(qx_ready, s + 1)
                if s >= 1:
                    pe.wait_ge(ysum_out, s)
                M(bank[6][:, :], GB[:, 0, s * P:(s + 1) * P], qx[:, :, :], start=True, stop=True).then_inc(att_ps, 1)
                pe.wait_ge(p_ready, s + 1)
                for m in range(8):
                    last = nc.tensor.transpose(bank[4 + m // 4][:, (m % 4) * P:(m % 4 + 1) * P],
                                               Pb[:, m, :], ident[:, :])
                last.then_inc(pt_ps, 1)
                if s + Q_AHEAD < NT:
                    token_unit(unit_q(s + Q_AHEAD), wQ, s + Q_AHEAD).then_inc(proj_ps, 1)
                pe.wait_ge(proj_out, unit_vg(s) + 1)
                if s >= 1:
                    pe.wait_ge(yb_ready, s)
                if s + 1 < NT:
                    pe.wait_ge(t1_out, s + 2)
                for c in range(2):
                    r_ = slice(CHUNK * c, CHUNK * (c + 1))
                    kv = bank[7][:, 0:256] if c == 0 else bank[3][:, 256:512]
                    M(kv, kdt[r_, s % 2, :], zVG[r_, s, 0:256], start=True, stop=True).then_inc(kv_ps, 1)
                pe.wait_ge(att_out, s + 1)
                for c in range(2):
                    k = 2 * s + c
                    pe.wait_ge(st_ready, k + 1)
                    M(bank[6][CHUNK * c:CHUNK * (c + 1), 0:256], GB[:, 1, k * CHUNK:(k + 1) * CHUNK],
                      St[:, k % 4, :], start=True, stop=False, skip_group_check=True)
                for h in range(GLA_H):
                    last = M(bank[6][:, h * GLA_DV:(h + 1) * GLA_DV], attT[:, h, :],
                             zVG[:, s, h * GLA_DV:(h + 1) * GLA_DV], start=False, stop=(h == GLA_H - 1),
                             skip_group_check=True)
                last.then_inc(o_ps, 1)
                pe.wait_ge(vE_ready, s + 1)
                pe.wait_ge(pt_out, 2 * s + 2)
                for g in range(2):
                    for c in range(2):
                        v = (zAV[:, s, GLA_R + 64 * g:GLA_R + 64 * g + 64] if c else
                             vE[:, s % 2, 64 * g:64 * g + 64])
                        for i in range(2):
                            o_ = bank[2][64 * i:64 * i + 64, :].rearrange("p (m k) -> p m k", m=4)
                            last = M(o_[:, 2 * g:2 * g + 2, CHUNK * c:CHUNK * (c + 1)], v,
                                     PT[:, 4 * g + 2 * c:4 * g + 2 * c + 2, 64 * i:64 * i + 64],
                                     start=True, stop=True)
                last.then_inc(pv_ps, 1)
            y_sum(NT - 1)
            yb_transposes(NT - 1)

            def xn_transposes(t):
                pe.wait_ge(xn_ready, t + 1)
                if t >= 1:
                    pe.wait_ge(h2T_ready, 2 * t)
                    pe.wait_ge(lg_out, t)
                for h in range(2):
                    for k in range(4):
                        last = nc.tensor.transpose(bank[6 + h][:, k * P:(k + 1) * P],
                                                   xn[t % 2][:, (4 * h + k) * P:(4 * h + k + 1) * P], ident[:, :])
                    last.then_inc(xn_ps, 1)

            def router(t):
                pe.wait_ge(h2T_ready, 2 * t + 2)
                for k in range(KD):
                    last = M(bank[6][:, 0:NR], h2T[t % 2][:, k, :], rw[:, k, :], start=(k == 0), stop=(k == KD - 1))
                last.then_inc(lg_ps, 1)

            pe.wait_ge(lru_done, 2)
            pe.wait_ge(proj_out, PROJ_ALL)
            pe.wait_ge(pt_out, 2 * NT)
            pe.wait_ge(ysum_out, NT)
            pe.wait_ge(yc_raw, NT)
            pe.wait_ge(st_ready, 2 * NT + 1)
            pe.wait_ge(yb_ready, NT)
            for t in range(NT):
                pe.wait_ge(y_lo_ready, t + 1)
                for h in range(2):
                    if t == 0:
                        pe.wait_ge(wo_lo, 4 * h + 4)
                    if t >= 1:
                        pe.wait_ge(x2_ready, 2 * t - 1 + h)
                    for part, ks in enumerate(((2, 3), (0, 1), (4, 5, 6, 7))):
                        for k in ks:
                            for n, (y, w) in enumerate(((y_hi, o_hi), (y_hi, o_lo), (y_lo, o_hi))):
                                last = M(bank[3 * h + part][:, :], y[t % 2][:, k * P:(k + 1) * P],
                                         w[h][:, k * BANK:(k + 1) * BANK], start=(k == ks[0] and n == 0),
                                         stop=(k == ks[-1] and n == 2))
                    last.then_inc(wo_ps, 1)
                    if t >= 2:
                        (xn_transposes if h == 0 else router)(t - 2)
            for t in range(NT - 2, NT):
                xn_transposes(t)
                router(t)

            pe.wait_ge(hot_ready, 1)
            Mb = uc[:, 1, 512:640].bitcast(BF16).rearrange("p (t e) -> p t e", e=NE)
            for t in range(NT + 1):
                for t0 in range(min(t + 1, NT)):
                    last = M(bank[5][:, t * NE:(t + 1) * NE], (ltri if t0 == t else onesb)[:, :], Mb[:, t0, :],
                             start=(t0 == 0), stop=(t0 == min(t, NT - 1)))
            last.then_inc(rank_ps, 1)

            W = [slots[m].rearrange("p (k n) -> p k n", k=KF if m == 2 else KD) for m in range(3)]

            def rows_T(b, h):
                for k in range(4):
                    last = nc.tensor.transpose(bank[2 + h][:, k * P:(k + 1) * P],
                                               xg[b][:, (4 * h + k) * P:(4 * h + k + 1) * P], ident[:, :])
                return last

            def first_half(bk, j, b):
                for k in range(4):
                    kk = 4 * (j % 2) + k
                    xk, wk = slice(kk * P, (kk + 1) * P), slice(k * FF, (k + 1) * FF)
                    for n, (l, w) in enumerate(((x_hi, w_hi), (x_hi, w_lo), (x_lo, w_hi))):
                        last = M(bank[bk][:, :], l[b][:, xk], w[j][:, wk], start=(kk == 0 and n == 0),
                                 stop=(kk == KD - 1 and n == 2))
                last.then_inc(e_used, 1)

            def down_half(j, m):
                for k in range(2):
                    kk = 2 * (j - 4) + k
                    for n, (l, w) in enumerate(((h_hi, w_hi), (h_hi, w_lo), (h_lo, w_hi))):
                        for h in range(2):
                            last = M(bank[5 + h][:, :], l[:, kk * P:(kk + 1) * P],
                                     w[m][:, k * D + h * BANK:k * D + (h + 1) * BANK],
                                     start=(kk == 0 and n == 0), stop=(kk == KF - 1 and n == 2))
                last.then_inc(e_used, 1)

            def product(bk, w):
                for k in range(KD):
                    last = M(bank[bk][:, :], xT[:, k, :], w[:, k, :], start=(k == 0), stop=(k == KD - 1))
                return last

            def hidden_T():
                for k in range(KF):
                    last = nc.tensor.transpose(bank[4][:, k * P:(k + 1) * P], hb[:, k * P:(k + 1) * P], ident[:, :])
                return last

            def step(e, b, has, first=False, second=False):
                pe.wait_ge(e_xT, 2 * e + 2)
                if not first:
                    pe.wait_ge(e_sg, e)
                pe.wait_ge(e_lo, nth(e, 0))
                first_half(0, 0, b)
                if not first:
                    pe.wait_ge(e_hb, e)
                    hidden_T().then_inc(e_hps, 1)
                pe.wait_ge(e_lo, nth(e, 1))
                first_half(0, 1, b)
                pe.wait_ge(e_x[1 - b], has)
                rows_T(1 - b, 0).then_inc(e_xps, 1)
                pe.wait_ge(e_lo, nth(e, 2))
                first_half(1, 2, b)
                rows_T(1 - b, 1).then_inc(e_xps, 1)
                pe.wait_ge(e_lo, nth(e, 3))
                first_half(1, 3, b)
                if not first:
                    pe.wait_ge(e_hT, e)
                    if not second:
                        pe.wait_ge(e_y, e - 1)
                    for j in (4, 5):
                        pe.wait_ge(e_lo, nth(e, j))
                        down_half(j, j)

            for n in range(TOPK * NT):
                if n % NT == 0:
                    pe.wait_ge(slot_hot, n // NT + 1)
                last = M(bank[7][:, 0:NBLK], slot_hots[:, n, :], blk_hots[:, n, :], start=(n == 0),
                         stop=(n == TOPK * NT - 1))
            last.then_inc(slot_ps, 1)
            pe.wait_ge(e_x[0], 16)
            for h in range(2):
                rows_T(0, h).then_inc(e_xps, 1)
            step(0, 0, 16, first=True)
            step(1, 1, 32, second=True)
            with pe.Fori(1, NE // 2) as i:
                for b in range(2):
                    step(2 * i + b, b, 16 * i + 16 * (b + 1))
            pe.wait_ge(e_hb, NE)
            hidden_T().then_inc(e_hps, 1)
            pe.wait_ge(e_hT, NE)
            pe.wait_ge(e_y, NE - 1)
            for j in (4, 5):
                pe.wait_ge(e_lo, nth(NE, j))
                down_half(j, place(NE, j))
            pe.wait_ge(e_xT, 2 * (NE + 1))
            pe.wait_ge(e_y, NE)
            pe.wait_ge(ctrl_ready, 1)
            n_ovf = pe.value_load(ctrl[0:1, 0:1], min_val=0, max_val=NOVF)
            with pe.If(0 < n_ovf):
                with pe.Fori(0, NOVF) as j:
                    with pe.If(j < n_ovf):
                        pe.wait_ge(o_x, 16 * j + 16)
                        for h in range(2):
                            last = rows_T(1, h)
                        last.then_inc(o_xps, 1)
                        pe.wait_ge(o_xT, 2 * j + 2)
                        pe.wait_ge(o_w, 48 * j + 48)
                        product(0, W[0])
                        product(1, W[1]).then_inc(o_gu, 1)
                        pe.wait_ge(e_hb, j + (NE + 1))
                        hidden_T().then_inc(e_hps, 1)
                        pe.wait_ge(o_hT, j + 1)
                        for h in range(2):
                            for k in range(KF):
                                last = M(bank[5 + h][:, :], hbT[:, k, :], W[2][:, k, h * BANK:(h + 1) * BANK],
                                         start=(k == 0), stop=(k == KF - 1))
                        last.then_inc(o_down, 1)
                        pe.wait_ge(o_y, j + 1)
                        pe.sem_inc(turn, 1)
                    pe.nop()


_INS = ["x", "positions", "norm1_g", "w_in", "lru_conv_w", "lru_conv_b", "lru_wr", "lru_br", "lru_wi", "lru_bi",
        "lru_lambda", "lru_out_g", "gla_wa2", "gla_ba", "gla_norm_g", "swa_q_norm_g", "swa_k_norm_g", "swa_sinks",
        "swa_out_g", "w_out", "norm2_g", "moe_wg", "moe_bg", "moe_we", "moe_be", "moe_w_gate", "moe_w_up",
        "moe_w_down"]


def kernel(**inputs):
    import numpy as _np
    import concourse.bacc as _bacc
    from concourse import mybir as _mybir
    from concourse.bass_utils import run_bass_kernel_spmd as _run

    nc = _bacc.Bacc("TRN2", target_bir_lowering=False, num_devices=1)
    arrays, args = {}, {}
    for name in _INS:
        x = _np.ascontiguousarray(inputs[name])
        arrays[f"in_{name}_dram"] = x
        args[name] = nc.dram_tensor(f"in_{name}_dram", x.shape, _mybir.dt.from_np(x.dtype), kind="ExternalInput").ap()
    out = nc.dram_tensor("out_0_dram", (1, T, D), F32, kind="ExternalOutput").ap()
    build(nc, args, out)
    r = _run(nc, [arrays], core_ids=[0])
    return r.results[0]["out_0_dram"]
```
